# Optimizing a Trainium2 kernel written in Bass

```python
import jax, jax.numpy as jnp
from jax import lax
import numpy as np

D_MODEL = 1024
BATCH = 1
SEQ = 256
DEPTH = 2

ATTN_HEAD_DIM = 64
ATTN_GROUPS = ((128, 1), (512, 4), (2048, 16))
ATTN_HEADS_PER_GROUP = 4
ATTN_HEADS = ATTN_HEADS_PER_GROUP * len(ATTN_GROUPS)
ATTN_WIDTH = ATTN_HEADS * ATTN_HEAD_DIM
ATTN_OUT_WIDTH = ATTN_HEADS_PER_GROUP * ATTN_HEAD_DIM
BAND_BLOCK = 128
CONV_WIDTH = 3 * D_MODEL // 4
CONV_K = 3
HGRN_HEAD_DIM = 128
HGRN_WIDTH = 3 * D_MODEL // 4
HGRN_HEADS = HGRN_WIDTH // HGRN_HEAD_DIM
HGRN_CHUNK = 64
LB_FLOOR = 1e-30
N_BRANCHES = 3
SPLIT_SIZES = (ATTN_WIDTH,) * 3 + (CONV_WIDTH,) * 3 + (HGRN_WIDTH,) * 4 + (D_MODEL,) * N_BRANCHES
IN_COLS = sum(SPLIT_SIZES)
D_FF_DENSE = 2816
N_EXPERTS = 8
TOP_K = 2
D_FF_EXPERT = 3584
N_DENSE = (DEPTH + 1) // 2
N_MOE = DEPTH // 2
RMS_EPS = 1e-6
NEG_BIG = -1e30

kernel_name = "hybrid_dilated_attn_shortconv_hgrn2_moe"

def _rmsnorm(x, gain):
    xf = x.astype(jnp.float32)
    y = xf * lax.rsqrt(jnp.mean(xf * xf, axis=-1, keepdims=True) + RMS_EPS)
    return (y * gain).astype(x.dtype)

def _swiglu(h, w1, w3, w2):
    return (jax.nn.silu(h @ w1) * (h @ w3)) @ w2

def _to_residue(t, d):
    B, S = t.shape[:2]
    t = t.reshape((B, S // d, d) + t.shape[2:])
    t = jnp.moveaxis(t, 2, 1)
    return t.reshape((B * d, S // d) + t.shape[3:])

def _from_residue(t, d, B):
    L = t.shape[1]
    t = t.reshape((B, d, L) + t.shape[2:])
    t = jnp.moveaxis(t, 1, 2)
    return t.reshape((B, L * d) + t.shape[3:])

def _banded_window_attention(q, k, v, win):
    N, L, H, E = q.shape
    nb = -(-L // BAND_BLOCK)
    pad_end = nb * BAND_BLOCK - L
    qb = jnp.pad(q, ((0, 0), (0, pad_end), (0, 0), (0, 0))).reshape(N, nb, BAND_BLOCK, H, E)

    def kv_blocks(t):
        tp = jnp.pad(t, ((0, 0), (BAND_BLOCK, pad_end), (0, 0), (0, 0)))
        tp = tp.reshape(N, nb + 1, BAND_BLOCK, H, E)
        return jnp.concatenate([tp[:, :-1], tp[:, 1:]], axis=2)

    kb, vb = kv_blocks(k), kv_blocks(v)
    s = jnp.einsum('nbqhe,nbkhe->nbhqk', qb, kb).astype(jnp.float32) * (E ** -0.5)
    qi = jnp.arange(BAND_BLOCK)[:, None]
    kj = jnp.arange(2 * BAND_BLOCK)[None, :]
    rel = qi + BAND_BLOCK - kj
    key_abs = (jnp.arange(nb) * BAND_BLOCK - BAND_BLOCK)[:, None, None] + kj
    valid = (rel >= 0) & (rel <= win) & (key_abs >= 0)
    s = jnp.where(valid[None, :, None], s, NEG_BIG)
    m = jnp.max(s, axis=-1, keepdims=True)
    p = jnp.exp(s - m)
    den = jnp.sum(p, axis=-1)
    o = jnp.einsum('nbhqk,nbkhe->nbqhe', p, vb.astype(jnp.float32))
    o = o / jnp.transpose(den, (0, 1, 3, 2))[..., None]
    lse = jnp.transpose(m[..., 0] + jnp.log(den), (0, 1, 3, 2))
    o = o.reshape(N, nb * BAND_BLOCK, H, E)[:, :L]
    lse = lse.reshape(N, nb * BAND_BLOCK, H)[:, :L]
    return o, lse

def _dilated_attention(q, k, v, q_gain, k_gain):
    B, S, _ = q.shape
    shp = (B, S, ATTN_HEADS, ATTN_HEAD_DIM)
    q = _rmsnorm(q.reshape(shp), q_gain)
    k = _rmsnorm(k.reshape(shp), k_gain)
    v = v.reshape(shp)
    outs, lses = [], []
    for g, (window, dilation) in enumerate(ATTN_GROUPS):
        hs = slice(g * ATTN_HEADS_PER_GROUP, (g + 1) * ATTN_HEADS_PER_GROUP)
        o, lse = _banded_window_attention(_to_residue(q[:, :, hs], dilation),
                                          _to_residue(k[:, :, hs], dilation),
                                          _to_residue(v[:, :, hs], dilation),
                                          window // dilation)
        outs.append(_from_residue(o, dilation, B))
        lses.append(_from_residue(lse, dilation, B))
    o = jnp.stack(outs)
    w = jax.nn.softmax(jnp.stack(lses), axis=0)
    o = jnp.einsum('gbsh,gbshe->bshe', w, o)
    return o.reshape(B, S, ATTN_OUT_WIDTH).astype(q.dtype)

def _short_conv(xb, b_gate, c_gate, conv_w):
    u = c_gate * xb
    S = u.shape[1]
    up = jnp.pad(u, ((0, 0), (CONV_K - 1, 0), (0, 0)))
    y = conv_w[0] * up[:, CONV_K - 1:CONV_K - 1 + S]
    for j in range(1, CONV_K):
        y = y + conv_w[j] * up[:, CONV_K - 1 - j:CONV_K - 1 - j + S]
    return b_gate * y

def _hgrn2_chunked(q, k, log_f, v):
    B, S, H, K = q.shape
    V = v.shape[-1]
    nc = S // HGRN_CHUNK

    def chunks(t):
        t = t.astype(jnp.float32).reshape(B, nc, HGRN_CHUNK, H, t.shape[-1])
        return jnp.transpose(t, (1, 0, 3, 2, 4))

    causal = jnp.tril(jnp.ones((HGRN_CHUNK, HGRN_CHUNK), dtype=bool))[:, :, None]

    def step(state, xs):
        qc, kc, gc, vc = xs
        b = jnp.cumsum(gc, axis=2)
        diff = b[:, :, :, None, :] - b[:, :, None, :, :]
        decay = jnp.where(causal, jnp.exp(jnp.where(causal, diff, 0.0)), 0.0)
        scores = jnp.einsum('bhtk,bhsk,bhtsk->bhts', qc, kc, decay)
        o = scores @ vc + jnp.einsum('bhtk,bhkv->bhtv', qc * jnp.exp(b), state)
        b_last = b[:, :, -1:, :]
        state = (jnp.exp(b_last[:, :, 0, :])[..., None] * state
                 + jnp.einsum('bhsk,bhsv->bhkv', kc * jnp.exp(b_last - b), vc))
        return state, o

    state0 = jnp.zeros((B, H, K, V), jnp.float32)
    _, o = lax.scan(step, state0, (chunks(q), chunks(k), chunks(log_f), chunks(v)))
    return jnp.transpose(o, (1, 0, 3, 2, 4)).reshape(B, S, H, V)

def _hgrn2(q, f_logit, i, g, lb, out_gain):
    B, S, _ = q.shape
    shp = (B, S, HGRN_HEADS, HGRN_HEAD_DIM)
    qh = jax.nn.silu(q).reshape(shp)
    lbh = lb.reshape(HGRN_HEADS, HGRN_HEAD_DIM)
    log_f = jnp.logaddexp(jnp.log(jnp.maximum(lbh, LB_FLOOR)),
                          jnp.log1p(-lbh) + jax.nn.log_sigmoid(f_logit.astype(jnp.float32).reshape(shp)))
    k = -jnp.expm1(log_f)
    o = _hgrn2_chunked(qh, k, log_f, i.reshape(shp))
    o = _rmsnorm(o, out_gain) * jax.nn.silu(g.astype(jnp.float32).reshape(shp))
    return o.reshape(B, S, HGRN_WIDTH).astype(q.dtype)

def _moe(h, router_w, w1, w3, w2):
    logits = (h @ router_w).astype(jnp.float32)
    top_vals, top_idx = lax.top_k(logits, TOP_K)
    gates = jax.nn.softmax(top_vals, axis=-1)
    combine = jnp.sum(jax.nn.one_hot(top_idx, N_EXPERTS, dtype=jnp.float32) * gates[..., None], axis=-2)
    out = jnp.zeros_like(h)
    for e in range(N_EXPERTS):
        out = out + combine[..., e:e + 1].astype(h.dtype) * _swiglu(h, w1[e], w3[e], w2[e])
    return out

def setup_inputs(seed: int = 0) -> dict:
    key = jax.random.key(seed)
    ks = jax.random.split(key, 22)
    f32 = jnp.float32

    def nrm(k, shape, fan_in):
        return jax.random.normal(k, shape, f32) * (fan_in ** -0.5)

    def gain(k, shape):
        return 1.0 + 0.1 * jax.random.normal(k, shape, f32)

    return {
        "x": jax.random.normal(ks[0], (BATCH, SEQ, D_MODEL), f32),
        "attn_norm": gain(ks[1], (DEPTH, D_MODEL)),
        "ffn_norm": gain(ks[2], (DEPTH, D_MODEL)),
        "w_in": nrm(ks[3], (DEPTH, D_MODEL, IN_COLS), D_MODEL),
        "q_norm": gain(ks[4], (DEPTH, ATTN_HEAD_DIM)),
        "k_norm": gain(ks[5], (DEPTH, ATTN_HEAD_DIM)),
        "conv_w": nrm(ks[6], (DEPTH, CONV_K, CONV_WIDTH), CONV_K),
        "hgrn_lower_bounds": 0.5 * jax.random.normal(ks[7], (DEPTH, HGRN_WIDTH), f32),
        "hgrn_out_norm": gain(ks[8], (DEPTH, HGRN_HEAD_DIM)),
        "w_proj_a": nrm(ks[9], (DEPTH, ATTN_OUT_WIDTH, D_MODEL), ATTN_OUT_WIDTH),
        "w_proj_b": nrm(ks[10], (DEPTH, CONV_WIDTH, D_MODEL), CONV_WIDTH),
        "w_proj_c": nrm(ks[11], (DEPTH, HGRN_WIDTH, D_MODEL), HGRN_WIDTH),
        "w_out": nrm(ks[12], (DEPTH, D_MODEL, D_MODEL), D_MODEL),
        "dense_w1": nrm(ks[13], (N_DENSE, D_MODEL, D_FF_DENSE), D_MODEL),
        "dense_w3": nrm(ks[14], (N_DENSE, D_MODEL, D_FF_DENSE), D_MODEL),
        "dense_w2": nrm(ks[15], (N_DENSE, D_FF_DENSE, D_MODEL), D_FF_DENSE),
        "router_w": nrm(ks[16], (N_MOE, D_MODEL, N_EXPERTS), D_MODEL),
        "moe_w1": nrm(ks[17], (N_MOE, N_EXPERTS, D_MODEL, D_FF_EXPERT), D_MODEL),
        "moe_w3": nrm(ks[18], (N_MOE, N_EXPERTS, D_MODEL, D_FF_EXPERT), D_MODEL),
        "moe_w2": nrm(ks[19], (N_MOE, N_EXPERTS, D_FF_EXPERT, D_MODEL), D_FF_EXPERT),
    }

def reference(x, attn_norm, ffn_norm, w_in, q_norm, k_norm, conv_w, hgrn_lower_bounds,
              hgrn_out_norm, w_proj_a, w_proj_b, w_proj_c, w_out, dense_w1, dense_w3,
              dense_w2, router_w, moe_w1, moe_w3, moe_w2):
    split_points = [int(p) for p in np.cumsum(SPLIT_SIZES)[:-1]]
    lbs = jax.nn.softmax(hgrn_lower_bounds.astype(jnp.float32), axis=0)
    lower_bound = jnp.cumsum(lbs, axis=0) - lbs[0]
    for layer in range(DEPTH):
        h = _rmsnorm(x, attn_norm[layer])
        proj = h @ w_in[layer]
        (qa, ka, va, xb, bb, cb, qc, fc, ic, gc,
         gate_a, gate_b, gate_c) = jnp.split(proj, split_points, axis=-1)
        ya = _dilated_attention(qa, ka, va, q_norm[layer], k_norm[layer]) @ w_proj_a[layer]
        yb = _short_conv(xb, bb, cb, conv_w[layer]) @ w_proj_b[layer]
        yc = _hgrn2(qc, fc, ic, gc, lower_bound[layer], hgrn_out_norm[layer]) @ w_proj_c[layer]
        merged = (jax.nn.sigmoid(gate_a) * ya + jax.nn.sigmoid(gate_b) * yb
                  + jax.nn.sigmoid(gate_c) * yc)
        x = x + merged @ w_out[layer]
        h = _rmsnorm(x, ffn_norm[layer])
        if layer % 2 == 0:
            j = layer // 2
            x = x + _swiglu(h, dense_w1[j], dense_w3[j], dense_w2[j])
        else:
            j = layer // 2
            x = x + _moe(h, router_w[j], moe_w1[j], moe_w3[j], moe_w2[j])
    return x


_drawn_inputs = setup_inputs


def setup_inputs(seed=0):
    import zlib

    import numpy as np

    out = dict(_drawn_inputs(seed))
    spreads = {}
    factors = {'k_norm': 2.928, 'hgrn_lower_bounds': 3.389}
    for name, (base, spread) in spreads.items():
        noise = np.random.default_rng([zlib.crc32(name.encode()), seed]).standard_normal(out[name].shape)
        drawn = base * np.exp(spread * noise) if base else spread * noise
        out[name] = __import__('jax').numpy.asarray(drawn.astype(out[name].dtype))
    for name, factor in factors.items():
        out[name] = (out[name] * factor).astype(out[name].dtype)
    return out
```

```python
from contextlib import ExitStack

import concourse.bass as bass
from concourse import mybir

F32 = mybir.dt.float32
F32R = mybir.dt.float32r
I32 = mybir.dt.int32
ALU = mybir.AluOpType
ACT = mybir.ActivationFunctionType
AX = mybir.AxisListType.X

P = 128
KB = 1024
EPS = 1e-6
NEG_BIG = -1e30
LB_FLOOR = 1e-30
GROUPS = ((128, 1), (512, 4), (2048, 16))
SLOTS_PER_GROUP = 4
HD = 64
COLS = 256
RAW, SPLIT = 3, 2
M_RAW, M_SPLIT = 6, 6
AHEAD = 3
PIECE = 2048
LN_SHIFT = 40
LN2 = 0.6931471805599453

SEGMENTS = (("q", 0, 3), ("k", 768, 3), ("v", 1536, 3), ("i", 6144, 3),
            ("f", 5376, 3), ("qc", 4608, 3), ("g", 6912, 3), ("gate_a", 7680, 4), ("proj_a", None, 4),
            ("xb", 2304, 3), ("cb", 3840, 3), ("bb", 3072, 3), ("gate_b", 8704, 4), ("gate_c", 9728, 4),
            ("proj_b", None, 4), ("proj_c", None, 4), ("w_out", None, 4))
ORDER = [(name, c, None if col is None else col + c * COLS)
         for name, col, n in SEGMENTS for c in range(n)]
FIRST = {}
for _n, (_name, _c, _col) in enumerate(ORDER):
    FIRST.setdefault(_name, _n)
MIX = len(ORDER)
LEVELS = (None, 64, 32, 16, 8, 4, 2, 1)
NLEV = len(LEVELS) - 1

ATTN_AT = {9 + 3 * j + s: (j, s) for j in range(SLOTS_PER_GROUP) for s in range(3)}
ATTN_O_AT = {12 + 3 * j: j for j in range(SLOTS_PER_GROUP)}
LEVEL_AT = {22 + 2 * n: n for n in range(NLEV + 1)}
CROSS_AT, HGRN_O_AT, HGRN_SS_AT = 38, 39, 40


def decoder(nc, x_in, attn_norm, ffn_norm, w_in, q_norm, k_norm, conv_w, hgrn_lb, hgrn_gain,
            w_proj_a, w_proj_b, w_proj_c, w_out, dense_w1, dense_w3, dense_w2, router_w,
            moe_w1, moe_w3, moe_w2, out, stop_at=None):
    DEPTH, D, _ = w_in.shape
    TOK = x_in.shape[1]
    TB = TOK // P
    DC = D // P
    FF = dense_w1.shape[2]
    NE, FFE = router_w.shape[2], moe_w1.shape[3]
    CW = conv_w.shape[2]
    CC = CW // P
    DENSE_UNITS = FF // COLS
    MOE_UNITS = FFE // COLS
    assert TB == 2 and D == 1024 and CC == 6 and DENSE_UNITS == 11 and MOE_UNITS % 2 == 0
    DENSE = 3 * DENSE_UNITS
    UNIT_PIECES = 3
    PASS_PIECES = 3 * MOE_UNITS
    OVER = 2 * TOK // (P + 1)
    PASSES = NE + OVER
    BASE = (0, MIX + DENSE)
    DENSE0 = MIX

    def landed_by(p):
        return 16 * sum(2 if DENSE0 <= s < DENSE0 + DENSE else 1 for s in range(p % RAW, p + 1, RAW))

    with ExitStack() as ctx:
        def sb(name, shape, dt=F32):
            return ctx.enter_context(nc.sbuf_tensor(name, shape, dt))

        def sem(name):
            return ctx.enter_context(nc.semaphore(name))

        x = sb("x", [P, TB, D])
        ident = sb("ident", [P, P])
        ones = sb("ones", [P, P])
        mean128 = sb("mean128", [P, P])
        before = sb("before", [P, P])
        lane = sb("lane", [P, P])
        part = sb("part", [P, 1])
        lane_i = sb("lane_i", [P, P], I32)
        part_i = sb("part_i", [P, 1], I32)
        eps = sb("eps", [P, 1])
        amask = sb("amask", [P, 3 * P + 3 * TOK])
        hmask = sb("hmask", [P, len(LEVELS), P])
        rows = sb("rows", [P, P])
        cols = sb("cols", [P, P])
        hrows = sb("hrows", [4, HD])
        hcols = sb("hcols", [HD, 4])
        router = sb("router", [P, DC, NE])
        router_hi = sb("router_hi", [P, DC, NE], F32R)
        router_lo = sb("router_lo", [P, DC, NE], F32R)
        lbm = sb("lbm", [P, DEPTH, CC])
        oml = sb("oml", [P, DEPTH, CC])
        kfix = sb("kfix", [P, DEPTH, CC])
        lbt = sb("lbt", [P, 4, CC])
        scol = sb("scol", [P, 4])
        ssq = sb("ssq", [P, TB])
        rstd = sb("rstd", [P, TB])
        qkss = sb("qkss", [P, 24])
        smax = sb("smax", [P, TB])
        den = sb("den", [P, TB])
        rden = sb("rden", [P, TB])
        hT_hi = sb("hT_hi", [P, DC, TOK], F32R)
        hT_lo = sb("hT_lo", [P, DC, TOK], F32R)

        base = nc.sbuf_base
        top = [base + (-base) % 64]

        def at(name, shape, dt=F32, offset=None):
            n = 4
            for s in shape[1:]:
                n *= s
            if offset is None:
                offset = top[0]
                top[0] += -(-n // 32) * 32
            return nc.alloc_sbuf_tensor_at(name, shape, dt, offset=offset), offset

        arena = top[0]
        raw, _ = at("raw", [P, RAW, PIECE])
        w_hi, _ = at("w_hi", [P, SPLIT, PIECE], F32R)
        w_lo, _ = at("w_lo", [P, SPLIT, PIECE], F32R)
        i_tm, _ = at("i_tm", [P, TB, CW])
        q_tm, q_at = at("q_tm", [P, TB, CW])
        k_tm, _ = at("k_tm", [P, TB, CW])
        v_tm, _ = at("v_tm", [P, TB, CW])
        sig_c, _ = at("sig_c", [P, DC, TOK], offset=q_at)
        xb, xb_at = at("xb", [P, CC, TOK])
        cb, cb_at = at("cb", [P, CC, TOK])
        bb, bb_at = at("bb", [P, CC, TOK])
        yb_hi, _ = at("yb_hi", [P, CC, TOK], F32R, offset=cb_at)
        yb_lo, _ = at("yb_lo", [P, CC, TOK], F32R, offset=bb_at)
        W3 = 3 * TOK
        qT, _ = at("qT", [HD, W3], offset=xb_at)
        kT, _ = at("kT", [HD, W3], offset=xb_at + 4 * W3)
        NS = 3 * P + W3
        prob, _ = at("prob", [P, NS], offset=xb_at + 8 * W3)
        probT, _ = at("probT", [P, NS], offset=xb_at + 8 * W3 + 4 * NS)
        h_tm, _ = at("h_tm", [P, TB, D], offset=xb_at)
        qc, qc_at = at("qc", [P, CC, TOK])
        kc, kc_at = at("kc", [P, CC, TOK])
        yc_hi, _ = at("yc_hi", [P, CC, TOK], F32R, offset=qc_at)
        yc_lo, _ = at("yc_lo", [P, CC, TOK], F32R, offset=kc_at)
        bcum, _ = at("bcum", [P, CC, TOK])
        E = [at(f"E{n}", [P, CC, TOK])[0] for n in range(2)]
        sc, _ = at("sc", [P, CC * TB, P])
        scx, _ = at("scx", [P, CC, P])
        gc, _ = at("gc", [P, CC, TOK])
        o_hi, _ = at("o_hi", [HD, SLOTS_PER_GROUP, TOK], F32R)
        o_lo, _ = at("o_lo", [HD, SLOTS_PER_GROUP, TOK], F32R)
        merged, _ = at("merged", [P, DC, TOK])
        sig_ab, _ = at("sig_ab", [P, DC, TOK])
        term, _ = at("term", [P, 2, TOK])
        assert top[0] <= nc.sbuf_usable_end, (top[0], nc.sbuf_usable_end)
        act_tm, off = at("act_tm", [P, TB, COLS], offset=q_at)
        actT_hi, off = at("actT_hi", [P, TB, 2, P], F32R, offset=off + 4 * TB * COLS)
        actT_lo, off = at("actT_lo", [P, TB, 2, P], F32R, offset=off + 4 * TB * COLS)

        top[0] = arena

        def slots(name, n, dt=F32):
            out = []
            for s in range(n):
                if top[0] < xb_at + 4 * TB * D and top[0] + 4 * PIECE > xb_at:
                    top[0] = xb_at + 4 * TB * D
                out.append(at(f"{name}{s}", [P, PIECE], dt)[0])
            return out

        m_raw = slots("m_raw", M_RAW)
        m_hi = slots("m_hi", M_SPLIT, F32R)
        m_lo = slots("m_lo", M_SPLIT, F32R)
        XT_hi, XT_lo = hT_hi[:, :, 0:P], hT_lo[:, :, 0:P]
        sel01, _ = at("sel01", [P, TB, P])
        selT, _ = at("selT", [P, TOK], F32R)
        gslot, _ = at("gslot", [P, 1])
        m_act, _ = at("m_act", [P, COLS])
        mT_hi, _ = at("mT_hi", [P, 2, P], F32R)
        mT_lo, _ = at("mT_lo", [P, 2, P], F32R)
        Y_hi, Y_at = at("Y_hi", [P, D], F32R)
        Y_lo, _ = at("Y_lo", [P, D], F32R)
        gain_row, _ = at("gain_row", [P, D], offset=Y_at)
        logit, _ = at("logit", [P, TB, NE])
        gt, _ = at("gt", [P, TB, NE, NE])
        eq, _ = at("eq", [P, TB, NE, NE])
        tri, _ = at("tri", [P, NE, NE])
        rank, _ = at("rank", [P, TB, NE])
        chosen, _ = at("chosen", [P, TB, NE])
        lmax, _ = at("lmax", [P, TB])
        ez, _ = at("ez", [P, TB, NE])
        esum, _ = at("esum", [P, TB])
        gate, _ = at("gate", [P, TB, NE])
        place, _ = at("place", [P, TB, NE])
        over, _ = at("over", [P, NE])
        over_n, _ = at("over_n", [P, NE])
        pick, _ = at("pick", [P, OVER, NE])
        tmp8, _ = at("tmp8", [P, TB, OVER, NE])
        iota8, _ = at("iota8", [P, NE])
        POS, _ = at("POS", [P, PASSES + 1, TB])
        GATE, _ = at("GATE", [P, PASSES, TB])
        tabf, _ = at("tabf", [P, PASSES + 1])
        tab, _ = at("tab", [P, PASSES + 1], I32)
        assert top[0] <= nc.sbuf_usable_end, (top[0], nc.sbuf_usable_end)

        ps = ctx.enter_context(nc.psum_tensor("ps", [P, 8, 512], F32))
        G = [ps[:, n, :] for n in range(2)]
        SA = ps[:, 2:5, :].rearrange("p a n -> p (a n)")
        TA = ps[:, 5:8, :].rearrange("p a n -> p (a n)")

        XT_psum = ps[:, 4:6, :].rearrange("p a (c t) -> p (a c) t", t=P)

        x_in_sem, vec_in, router_in, gain_in = sem("x_loaded"), sem("vectors_loaded"), sem("router_loaded"), sem("gain_loaded")
        landed = [sem(f"raw_landed{r}") for r in range(RAW)]
        hi_done, lo_done, used = sem("hi_done"), sem("lo_done"), sem("piece_used")
        g_free = [sem(f"g_free{n}") for n in range(2)]
        masks = sem("masks_built")
        pool_step, dve_step = sem("pool_step"), sem("dve_step")
        vec_T = sem("vectors_turned")
        lb_diff, lb_exp = sem("lb_diff"), sem("lb_exp")
        squared = sem("x_squared")
        h_ready = sem("h_ready")
        hT_psum = sem("hT_in_psum")
        hT_hi_done = sem("hT_hi_done")
        hT_ready = sem("hT_ready")
        f_sig, f_arg, f_ln, cum = sem("forget_sigmoid"), sem("ln_argument"), sem("ln_done"), sem("cumsum_done")
        qk_normed = sem("qk_normed")
        conv_y, conv_hi, conv_lo = sem("conv_y"), sem("conv_hi"), sem("conv_lo")
        diff, decay, qk_level, level_mm, level_ev, level_add = (sem("level_diff"), sem("level_decay"), sem("level_qk"),
                                                                sem("level_mm"), sem("level_evacuated"), sem("level_added"))
        x_decay, x_qk, x_mm, x_ev = sem("cross_decay"), sem("cross_qk"), sem("cross_mm"), sem("cross_evacuated")
        o_mm, o_sq, o_ss, o_gated, yc_hi_done, yc_done = (sem("hgrn_o"), sem("hgrn_squared"), sem("hgrn_ss"), sem("hgrn_gated"),
                                                         sem("yc_hi_done"), sem("yc_done"))
        o_read = sem("hgrn_o_read")
        a_turn, a_qk, a_score, a_masked, a_max, a_exp, a_prob, a_pturn, a_pT, a_o, a_ohi, a_olo = (
            sem("attn_turned"), sem("attn_qkT"), sem("attn_scores"), sem("attn_masked"), sem("attn_max"), sem("attn_exp"),
            sem("attn_prob"), sem("attn_prob_turned"), sem("attn_probT"), sem("attn_o"), sem("attn_o_hi"), sem("attn_o_lo"))
        kc_done = sem("kc_done")
        x_root, qk_ss, qk_root, o_root = sem("x_root"), sem("qk_ss"), sem("qk_root"), sem("hgrn_root")
        merge = sem("merged_done")
        merged_hi, merged_lo = sem("merged_hi"), sem("merged_lo")
        silu, act_done, aT_psum, aT_hi, aT_lo = sem("dense_silu"), sem("dense_act"), sem("dense_actT_psum"), sem("dense_actT_hi"), sem("dense_actT_lo")
        x_done = sem("dense_x")
        hg = sem("h_gained")
        r_hi, r_lo, logits, z_ready, z_exp = sem("router_hi_done"), sem("router_lo_done"), sem("logits"), sem("z_ready"), sem("z_exp")
        chosen_ready, counted, table = sem("chosen_ready"), sem("tokens_counted"), sem("pass_table_ready")
        m_landed = [sem(f"moe_raw_landed{r}") for r in range(M_RAW)]
        m_raw_free = sem("moe_raw_free")
        m_hi_done = sem("moe_hi_done")
        m_split_free = sem("moe_split_free")
        sel_built, gathered, XT_hi_done, XT_lo_done = sem("sel_built"), sem("gathered"), sem("XT_hi_done"), sem("XT_lo_done")
        sel_turned, selT_done, gslot_done = sem("sel_turned"), sem("selT_done"), sem("gslot_done")
        m_silu, m_act_done, mT_psum, mT_hi_done, mT_lo_done = (sem("moe_silu"), sem("moe_act"), sem("moe_actT_psum"),
                                                               sem("moe_actT_hi"), sem("moe_actT_lo"))
        Y_hi_done, Y_lo_done, scattered = sem("Y_hi_done"), sem("Y_lo_done"), sem("scattered")
        x_added = sem("x_added")
        stored = sem("stored")

        R_AN, R_FN = 0, DEPTH * DC
        R_CV = 2 * DEPTH * DC
        R_LB = R_CV + DEPTH * 3 * CC
        R_HG = R_LB + DEPTH * CC
        NROWS = R_HG + DEPTH
        N_VEC, N_MASKS = 7, 9

        def col(r):
            return cols[:, r:r + 1]

        def conv_col(L, j, c):
            return col(R_CV + (L * 3 + j) * CC + c)

        def piece_view(t, s, parts, k):
            return t[0:parts, s, 0:k * COLS].rearrange("p (k n) -> p k n", k=k)

        SHAPE = {"proj_a": (HD, 4), "proj_b": (P, CC), "proj_c": (P, CC)}

        def source(L, m):
            name, c, c0 = ORDER[m]
            if c0 is not None:
                return w_in[L].rearrange("(k p) n -> p k n", p=P)[:, :, c0:c0 + COLS]
            w, p = {"proj_a": (w_proj_a, HD), "proj_b": (w_proj_b, P), "proj_c": (w_proj_c, P), "w_out": (w_out, P)}[name]
            return w[L].rearrange("(k p) n -> p k n", p=p)[:, :, c * COLS:(c + 1) * COLS]

        TOKEN_MAJOR = ("i", "q", "k", "v", "w_out")
        DEST = {"i": i_tm, "q": q_tm, "k": k_tm, "v": v_tm, "xb": xb, "cb": cb, "bb": bb}
        LAYERS = DEPTH if stop_at in (None, "mixer1") else 1

        def evacuated(eng, L, m):
            for q in (m - 1, m):
                eng.wait_ge(g_free[q % 2], L * (MIX // 2) + q // 2 + 1)

        def halves(t, h):
            v = t[:].rearrange("p c t -> p (c t)").rearrange("p (g w) -> p g w", w=2 * h)
            return v[:, :, 0:h], v[:, :, h:2 * h]

        def flat(t):
            return t.rearrange("p a b -> p (a b)")

        def h_bank(v, b):
            return ps[:, 2 * (v % 2) + b, :]

        def n_passes(eng):
            return eng.value_load(tab[0:1, PASSES:PASSES + 1], min_val=NE, max_val=PASSES)

        def m_piece(v, c):
            return 3 * v + c

        M_UNIT_PAIRS = (MOE_UNITS - 4) // 2
        assert PASS_PIECES % M_RAW == 0 and M_RAW == M_SPLIT == 2 * 3 and AHEAD == 3

        block = ctx.enter_context(nc.Block())

        @block.sync
        def _(sp):
            sp.dma_start(x[:], x_in[0].rearrange("(b p) d -> p b d", p=P)).then_inc(x_in_sem, 16)

            def load_mixer(L):
                for m in range(MIX):
                    p = BASE[L] + m
                    parts, k = SHAPE.get(ORDER[m][0], (P, DC))
                    if p >= RAW:
                        sp.wait_ge(lo_done, p - RAW + 1)
                    sp.dma_start(piece_view(raw, p % RAW, parts, k), source(L, m)).then_inc(landed[p % RAW], 16)

            w1 = dense_w1[0].rearrange("(k p) n -> p k n", p=P)
            w3 = dense_w3[0].rearrange("(k p) n -> p k n", p=P)
            w2 = dense_w2[0].rearrange("(u c p) n -> u p c n", p=P, c=2)

            def load_up(q, n, half, c0):
                slot = (DENSE0 + q) % RAW
                sp.wait_ge(lo_done, n * 3 + (DENSE0 + q - RAW + 1))
                dst = raw[:, slot, :].rearrange("p (k w n) -> p k w n", k=4, w=2)
                for w, src in enumerate((w1, w3)):
                    sp.dma_start(dst[:, :, w, :], src[:, 4 * half:4 * half + 4, c0]).then_inc(landed[slot], 16)

            def load_down(q, n, src):
                slot = (DENSE0 + q) % RAW
                sp.wait_ge(lo_done, n * 3 + (DENSE0 + q - RAW + 1))
                dst = raw[:, slot, :].rearrange("p (c n) -> p c n", c=2)
                for c in range(2):
                    sp.dma_start(dst[:, c, :], src[:, c, :]).then_inc(landed[slot], 16)

            def load_dense():
                for half in range(2):
                    load_up(half, 0, half, slice(0, COLS))
                with sp.Fori(0, DENSE_UNITS - 1) as n:
                    for half in range(2):
                        load_up(2 + half, n, half, bass.ds((n + 1) * COLS, COLS))
                    load_down(4, n, w2[n])
                load_down(DENSE - 1, 0, w2[DENSE_UNITS - 1])

            e1 = moe_w1[0].rearrange("e (k p) n -> e p k n", p=P)
            e3 = moe_w3[0].rearrange("e (k p) n -> e p k n", p=P)
            e2 = moe_w2[0].rearrange("e (u c p) n -> (e u) p c n", p=P, c=2)

            def moe_up(i, e, q, n, half, u):
                sp.wait_ge(m_raw_free, i * PASS_PIECES + n * 6 + (q + 1))
                dst = m_raw[q % M_RAW][:].rearrange("p (k w n) -> p k w n", k=4, w=2)
                for w, src in enumerate((e1, e3)):
                    sp.dma_start(dst[:, :, w, :], src[e, :, 4 * half:4 * half + 4, bass.ds(u * COLS, COLS)])\
                      .then_inc(m_landed[q % M_RAW], 16)

            def moe_down(i, e, q, n, u):
                sp.wait_ge(m_raw_free, i * PASS_PIECES + n * 6 + (q + 1))
                dst = m_raw[q % M_RAW][:].rearrange("p (c n) -> p c n", c=2)
                for c in range(2):
                    sp.dma_start(dst[:, c, :], e2[e * MOE_UNITS + u, :, c, :]).then_inc(m_landed[q % M_RAW], 16)

            def load_pass(i, e):
                for half in range(2):
                    moe_up(i, e, half, 0, half, 0)
                with sp.Fori(0, (MOE_UNITS - 2) // 2) as n:
                    for v in (1, 2):
                        for half in range(2):
                            moe_up(i, e, m_piece(v, half - 1), n, half, n * 2 + v)
                        moe_down(i, e, m_piece(v, 1), n, n * 2 + (v - 1))
                last = MOE_UNITS - 1
                for half in range(2):
                    moe_up(i, e, m_piece(last, half - 1), 0, half, last)
                moe_down(i, e, m_piece(last, 1), 0, last - 1)
                moe_down(i, e, m_piece(last, 2), 0, last)

            def load_moe():
                load_pass(0, 0)
                sp.wait_ge(table, 1)
                T = n_passes(sp)
                with sp.Fori(1, T) as i:
                    load_pass(i, sp.value_load(tab[0:1, bass.ds(i, 1)], min_val=0, max_val=NE - 1))
                for q in range(AHEAD):
                    sp.wait_ge(m_raw_free, T * PASS_PIECES + (q + 1))
                    for w, src in enumerate((e1, e3)):
                        sp.dma_start(m_raw[q][:, w * 16:(w + 1) * 16], src[0, :, 0, 0:16]).then_inc(m_landed[q], 16)
                sp.wait_ge(x_added, T * TB + TB)

            load_mixer(0)
            if stop_at != "mixer0":
                load_dense()
            if LAYERS == 2:
                load_mixer(1)
            if stop_at is None:
                load_moe()
            elif stop_at == "dense":
                sp.wait_ge(x_done, 2)
            else:
                evacuated(sp, LAYERS - 1, MIX - 1)
            sp.dma_start(out[0].rearrange("(b p) d -> p b d", p=P), x[:]).then_inc(stored, 16)
            sp.wait_ge(stored, 16)

        @block.gpsimd
        def _(pool):
            pool.dma_start(rows[R_AN:R_FN, :], attn_norm.rearrange("l (c p) -> (l c) p", p=P)).then_inc(vec_in, 16)
            pool.dma_start(rows[R_FN:R_CV, :], ffn_norm.rearrange("l (c p) -> (l c) p", p=P)).then_inc(vec_in, 16)
            pool.dma_start(rows[R_CV:R_LB, :], conv_w.rearrange("l j (c p) -> (l j c) p", p=P)).then_inc(vec_in, 16)
            pool.dma_start(rows[R_LB:R_HG, :], hgrn_lb.rearrange("l (c p) -> (l c) p", p=P)).then_inc(vec_in, 16)
            pool.dma_start(rows[R_HG:NROWS, :], hgrn_gain).then_inc(vec_in, 16)
            pool.dma_start(hrows[0:2, :], q_norm).then_inc(vec_in, 16)
            pool.dma_start(hrows[2:4, :], k_norm).then_inc(vec_in, 16)
            pool.dma_start(router[:], router_w[0].rearrange("(k p) e -> p k e", p=P)).then_inc(router_in, 16)
            pool.memset(ident[:], 0.0).then_inc(pool_step, 1)
            pool.memset(before[:], 1.0).then_inc(pool_step, 1)
            pool.memset(eps[:], EPS).then_inc(masks, 1)
            pool.iota(lane[:], pattern=[[1, P]], base=0, channel_multiplier=0,
                      allow_small_or_imprecise_dtypes=True).then_inc(masks, 1)
            pool.iota(part[:], pattern=[[0, 1]], base=0, channel_multiplier=1,
                      allow_small_or_imprecise_dtypes=True).then_inc(masks, 1)
            pool.iota(lane_i[:], pattern=[[1, P]], base=0, channel_multiplier=0).then_inc(masks, 1)
            pool.iota(part_i[:], pattern=[[0, 1]], base=0, channel_multiplier=1).then_inc(masks, 1)
            pool.iota(amask[:, 0:3 * P].bitcast(I32).rearrange("p (g j) -> p g j", g=3), pattern=[[0, 3], [-1, P]],
                      base=TOK, channel_multiplier=1).then_inc(masks, 1)
            pool.iota(amask[:, 3 * P:].bitcast(I32).rearrange("p (g j) -> p g j", g=3), pattern=[[0, 3], [-1, TOK]],
                      base=TOK + P, channel_multiplier=1).then_inc(masks, 1)
            pool.wait_ge(pool_step, 2)
            pool.affine_select(out=ident[:], in_=ident[:], compare_op=ALU.not_equal, fill=1.0, base=0,
                               pattern=[[-1, P]], channel_multiplier=1).then_inc(masks, 1)
            pool.affine_select(out=before[:], in_=before[:], compare_op=ALU.is_gt, fill=0.0, base=0,
                               pattern=[[1, P]], channel_multiplier=-1).then_inc(masks, 1)

            def level_diff(L, n):
                h = LEVELS[n]
                if n == 1:
                    pool.wait_ge(cum, L + 1)
                if n > 2:
                    pool.wait_ge(level_add, L * NLEV + n - 2)
                e1, e2 = halves(E[n % 2], h)
                b1, b2 = halves(bcum, h)
                mid = b1[:, :, h - 1:h].broadcast_to(b1.shape)
                pool.tensor_tensor(e1, mid, b1, ALU.subtract).then_inc(diff, 1)
                pool.tensor_tensor(e2, b2, mid, ALU.subtract).then_inc(diff, 1)

            def level_sum(L, n):
                pool.wait_ge(level_ev, L * (NLEV + 1) + n + 1)
                if n > 1:
                    pool.wait_ge(level_add, L * NLEV + n - 1)
                pool.tensor_tensor(flat(sc[:]), flat(sc[:]), flat(E[n % 2][:]), ALU.add).then_inc(level_add, 1)

            for L in range(LAYERS):
                level_diff(L, 1)
                level_diff(L, 2)
                for n in range(1, NLEV + 1):
                    level_sum(L, n)
                    if n + 2 <= NLEV:
                        level_diff(L, n + 2)
            if stop_at is None:
                evacuated(pool, DEPTH - 1, MIX - 1)
                pool.dma_start(gain_row[:], ffn_norm[DEPTH - 1:DEPTH, :].broadcast_to([P, D])).then_inc(gain_in, 16)
                pool.iota(iota8[:], pattern=[[1, NE]], base=0, channel_multiplier=0,
                          allow_small_or_imprecise_dtypes=True).then_inc(masks, 1)
                pool.memset(tri[:], 1.0).then_inc(pool_step, 1)
                pool.wait_ge(pool_step, 3)
                pool.affine_select(out=tri[:], in_=tri[:], compare_op=ALU.is_gt, fill=0.0, base=0,
                                   pattern=[[1, NE], [-1, NE]], channel_multiplier=0).then_inc(masks, 1)

        @block.scalar
        def _(act):
            A = nc.scalar.activation

            def hi(p, parts=P, n=PIECE):
                act.wait_ge(landed[p % RAW], landed_by(p))
                if p >= SPLIT:
                    act.wait_ge(used, p - SPLIT + 1)
                A(w_hi[0:parts, p % SPLIT, 0:n], raw[0:parts, p % RAW, 0:n], ACT.Copy).then_inc(hi_done, 1)

            def normalise(n):
                if n == 0:
                    act.wait_ge(x_in_sem, 16)
                elif n % 2:
                    evacuated(act, n // 2, MIX - 1)
                else:
                    act.wait_ge(x_done, TB)
                for b in range(TB):
                    A(h_tm[:, b, :], x[:, b, :], ACT.Square, scale=float(D) ** -0.5,
                      accum_out=ssq[:, b:b + 1]).then_inc(squared, 1)
                act.wait_ge(squared, TB * (n + 1))
                A(rstd[:], ssq[:], ACT.Sqrt, bias=eps[:, 0:1]).then_inc(x_root, 1)
                first = R_AN if n % 2 == 0 else R_FN
                for j in range(DC // 2):
                    act.wait_ge(hT_psum, (DC // 2) * n + j + 1)
                    for c in range(2):
                        A(hT_hi[:, 2 * j + c, :], ps[:, 2 + j, c * TOK:(c + 1) * TOK], ACT.Copy,
                          scale=col(first + (n // 2) * DC + 2 * j + c)).then_inc(hT_hi_done, 1)

            def evacuate(L, m):
                name, c, _ = ORDER[m]
                if name in ("proj_a", "proj_b", "proj_c", "w_out"):
                    return
                act.wait_ge(used, BASE[L] + m + 1)
                g, free = G[m % 2], g_free[m % 2]
                if name in ("i", "q", "k", "v"):
                    A(DEST[name][:, :, c * COLS:(c + 1) * COLS], g.rearrange("p (b n) -> p b n", b=TB),
                      ACT.Copy).then_inc(free, 1)
                    return
                g = g.rearrange("p (c t) -> p c t", c=2)
                two = slice(2 * c, 2 * c + 2)
                if name in ("xb", "cb", "bb"):
                    if name == "xb" and c == 0:
                        act.wait_ge(a_o, (L + 1) * SLOTS_PER_GROUP)
                    A(DEST[name][:, two, :], g, ACT.Copy).then_inc(free, 1)
                elif name == "f":
                    A(bcum[:, two, :], g, ACT.Sigmoid).then_inc(f_sig, 1)
                    A(kc[:, two, :], g, ACT.Sigmoid, scale=-1.0).then_inc(free, 1)
                elif name in ("qc", "g"):
                    A((qc if name == "qc" else gc)[:, two, :], g, ACT.Silu).then_inc(free, 1)
                elif name == "gate_c":
                    act.wait_ge(a_turn, (L + 1) * SLOTS_PER_GROUP)
                    A(sig_c[:, two, :], g, ACT.Sigmoid).then_inc(free, 1)
                else:
                    if name == "gate_b":
                        evacuated(act, L, FIRST["proj_a"] + c)
                    A(sig_ab[:, two, :], g, ACT.Sigmoid).then_inc(free, 1)

            def cross_exp(L):
                act.wait_ge(level_add, L * NLEV + NLEV - 1)
                A(E[0][:, :, P:TOK], bcum[:, :, P:TOK], ACT.Exp).then_inc(x_decay, 1)
                for c in range(CC):
                    A(E[0][:, c, 0:P], bcum[:, c, 0:P], ACT.Exp, scale=-1.0,
                      bias=bcum[:, c, P - 1:P]).then_inc(x_decay, 1)

            def attention(L, j, stage):
                n = L * SLOTS_PER_GROUP + j
                if stage == 0:
                    act.wait_ge(a_turn, n + 1)
                    A(qT[:], TA[0:HD, 0:W3], ACT.Copy, scale=hcols[:, L:L + 1]).then_inc(a_qk, 1)
                    A(kT[:], TA[0:HD, W3:2 * W3], ACT.Copy, scale=hcols[:, 2 + L:3 + L]).then_inc(a_qk, 1)
                elif stage == 1:
                    act.wait_ge(a_max, n + 1)
                    A(prob[:, 0:3 * P], prob[:, 0:3 * P], ACT.Exp, bias=smax[:, 0:1],
                      accum_out=den[:, 0:1]).then_inc(a_exp, 1)
                    A(prob[:, 3 * P:], prob[:, 3 * P:], ACT.Exp, bias=smax[:, 1:2],
                      accum_out=den[:, 1:2]).then_inc(a_exp, 1)
                elif stage == 2:
                    act.wait_ge(a_pturn, n + 1)
                    A(probT[:], TA[:, 0:NS], ACT.Copy).then_inc(a_pT, 1)

            def mixer(L):
                normalise(2 * L)
                for m in range(MIX + 2):
                    if m < MIX:
                        parts, k = SHAPE.get(ORDER[m][0], (P, DC))
                        hi(BASE[L] + m, parts, k * COLS)
                    if m >= 2:
                        evacuate(L, m - 2)
                    if m - 1 in ATTN_O_AT:
                        j = ATTN_O_AT[m - 1]
                        act.wait_ge(a_o, L * SLOTS_PER_GROUP + j + 1)
                        A(o_hi[:, j, :], SA[0:HD, 0:TOK], ACT.Copy).then_inc(a_ohi, 1)
                    if m - 1 in ATTN_AT:
                        attention(L, *ATTN_AT[m - 1])
                    if m in (FIRST["q"] + 5, FIRST["k"] + 5):
                        n = 2 * L + (1 if m == FIRST["q"] + 5 else 2)
                        act.wait_ge(qk_ss, n)
                        A(qkss[:], qkss[:], ACT.Sqrt, scale=1.0 / HD, bias=eps[:, 0:1]).then_inc(qk_root, 1)
                    if m == 18:
                        act.wait_ge(f_arg, L + 1)
                        A(bcum[:], bcum[:], ACT.Ln).then_inc(f_ln, 1)
                    if m + 1 in LEVEL_AT and LEVEL_AT[m + 1]:
                        n = LEVEL_AT[m + 1]
                        act.wait_ge(diff, 2 * (L * NLEV + n))
                        A(E[n % 2][:], E[n % 2][:], ACT.Exp).then_inc(decay, 1)
                    if m == CROSS_AT:
                        cross_exp(L)
                    if m == CROSS_AT + 1:
                        act.wait_ge(x_mm, L + 1)
                        A(scx[:], SA[:, 0:CC * P].rearrange("p (c t) -> p c t", c=CC), ACT.Copy).then_inc(x_ev, 1)
                    if m == HGRN_O_AT + 1:
                        act.wait_ge(o_mm, L + 1)
                        A(flat(E[1][:]), TA, ACT.Square).then_inc(o_sq, 1)
                    if m == HGRN_SS_AT + 1:
                        act.wait_ge(o_ss, L + 1)
                        A(flat(E[0][:]), SA, ACT.Sqrt, bias=eps[:, 0:1]).then_inc(o_root, 1)
                        act.wait_ge(o_gated, L + 1)
                        A(yc_hi[:], E[1][:], ACT.Copy).then_inc(yc_hi_done, 1)
                    if m == FIRST["bb"] + 5:
                        act.wait_ge(conv_y, L + 1)
                        A(yb_hi[:], xb[:], ACT.Copy).then_inc(conv_hi, 1)
                    if m >= 2 and ORDER[m - 2][0] == "proj_c":
                        c = ORDER[m - 2][1]
                        act.wait_ge(merge, 4 * L + c + 1)
                        A(hT_hi[:, 2 * c:2 * c + 2, :], merged[:, 2 * c:2 * c + 2, :], ACT.Copy).then_inc(merged_hi, 1)

            def dense():
                def hi_of(q, n):
                    p = DENSE0 + q
                    act.wait_ge(landed[p % RAW], n * 64 + landed_by(p))
                    act.wait_ge(used, n * 6 + (p - SPLIT + 1))
                    A(w_hi[:, p % SPLIT, :], raw[:, p % RAW, :], ACT.Copy).then_inc(hi_done, 1)

                def silu_of(v, n):
                    act.wait_ge(used, n * 6 + (DENSE0 + max(3 * v, 1) + 1))
                    for b in range(TB):
                        A(act_tm[:, b, :], h_bank(v, b)[:, 0:COLS], ACT.Silu).then_inc(silu, 1)

                def turned(v, n):
                    for b in range(TB):
                        act.wait_ge(aT_psum, n * 4 + (TB * v + b + 1))
                        A(flat(actT_hi[:, b]), h_bank(v, b)[:, 0:COLS], ACT.Copy).then_inc(aT_hi, 1)

                for q in range(2):
                    hi_of(q, 0)
                silu_of(0, 0)
                hi_of(2, 0)
                turned(0, 0)
                with act.Fori(0, (DENSE_UNITS - 1) // 2) as n:
                    for v in range(1, 3):
                        hi_of(3 * v, n)
                        hi_of(3 * v + 1, n)
                        silu_of(v, n)
                        hi_of(3 * v + 2, n)
                        turned(v, n)

            def moe():
                def hi_of(i, q, n):
                    act.wait_ge(m_landed[q % M_RAW], i * (32 * PASS_PIECES // M_RAW) + n * 32 + 32 * (q // M_RAW + 1))
                    act.wait_ge(m_split_free, i * PASS_PIECES + n * 6 + (q + 1))
                    A(m_hi[q % M_SPLIT][:], m_raw[q % M_RAW][:], ACT.Copy).then_inc(m_hi_done, 1)

                def silu_of(i, v, n):
                    act.wait_ge(m_split_free, i * PASS_PIECES + n * 6 + (M_SPLIT + max(m_piece(v, 0), 1) + 1))
                    A(m_act[:], ps[:, v % 2, 0:COLS], ACT.Silu).then_inc(m_silu, 1)

                def turned(i, v, n):
                    act.wait_ge(mT_psum, i * MOE_UNITS + n * 2 + (v + 1))
                    A(flat(mT_hi[:]), ps[:, v % 2, 0:COLS], ACT.Copy).then_inc(mT_hi_done, 1)

                def unit(i, v, n):
                    hi_of(i, m_piece(v, 0) + AHEAD, n)
                    hi_of(i, m_piece(v, 1) + AHEAD, n)
                    silu_of(i, v, n)
                    hi_of(i, m_piece(v, 2) + AHEAD, n)
                    turned(i, v, n)

                def gathered_hi(i):
                    act.wait_ge(gathered, i + 1)
                    A(XT_hi, XT_psum, ACT.Copy).then_inc(XT_hi_done, 1)

                act.wait_ge(router_in, 16)
                A(router_hi[:], router[:], ACT.Copy).then_inc(r_hi, 1)
                for q in range(AHEAD):
                    hi_of(0, q, 0)
                act.wait_ge(z_ready, 1)
                A(ez[:], ez[:], ACT.Exp).then_inc(z_exp, 1)
                act.wait_ge(table, 1)
                T = n_passes(act)
                gathered_hi(0)
                with act.Fori(0, T) as i:
                    unit(i, 0, 0)
                    unit(i, 1, 0)
                    act.wait_ge(sel_turned, i + 1)
                    A(selT[:], ps[:, 6, 0:TOK], ACT.Copy).then_inc(selT_done, 1)
                    with act.Fori(0, M_UNIT_PAIRS) as n:
                        for v in (2, 3):
                            unit(i, v, n)
                    for v in (MOE_UNITS - 2, MOE_UNITS - 1):
                        unit(i, v, 0)
                    gathered_hi(i + 1)
                    act.wait_ge(m_split_free, (i + 1) * PASS_PIECES + M_SPLIT)
                    act.wait_ge(gslot_done, i + 2)
                    A(Y_hi[:], flat(ps[:, 2:4, :]), ACT.Copy, scale=gslot[:, 0:1]).then_inc(Y_hi_done, 1)

            act.wait_ge(masks, N_MASKS)
            act.wait_ge(lb_diff, 1)
            A(lbt[:, 2:4, :], lbt[:, 0:2, :], ACT.Exp).then_inc(lb_exp, 1)
            mixer(0)
            if stop_at != "mixer0":
                normalise(1)
                dense()
            if LAYERS == 2:
                mixer(1)
            if stop_at is None:
                normalise(3)
                moe()

        @block.tensor
        def _(pe):
            mm = nc.tensor.matmul

            def turn(dst, src, n=P):
                return nc.tensor.transpose(dst, src, ident[0:n, 0:n])

            def split_mm(dst, a_hi, a_lo, b_hi, b_lo, first, last):
                mm(dst, a_hi, b_hi, start=first, stop=False)
                mm(dst, a_lo, b_hi, start=False, stop=False)
                return mm(dst, a_hi, b_lo, start=False, stop=last)

            def normalise(n):
                pe.wait_ge(h_ready, n + 1)
                for j in range(DC // 2):
                    for c in range(2):
                        for b in range(TB):
                            last = turn(ps[:, 2 + j, c * TOK + b * P:c * TOK + (b + 1) * P],
                                        h_tm[:, b, (2 * j + c) * P:(2 * j + c + 1) * P])
                    last.then_inc(hT_psum, 1)

            ACTS = {"proj_a": (o_hi, o_lo), "proj_b": (yb_hi, yb_lo), "proj_c": (yc_hi, yc_lo)}

            def piece(L, m):
                name, _, _ = ORDER[m]
                p = BASE[L] + m
                parts, k = SHAPE.get(name, (P, DC))
                if m == 0:
                    pe.wait_ge(hT_ready, 2 * L + 1)
                ready = {"proj_a": (a_olo, SLOTS_PER_GROUP * (L + 1)), "proj_b": (conv_lo, L + 1),
                         "proj_c": (yc_done, L + 1), "w_out": (merged_lo, 4 * (L + 1))}
                if name in ready and m == FIRST[name]:
                    pe.wait_ge(*ready[name])
                a_hi, a_lo = ACTS.get(name, (hT_hi, hT_lo))
                pe.wait_ge(lo_done, p + 1)
                pe.wait_ge(g_free[m % 2], L * (MIX // 2) + m // 2)
                wh, wl = (piece_view(t, p % SPLIT, parts, k) for t in (w_hi, w_lo))
                g = G[m % 2]
                for half in range(2):
                    dst = g[:, half * COLS:(half + 1) * COLS]
                    for c in range(k):
                        if name in TOKEN_MAJOR:
                            tok = slice(half * P, (half + 1) * P)
                            last = split_mm(dst, a_hi[:, c, tok], a_lo[:, c, tok], wh[:, c, :], wl[:, c, :],
                                            c == 0, c == k - 1)
                        else:
                            out_c = slice(half * P, (half + 1) * P)
                            last = split_mm(dst, wh[:, c, out_c], wl[:, c, out_c], a_hi[:, c, :], a_lo[:, c, :],
                                            c == 0, c == k - 1)
                last.then_inc(used, 1)

            def attention(L, j, stage):
                n = L * SLOTS_PER_GROUP + j
                heads = [g * SLOTS_PER_GROUP + j for g in range(len(GROUPS))]
                if stage == 0:
                    if j == 0:
                        pe.wait_ge(qk_normed, 2 * (L + 1))
                    pe.wait_ge(a_pT, n)
                    if L and j == 0:
                        pe.wait_ge(o_read, L)
                    for w, t in enumerate((q_tm, k_tm)):
                        for g, hd in enumerate(heads):
                            for b in range(TB):
                                o = w * W3 + g * TOK + b * P
                                last = turn(TA[0:HD, o:o + P], t[:, b, hd * HD:(hd + 1) * HD])
                    last.then_inc(a_turn, 1)
                elif stage == 1:
                    pe.wait_ge(a_qk, 2 * (n + 1))
                    pe.wait_ge(a_olo, n)
                    for g in range(3):
                        mm(SA[:, g * P:(g + 1) * P], qT[:, g * TOK:g * TOK + P], kT[:, g * TOK:g * TOK + P],
                           start=True, stop=True)
                    for g in range(3):
                        last = mm(SA[:, 512 + g * TOK:512 + (g + 1) * TOK], qT[:, g * TOK + P:(g + 1) * TOK],
                                  kT[:, g * TOK:(g + 1) * TOK], start=True, stop=True)
                    last.then_inc(a_score, 1)
                elif stage == 2:
                    pe.wait_ge(a_prob, n + 1)
                    for q in range(NS // P):
                        last = turn(TA[:, q * P:(q + 1) * P], prob[:, q * P:(q + 1) * P])
                    last.then_inc(a_pturn, 1)
                else:
                    if j == 0:
                        evacuated(pe, L, FIRST["v"] + 2)
                    pe.wait_ge(a_pT, n + 1)
                    for g, hd in enumerate(heads):
                        mm(SA[0:HD, 0:P], v_tm[:, 0, hd * HD:(hd + 1) * HD], probT[:, g * P:(g + 1) * P],
                           start=g == 0, stop=g == 2)
                    for g, hd in enumerate(heads):
                        for b in range(TB):
                            o = 3 * P + g * TOK + b * P
                            last = mm(SA[0:HD, P:TOK], v_tm[:, b, hd * HD:(hd + 1) * HD], probT[:, o:o + P],
                                      start=g == b == 0, stop=g == 2 and b == 1)
                    last.then_inc(a_o, 1)

            def level(L, n):
                if n == 0:
                    pe.wait_ge(kc_done, L + 1)
                    evacuated(pe, L, FIRST["qc"] + 2)
                    pe.wait_ge(a_olo, SLOTS_PER_GROUP * (L + 1))
                    left, right = kc, qc
                else:
                    pe.wait_ge(qk_level, 2 * (L * NLEV + n))
                    pe.wait_ge(level_ev, L * (NLEV + 1) + n)
                    left = right = E[n % 2]
                for c in range(CC):
                    for b in range(TB):
                        o = (c * TB + b) * P
                        last = mm(SA[:, o:o + P], left[:, c, b * P:(b + 1) * P], right[:, c, b * P:(b + 1) * P],
                                  start=True, stop=True)
                last.then_inc(level_mm, 1)

            def cross(L):
                pe.wait_ge(x_qk, 2 * (L + 1))
                pe.wait_ge(level_ev, (L + 1) * (NLEV + 1))
                for c in range(CC):
                    last = mm(SA[:, c * P:(c + 1) * P], E[0][:, c, 0:P], E[0][:, c, P:TOK], start=True, stop=True)
                last.then_inc(x_mm, 1)

            def hgrn_out(L):
                evacuated(pe, L, FIRST["i"] + 2)
                pe.wait_ge(level_add, (L + 1) * NLEV)
                pe.wait_ge(x_ev, L + 1)
                for c in range(CC):
                    hd = slice(c * P, (c + 1) * P)
                    mm(TA[:, c * TOK:c * TOK + P], i_tm[:, 0, hd], sc[:, c * TB, :], start=True, stop=True)
                    mm(TA[:, c * TOK + P:(c + 1) * TOK], i_tm[:, 0, hd], scx[:, c, :], start=True, stop=False)
                    last = mm(TA[:, c * TOK + P:(c + 1) * TOK], i_tm[:, 1, hd], sc[:, c * TB + 1, :],
                              start=False, stop=True)
                last.then_inc(o_mm, 1)

            def hgrn_ss(L):
                pe.wait_ge(o_sq, L + 1)
                for q in range(3):
                    last = mm(SA[:, q * 512:(q + 1) * 512], mean128[:], flat(E[1][:])[:, q * 512:(q + 1) * 512],
                              start=True, stop=True)
                last.then_inc(o_ss, 1)

            def mixer(L):
                normalise(2 * L)
                for m in range(MIX):
                    piece(L, m)
                    if m in ATTN_O_AT:
                        attention(L, ATTN_O_AT[m], 3)
                    if m in ATTN_AT:
                        attention(L, *ATTN_AT[m])
                    if m in LEVEL_AT:
                        level(L, LEVEL_AT[m])
                    if m == CROSS_AT:
                        cross(L)
                    if m == HGRN_O_AT:
                        hgrn_out(L)
                    if m == HGRN_SS_AT:
                        hgrn_ss(L)

            def dense():
                Y = [ps[:, 4 + b * 2 + h, :] for b in range(TB) for h in range(2)]

                def up(v, n):
                    for half in range(2):
                        p = DENSE0 + (half if v == 0 else 3 * v - 1 + half)
                        pe.wait_ge(lo_done, n * 6 + (p + 1))
                        wh, wl = (t[:, p % SPLIT, :].rearrange("p (k n) -> p k n", k=4) for t in (w_hi, w_lo))
                        for b in range(TB):
                            if half == 0 and v > 1:
                                pe.wait_ge(aT_lo, n * 4 + (TB * (v - 2) + b + 1))
                            tok = slice(b * P, (b + 1) * P)
                            for c in range(4):
                                k = 4 * half + c
                                last = split_mm(h_bank(v, b), hT_hi[:, k, tok], hT_lo[:, k, tok], wh[:, c, :], wl[:, c, :],
                                                k == 0, k == DC - 1)
                        last.then_inc(used, 1)

                def down(v, n, first=False, final=False):
                    p = DENSE0 + (DENSE - 1 if final else 3 * (v + 1) + 1)
                    pe.wait_ge(lo_done, n * 6 + (p + 1))
                    pe.wait_ge(aT_lo, n * 4 + TB * (v + 1))
                    wh, wl = (t[:, p % SPLIT, :].rearrange("p (c h n) -> p c h n", c=2, h=2) for t in (w_hi, w_lo))
                    for b in range(TB):
                        for c in range(2):
                            for h in range(2):
                                last = split_mm(Y[b * 2 + h], actT_hi[:, b, c, :], actT_lo[:, b, c, :], wh[:, c, h, :],
                                                wl[:, c, h, :], first and c == 0, final and c == 1)
                    last.then_inc(used, 1)

                def turn_act(v, n):
                    for b in range(TB):
                        pe.wait_ge(act_done, n * 4 + (TB * v + b + 1))
                        for c in range(2):
                            last = turn(h_bank(v, b)[:, c * P:(c + 1) * P], act_tm[:, b, c * P:(c + 1) * P])
                        last.then_inc(aT_psum, 1)

                up(0, 0)
                turn_act(0, 0)
                for v in (1, 2):
                    up(v, 0)
                    down(v - 1, 0, first=v == 1)
                    turn_act(v, 0)
                with pe.Fori(0, (DENSE_UNITS - 3) // 2) as n:
                    for v in (3, 4):
                        up(v, n)
                        down(v - 1, n)
                        turn_act(v, n)
                down(DENSE_UNITS - 1, 0, final=True)

            def moe():
                pe.sem_inc(m_split_free, M_SPLIT)
                pe.wait_ge(r_lo, 1)
                for b in range(TB):
                    tok = slice(b * P, (b + 1) * P)
                    for k in range(DC):
                        last = split_mm(ps[:, 2, b * NE:(b + 1) * NE], hT_hi[:, k, tok], hT_lo[:, k, tok],
                                        router_hi[:, k, :], router_lo[:, k, :], k == 0, k == DC - 1)
                last.then_inc(logits, 1)
                pe.wait_ge(chosen_ready, 1)
                mm(ps[:, 3, 0:NE], before[:], chosen[:, 0, :], start=True, stop=True)
                mm(ps[:, 3, NE:2 * NE], before[:], chosen[:, 1, :], start=True, stop=False)
                mm(ps[:, 3, NE:2 * NE], ones[:], chosen[:, 0, :], start=False, stop=True)
                mm(ps[:, 3, 2 * NE:3 * NE], ones[:], chosen[:, 0, :], start=True, stop=False)
                mm(ps[:, 3, 2 * NE:3 * NE], ones[:], chosen[:, 1, :], start=False, stop=True).then_inc(counted, 1)
                pe.wait_ge(hg, 1)
                pe.wait_ge(table, 1)
                T = n_passes(pe)

                def gather(i):
                    pe.wait_ge(sel_built, i + 1)
                    for k in range(DC):
                        for b in range(TB):
                            last = mm(XT_psum[:, k, :], h_tm[:, b, k * P:(k + 1) * P], sel01[:, b, :],
                                      start=b == 0, stop=b == TB - 1)
                    last.then_inc(gathered, 1)

                def turn_sel(i):
                    pe.wait_ge(x_added, i * TB + TB)
                    for b in range(TB):
                        turn(ps[:, 6, b * P:(b + 1) * P], sel01[:, b, :])
                    for b in range(TB):
                        last = mm(ps[:, 7, 0:1], sel01[:, b, :], GATE[:, bass.ds(i, 1), b], start=b == 0, stop=b == TB - 1)
                    last.then_inc(sel_turned, 1)

                def scatter(i):
                    pe.wait_ge(Y_lo_done, i + 1)
                    pe.wait_ge(selT_done, i + 1)
                    pe.wait_ge(gslot_done, i + 1)
                    for b in range(TB):
                        for h in range(2):
                            half = slice(h * 512, (h + 1) * 512)
                            for y in (Y_hi, Y_lo):
                                last = mm(ps[:, 4 + 2 * b + h, :], selT[:, b * P:(b + 1) * P], y[:, half],
                                          start=y is Y_hi, stop=y is Y_lo)
                        last.then_inc(scattered, 1)

                def up(i, v, n):
                    if v > 1:
                        pe.wait_ge(mT_lo_done, i * MOE_UNITS + n * 2 + (v - 1))
                    for half in range(2):
                        q = m_piece(v, half - 1) if v else half
                        pe.wait_ge(m_raw_free, i * PASS_PIECES + n * 6 + (M_RAW + q + 1))
                        wh, wl = (t[q % M_SPLIT][:].rearrange("p (k n) -> p k n", k=4) for t in (m_hi, m_lo))
                        for c in range(4):
                            k = 4 * half + c
                            last = split_mm(ps[:, v % 2, :], XT_hi[:, k, :], XT_lo[:, k, :], wh[:, c, :], wl[:, c, :],
                                            k == 0, k == DC - 1)
                        last.then_inc(m_split_free, 1)

                def down(i, v, n):
                    q = m_piece(v + 1, 1) if v < MOE_UNITS - 1 else PASS_PIECES - 1
                    pe.wait_ge(m_raw_free, i * PASS_PIECES + n * 6 + (M_RAW + q + 1))
                    pe.wait_ge(mT_lo_done, i * MOE_UNITS + n * 2 + (v + 1))
                    wh, wl = (t[q % M_SPLIT][:].rearrange("p (c h n) -> p c h n", c=2, h=2) for t in (m_hi, m_lo))
                    for c in range(2):
                        for h in range(2):
                            last = split_mm(ps[:, 2 + h, :], mT_hi[:, c, :], mT_lo[:, c, :], wh[:, c, h, :],
                                            wl[:, c, h, :], v == 0 and c == 0, v == MOE_UNITS - 1 and c == 1)
                    last.then_inc(m_split_free, 1)

                def turn_act(i, v, n):
                    pe.wait_ge(m_act_done, i * MOE_UNITS + n * 2 + (v + 1))
                    for c in range(2):
                        last = turn(ps[:, v % 2, c * P:(c + 1) * P], m_act[:, c * P:(c + 1) * P])
                    last.then_inc(mT_psum, 1)

                def unit(i, v, n):
                    up(i, v, n)
                    down(i, v - 1, n)
                    turn_act(i, v, n)

                gather(0)
                with pe.Fori(0, T) as i:
                    pe.wait_ge(XT_lo_done, i + 1)
                    up(i, 0, 0)
                    scatter(i)
                    turn_act(i, 0, 0)
                    unit(i, 1, 0)
                    turn_sel(i)
                    unit(i, 2, 0)
                    unit(i, 3, 0)
                    with pe.Fori(0, M_UNIT_PAIRS - 1) as n:
                        for v in (4, 5):
                            unit(i, v, n)
                    for v in (MOE_UNITS - 2, MOE_UNITS - 1):
                        unit(i, v, 0)
                    gather(i + 1)
                    down(i, MOE_UNITS - 1, 0)
                pe.wait_ge(XT_lo_done, T + 1)
                scatter(T)

            pe.wait_ge(vec_in, 16 * N_VEC)
            pe.wait_ge(masks, N_MASKS)
            turn(ps[:, 7, 0:NROWS], rows[0:NROWS, :], NROWS).then_inc(vec_T, 1)
            turn(ps[0:HD, 6, 0:4], hrows[:, :], 4).then_inc(vec_T, 1)
            mixer(0)
            if stop_at != "mixer0":
                normalise(1)
                pe.wait_ge(hT_ready, 2)
                dense()
            if LAYERS == 2:
                mixer(1)
            if stop_at is None:
                normalise(3)
                pe.wait_ge(hT_ready, 2 * DEPTH)
                moe()

        @block.vector
        def _(dve):
            V = nc.vector
            steps = {"n": 0}

            def link(ins):
                steps["n"] += 1
                ins.then_inc(dve_step, 1)
                dve.wait_ge(dve_step, steps["n"])

            def lo(p, parts=P, n=PIECE):
                dve.wait_ge(hi_done, p + 1)
                V.tensor_tensor(w_lo[0:parts, p % SPLIT, 0:n], raw[0:parts, p % RAW, 0:n],
                                w_hi[0:parts, p % SPLIT, 0:n].bitcast(F32), ALU.subtract).then_inc(lo_done, 1)

            def constants():
                dve.wait_ge(masks, N_MASKS)
                V.memset(ones[:], 1.0)
                V.memset(mean128[:], 1.0 / P)
                V.memset(lbm[:, 0, :], LB_FLOOR)
                V.memset(oml[:, 0, :], 1.0)
                V.memset(kfix[:, 0, :], LB_FLOOR)
                dve.wait_ge(vec_T, 2)
                V.tensor_copy(cols[:, 0:NROWS], ps[:, 7, 0:NROWS])
                link(V.tensor_copy(hcols[:], ps[0:HD, 6, 0:4]))
                a0, a1 = cols[:, R_LB:R_LB + CC], cols[:, R_LB + CC:R_LB + 2 * CC]
                link(V.tensor_tensor(lbt[:, 2, :], a0, a1, ALU.max))
                V.tensor_tensor(lbt[:, 0, :], a0, lbt[:, 2, :], ALU.subtract)
                V.tensor_tensor(lbt[:, 1, :], a1, lbt[:, 2, :], ALU.subtract).then_inc(lb_diff, 1)
                dve.wait_ge(lb_exp, 1)
                link(V.tensor_tensor(lbt[:, 0, :], lbt[:, 2, :], lbt[:, 3, :], ALU.add))
                link(V.reciprocal(lbt[:, 1, :], lbt[:, 0, :]))
                V.tensor_tensor(oml[:, 1, :], lbt[:, 2, :], lbt[:, 1, :], ALU.mult)
                link(V.tensor_tensor(lbt[:, 0, :], lbt[:, 3, :], lbt[:, 1, :], ALU.mult))
                link(V.tensor_scalar(lbm[:, 1, :], lbt[:, 0, :], LB_FLOOR, None, ALU.max))
                link(V.tensor_tensor(kfix[:, 1, :], lbm[:, 1, :], lbt[:, 0, :], ALU.subtract))

            def attention_masks():
                for at0, n in ((0, P), (3 * P, TOK)):
                    for g, (window, dilation) in enumerate(GROUPS):
                        d = amask[:, at0 + g * n:at0 + (g + 1) * n]
                        ok, dist, rem = E[0][:, 0, 0:n], E[0][:, 1, 0:n], E[1][:, 0, 0:n].bitcast(I32)
                        link(V.tensor_copy(dist, d.bitcast(I32)))
                        link(V.tensor_scalar(ok, dist, float(TOK), None, ALU.is_ge))
                        if dilation > 1:
                            link(V.tensor_scalar(rem, d.bitcast(I32), dilation - 1, None, ALU.bitwise_and))
                            link(V.tensor_copy(dist, rem))
                            link(V.scalar_tensor_tensor(ok, dist, 0.0, ok, ALU.is_equal, ALU.mult))
                        if window < TOK:
                            link(V.scalar_tensor_tensor(ok, dist, float(TOK + window), ok, ALU.is_le, ALU.mult))
                        link(V.tensor_scalar(d, ok, 1.0, -NEG_BIG, ALU.subtract, ALU.mult))

            def level_masks():
                V.tensor_copy(hmask[:, 0, :], ident[:])
                for n in range(1, NLEV + 1):
                    h = LEVELS[n]
                    rem, start = E[0][:, 0, 0:P], E[1][:, 0, 0:P]
                    s_rem, s_start, s_first = (scol[:, q:q + 1] for q in range(3))
                    V.tensor_scalar(E[0][:, 1, 0:P].bitcast(I32), lane_i[:], 2 * h - 1, None, ALU.bitwise_and)
                    link(V.tensor_scalar(scol[:, 3:4].bitcast(I32), part_i[:], 2 * h - 1, None, ALU.bitwise_and))
                    V.tensor_copy(rem, E[0][:, 1, 0:P].bitcast(I32))
                    link(V.tensor_copy(s_rem, scol[:, 3:4].bitcast(I32)))
                    V.tensor_tensor(start, lane[:], rem, ALU.subtract)
                    V.tensor_tensor(s_start, part[:], s_rem, ALU.subtract)
                    link(V.tensor_scalar(s_first, s_rem, float(h), None, ALU.is_lt))
                    link(V.tensor_scalar(hmask[:, n, :], start, s_start, s_first, ALU.is_equal, ALU.mult))
                    link(V.scalar_tensor_tensor(hmask[:, n, :], rem, float(h), hmask[:, n, :], ALU.is_ge, ALU.mult))

            def normalise(n):
                dve.wait_ge(x_root, n + 1)
                link(V.reciprocal(rstd[:], rstd[:]))
                for b in range(TB):
                    last = V.tensor_scalar(h_tm[:, b, :], x[:, b, :], rstd[:, b:b + 1], None, ALU.mult)
                last.then_inc(h_ready, 1)
                first = (R_AN if n % 2 == 0 else R_FN) + (n // 2) * DC
                for k in range(DC):
                    dve.wait_ge(hT_hi_done, DC * n + 2 * (k // 2) + 2)
                    last = V.scalar_tensor_tensor(hT_lo[:, k, :], ps[:, 2 + k // 2, (k % 2) * TOK:(k % 2 + 1) * TOK],
                                                  col(first + k), hT_hi[:, k, :].bitcast(F32), ALU.mult, ALU.subtract)
                last.then_inc(hT_ready, 1)

            def evacuate(L, m):
                name, c, _ = ORDER[m]
                if name not in ("proj_a", "proj_b", "proj_c", "w_out"):
                    return
                dve.wait_ge(used, BASE[L] + m + 1)
                g, free = G[m % 2], g_free[m % 2]
                if name == "w_out":
                    xs = x[:, :, c * COLS:(c + 1) * COLS]
                    V.tensor_tensor(xs, g.rearrange("p (b n) -> p b n", b=TB), xs, ALU.add).then_inc(free, 1)
                    return
                g = g.rearrange("p (c t) -> p c t", c=2)
                two = slice(2 * c, 2 * c + 2)
                gate = {"proj_a": "gate_a", "proj_b": "gate_b", "proj_c": "gate_c"}[name]
                evacuated(dve, L, FIRST[gate] + c)
                if name == "proj_a":
                    V.tensor_tensor(merged[:, two, :], g, sig_ab[:, two, :], ALU.mult).then_inc(free, 1)
                    return
                V.tensor_tensor(term[:], g, (sig_ab if name == "proj_b" else sig_c)[:, two, :], ALU.mult).then_inc(free, 1)
                evacuated(dve, L, m)
                last = V.tensor_tensor(merged[:, two, :], merged[:, two, :], term[:], ALU.add)
                if name == "proj_b":
                    link(last)
                else:
                    last.then_inc(merge, 1)
                    dve.wait_ge(merged_hi, 4 * L + c + 1)
                    V.tensor_tensor(hT_lo[:, two, :], merged[:, two, :], hT_hi[:, two, :].bitcast(F32),
                                    ALU.subtract).then_inc(merged_lo, 1)

            def qk_norm(L, t, name):
                evacuated(dve, L, FIRST[name] + 2)
                v = t[:].rearrange("p b (h e) -> p (b h) e", e=HD)
                sq = flat(E[0][:]).rearrange("p (h e) -> p h e", e=HD)
                link(V.tensor_tensor(sq, v, v, ALU.mult))
                V.tensor_reduce(qkss[:], sq, AX, ALU.add).then_inc(qk_ss, 1)
                dve.wait_ge(qk_root, 2 * L + (1 if name == "q" else 2))
                link(V.reciprocal(qkss[:], qkss[:]))
                V.tensor_tensor(v, v, qkss[:].rearrange("p (h o) -> p h o", o=1).broadcast_to(v.shape),
                                ALU.mult).then_inc(qk_normed, 1)
                dve.wait_ge(qk_normed, 2 * L + (1 if name == "q" else 2))

            def forget(L):
                evacuated(dve, L, FIRST["f"] + 2)
                for c in range(CC):
                    V.tensor_scalar(kc[:, c, :], kc[:, c, :], oml[:, L, c:c + 1], kfix[:, L, c:c + 1],
                                    ALU.mult, ALU.subtract)
                    last = V.tensor_scalar(bcum[:, c, :], bcum[:, c, :], oml[:, L, c:c + 1], lbm[:, L, c:c + 1],
                                           ALU.mult, ALU.add)
                last.then_inc(kc_done, 1)
                dve.wait_ge(kc_done, L + 1)
                link(V.tensor_scalar(E[0][:], bcum[:], 2.0 ** -LN_SHIFT, None, ALU.is_lt))
                link(V.tensor_scalar(E[1][:], E[0][:], 2.0 ** LN_SHIFT, 1.0, ALU.mult, ALU.max))
                V.tensor_tensor(bcum[:], bcum[:], E[1][:], ALU.mult).then_inc(f_arg, 1)

            def cumulate(L):
                dve.wait_ge(f_ln, L + 1)
                link(V.scalar_tensor_tensor(bcum[:], E[0][:], -LN_SHIFT * LN2, bcum[:], ALU.mult, ALU.add))
                for c in range(CC):
                    for b in range(TB):
                        s = bcum[:, c, b * P:(b + 1) * P]
                        last = V.tensor_tensor_scan(s, ones[:], s, 0.0, ALU.mult, ALU.add)
                last.then_inc(cum, 1)

            def level_read(L, n):
                dve.wait_ge(level_mm, L * (NLEV + 1) + n + 1)
                dst = sc[:] if n == 0 else flat(E[n % 2][:]).rearrange("p (a t) -> p a t", t=P)
                V.tensor_tensor(dst, SA.rearrange("p (a t) -> p a t", t=P),
                                hmask[:, n:n + 1, :].broadcast_to([P, CC * TB, P]), ALU.mult).then_inc(level_ev, 1)

            def level_qk(L, n):
                h = LEVELS[n]
                dve.wait_ge(decay, L * NLEV + n)
                e1, e2 = halves(E[n % 2], h)
                V.tensor_tensor(e1, e1, halves(kc, h)[0], ALU.mult).then_inc(qk_level, 1)
                V.tensor_tensor(e2, e2, halves(qc, h)[1], ALU.mult).then_inc(qk_level, 1)

            def cross_qk(L):
                dve.wait_ge(x_decay, (L + 1) * (CC + 1))
                V.tensor_tensor(E[0][:, :, 0:P], E[0][:, :, 0:P], kc[:, :, 0:P], ALU.mult).then_inc(x_qk, 1)
                V.tensor_tensor(E[0][:, :, P:TOK], E[0][:, :, P:TOK], qc[:, :, P:TOK], ALU.mult).then_inc(x_qk, 1)

            def hgrn_gate(L):
                dve.wait_ge(o_root, L + 1)
                evacuated(dve, L, FIRST["g"] + 2)
                link(V.reciprocal(E[0][:], E[0][:]))
                V.scalar_tensor_tensor(flat(E[1][:]), TA, col(R_HG + L), flat(E[0][:]), ALU.mult,
                                       ALU.mult).then_inc(o_read, 1)
                dve.wait_ge(o_read, L + 1)
                V.tensor_tensor(E[1][:], E[1][:], gc[:], ALU.mult).then_inc(o_gated, 1)

            def attention(L, j):
                n = L * SLOTS_PER_GROUP + j
                parts = ((slice(0, 3 * P), SA[:, 0:3 * P]), (slice(3 * P, NS), SA[:, 512:512 + W3]))
                dve.wait_ge(a_score, n + 1)
                dve.wait_ge(a_pturn, n)
                for s, scores in parts:
                    last = V.scalar_tensor_tensor(prob[:, s], scores, float(HD) ** -0.5, amask[:, s], ALU.mult, ALU.add)
                link(last)
                for b, (s, _) in enumerate(parts):
                    last = V.tensor_reduce(smax[:, b:b + 1], prob[:, s], AX, ALU.max)
                link(last)
                V.tensor_scalar(smax[:], smax[:], -1.0, None, ALU.mult).then_inc(a_max, 1)
                dve.wait_ge(a_exp, 2 * (n + 1))
                link(V.reciprocal(rden[:], den[:]))
                for b, (s, _) in enumerate(parts):
                    last = V.tensor_scalar(prob[:, s], prob[:, s], rden[:, b:b + 1], None, ALU.mult)
                last.then_inc(a_prob, 1)

            def conv(L):
                evacuated(dve, L, FIRST["cb"] + 2)
                link(V.tensor_tensor(xb[:], xb[:], cb[:], ALU.mult))
                for c in range(CC):
                    last = V.tensor_scalar(cb[:, c, :], xb[:, c, :], conv_col(L, 0, c), None, ALU.mult)
                link(last)
                for j in range(1, conv_w.shape[1]):
                    for c in range(CC):
                        y = cb[:, c, j:TOK]
                        last = V.scalar_tensor_tensor(y, xb[:, c, 0:TOK - j], conv_col(L, j, c), y, ALU.mult, ALU.add)
                    link(last)

            def mixer(L):
                normalise(2 * L)
                for m in range(MIX + 2):
                    if m < MIX:
                        parts, k = SHAPE.get(ORDER[m][0], (P, DC))
                        lo(BASE[L] + m, parts, k * COLS)
                    if m >= 2:
                        evacuate(L, m - 2)
                    if L == 0 and m == 1:
                        attention_masks()
                    if L == 0 and m == 15:
                        level_masks()
                    if m == FIRST["q"] + 5:
                        qk_norm(L, q_tm, "q")
                    if m == FIRST["k"] + 5:
                        qk_norm(L, k_tm, "k")
                    if m - 1 in ATTN_O_AT:
                        j = ATTN_O_AT[m - 1]
                        dve.wait_ge(a_ohi, L * SLOTS_PER_GROUP + j + 1)
                        V.tensor_tensor(o_lo[:, j, :], SA[0:HD, 0:TOK], o_hi[:, j, :].bitcast(F32),
                                        ALU.subtract).then_inc(a_olo, 1)
                    if m - 1 in ATTN_AT and ATTN_AT[m - 1][1] == 1:
                        attention(L, ATTN_AT[m - 1][0])
                    if m == 17:
                        forget(L)
                    if m == 19:
                        cumulate(L)
                    if m - 1 in LEVEL_AT:
                        level_read(L, LEVEL_AT[m - 1])
                    if m in LEVEL_AT and LEVEL_AT[m]:
                        level_qk(L, LEVEL_AT[m])
                    if m == CROSS_AT:
                        cross_qk(L)
                    if m == HGRN_SS_AT + 1:
                        hgrn_gate(L)
                    if m == HGRN_SS_AT + 2:
                        dve.wait_ge(yc_hi_done, L + 1)
                        V.tensor_tensor(yc_lo[:], E[1][:], yc_hi[:].bitcast(F32), ALU.subtract).then_inc(yc_done, 1)
                    if m == FIRST["cb"] + 5:
                        conv(L)
                    if m == FIRST["bb"] + 5:
                        evacuated(dve, L, FIRST["bb"] + 2)
                        V.tensor_tensor(xb[:], cb[:], bb[:], ALU.mult).then_inc(conv_y, 1)
                    if m == FIRST["bb"] + 7:
                        dve.wait_ge(conv_hi, L + 1)
                        V.tensor_tensor(yb_lo[:], xb[:], yb_hi[:].bitcast(F32), ALU.subtract).then_inc(conv_lo, 1)

            def dense():
                def lo_of(q, n):
                    p = DENSE0 + q
                    dve.wait_ge(hi_done, n * 6 + (p + 1))
                    V.tensor_tensor(w_lo[:, p % SPLIT, :], raw[:, p % RAW, :], w_hi[:, p % SPLIT, :].bitcast(F32),
                                    ALU.subtract).then_inc(lo_done, 1)

                def gate_up(v, n):
                    for b in range(TB):
                        dve.wait_ge(silu, n * 4 + (TB * v + b + 1))
                        V.tensor_tensor(act_tm[:, b, :], act_tm[:, b, :], h_bank(v, b)[:, COLS:2 * COLS],
                                        ALU.mult).then_inc(act_done, 1)

                def turned(v, n):
                    for b in range(TB):
                        dve.wait_ge(aT_hi, n * 4 + (TB * v + b + 1))
                        V.tensor_tensor(flat(actT_lo[:, b]), h_bank(v, b)[:, 0:COLS],
                                        flat(actT_hi[:, b]).bitcast(F32), ALU.subtract).then_inc(aT_lo, 1)

                for q in range(2):
                    lo_of(q, 0)
                gate_up(0, 0)
                lo_of(2, 0)
                turned(0, 0)
                with dve.Fori(0, (DENSE_UNITS - 1) // 2) as n:
                    for v in range(1, 3):
                        lo_of(3 * v, n)
                        lo_of(3 * v + 1, n)
                        gate_up(v, n)
                        lo_of(3 * v + 2, n)
                        turned(v, n)
                dve.wait_ge(used, DENSE0 + DENSE)
                for b in range(TB):
                    V.tensor_tensor(x[:, b, :], x[:, b, :], flat(ps[:, 4 + 2 * b:6 + 2 * b, :]), ALU.add).then_inc(x_done, 1)
                dve.wait_ge(x_done, TB)

            def moe():
                dve.wait_ge(r_hi, 1)
                V.tensor_tensor(router_lo[:], router[:], router_hi[:].bitcast(F32), ALU.subtract).then_inc(r_lo, 1)
                def lo_of(i, q, n):
                    dve.wait_ge(m_hi_done, i * PASS_PIECES + n * 6 + (q + 1))
                    V.tensor_tensor(m_lo[q % M_SPLIT][:], m_raw[q % M_RAW][:], m_hi[q % M_SPLIT][:].bitcast(F32),
                                    ALU.subtract).then_inc(m_raw_free, 1)

                dve.wait_ge(gain_in, 16)
                for b in range(TB):
                    last = V.tensor_tensor(h_tm[:, b, :], h_tm[:, b, :], gain_row[:], ALU.mult)
                last.then_inc(hg, 1)
                for q in range(AHEAD):
                    lo_of(0, q, 0)
                dve.wait_ge(masks, N_MASKS + 2)
                dve.wait_ge(logits, 1)
                link(V.tensor_copy(flat(logit[:]), ps[:, 2, 0:TB * NE]))
                other = logit[:].rearrange("p b (o e) -> p b o e", o=1).broadcast_to([P, TB, NE, NE])
                own = logit[:].rearrange("p b (e o) -> p b e o", o=1).broadcast_to([P, TB, NE, NE])
                V.tensor_tensor(gt[:], other, own, ALU.is_gt)
                link(V.tensor_tensor(eq[:], other, own, ALU.is_equal))
                link(V.tensor_tensor(eq[:], eq[:], tri[:].rearrange("p (o e) f -> p o e f", o=1)
                                     .broadcast_to([P, TB, NE, NE]), ALU.mult))
                link(V.tensor_tensor(gt[:], gt[:], eq[:], ALU.add))
                link(V.tensor_reduce(rank[:], gt[:], AX, ALU.add))
                V.tensor_scalar(chosen[:], rank[:], 1.5, None, ALU.is_lt).then_inc(chosen_ready, 1)
                link(V.tensor_reduce(lmax[:], logit[:], AX, ALU.max))
                V.tensor_tensor(ez[:], logit[:], lmax[:].rearrange("p (b o) -> p b o", o=1).broadcast_to([P, TB, NE]),
                                ALU.subtract).then_inc(z_ready, 1)
                dve.wait_ge(z_exp, 1)
                link(V.tensor_tensor(ez[:], ez[:], chosen[:], ALU.mult))
                link(V.tensor_reduce(esum[:], ez[:], AX, ALU.add))
                link(V.reciprocal(esum[:], esum[:]))
                link(V.tensor_tensor(gate[:], ez[:], esum[:].rearrange("p (b o) -> p b o", o=1)
                                     .broadcast_to([P, TB, NE]), ALU.mult))
                dve.wait_ge(counted, 1)
                link(V.scalar_tensor_tensor(flat(place[:]), ps[:, 3, 0:TB * NE], 1000.0, flat(chosen[:]), ALU.add, ALU.mult))
                link(V.tensor_scalar(place[:], place[:], 1000.0, None, ALU.subtract))
                link(V.tensor_scalar(over[:], ps[:, 3, TB * NE:(TB + 1) * NE], P + 0.5, None, ALU.is_gt))
                link(V.tensor_tensor_scan(over_n[:], ones[:, 0:NE], over[:], 0.0, ALU.mult, ALU.add))
                link(V.tensor_scalar(tabf[:, PASSES:PASSES + 1], over_n[:, NE - 1:NE], float(NE), None, ALU.add))
                link(V.tensor_tensor(over_n[:], over_n[:], over[:], ALU.subtract))
                for j in range(OVER):
                    last = V.scalar_tensor_tensor(pick[:, j, :], over_n[:], float(j), over[:], ALU.is_equal, ALU.mult)
                link(last)
                for t, tb, shift in ((POS, place, float(P)), (GATE, gate, 0.0)):
                    V.tensor_copy(t[:, 0:NE, :].rearrange("p e b -> p b e"), tb[:])
                    for b in range(TB):
                        last = V.tensor_tensor(tmp8[:, b], pick[:], tb[:, b:b + 1, :].broadcast_to([P, OVER, NE]), ALU.mult)
                    link(last)
                    o = t[:, NE:PASSES, :].rearrange("p j b -> p b j")
                    link(V.tensor_reduce(o, tmp8[:], AX, ALU.add))
                    link(V.tensor_scalar(o, o, shift, None, ALU.subtract))
                V.tensor_copy(tabf[:, 0:NE], iota8[:])
                link(V.tensor_tensor(tmp8[:, 0], pick[:], iota8[:].rearrange("p (o e) -> p o e", o=1)
                                     .broadcast_to([P, OVER, NE]), ALU.mult))
                link(V.tensor_reduce(tabf[:, NE:PASSES], tmp8[:, 0], AX, ALU.add))
                V.memset(POS[:, PASSES, :], -1.0)
                V.tensor_copy(tab[:], tabf[:]).then_inc(table, 1)
                dve.wait_ge(table, 1)
                T = n_passes(dve)

                def gate_up(i, v, n):
                    dve.wait_ge(m_silu, i * MOE_UNITS + n * 2 + (v + 1))
                    V.tensor_tensor(m_act[:], m_act[:], ps[:, v % 2, COLS:2 * COLS], ALU.mult).then_inc(m_act_done, 1)

                def turned(i, v, n):
                    dve.wait_ge(mT_hi_done, i * MOE_UNITS + n * 2 + (v + 1))
                    V.tensor_tensor(flat(mT_lo[:]), ps[:, v % 2, 0:COLS], flat(mT_hi[:]).bitcast(F32),
                                    ALU.subtract).then_inc(mT_lo_done, 1)

                def unit(i, v, n, between=None):
                    lo_of(i, m_piece(v, 0) + AHEAD, n)
                    lo_of(i, m_piece(v, 1) + AHEAD, n)
                    gate_up(i, v, n)
                    lo_of(i, m_piece(v, 2) + AHEAD, n)
                    if between is not None:
                        between(i)
                    turned(i, v, n)

                def select(i):
                    for b in range(TB):
                        last = V.tensor_scalar(sel01[:, b, :], lane[:], POS[:, bass.ds(i, 1), b], None, ALU.is_equal)
                    last.then_inc(sel_built, 1)

                def gathered_lo(i):
                    dve.wait_ge(XT_hi_done, i + 1)
                    V.tensor_tensor(XT_lo, XT_psum, XT_hi.bitcast(F32), ALU.subtract).then_inc(XT_lo_done, 1)

                def add_x(i):
                    for b in range(TB):
                        dve.wait_ge(scattered, i * TB + (b + 1))
                        V.tensor_tensor(x[:, b, :], x[:, b, :], flat(ps[:, 4 + 2 * b:6 + 2 * b, :]),
                                        ALU.add).then_inc(x_added, 1)

                V.memset(Y_hi[:].bitcast(F32), 0.0)
                V.memset(selT[:].bitcast(F32), 0.0).then_inc(selT_done, 1)
                V.memset(gslot[:], 0.0).then_inc(gslot_done, 1)
                V.memset(Y_lo[:].bitcast(F32), 0.0).then_inc(Y_lo_done, 1)
                select(0)
                gathered_lo(0)
                with dve.Fori(0, T) as i:
                    dve.wait_ge(Y_lo_done, i + 1)
                    unit(i, 0, 0, add_x)
                    unit(i, 1, 0)
                    dve.wait_ge(sel_turned, i + 1)
                    V.tensor_copy(gslot[:], ps[:, 7, 0:1]).then_inc(gslot_done, 1)
                    with dve.Fori(0, M_UNIT_PAIRS) as n:
                        for v in (2, 3):
                            unit(i, v, n)
                    select(i + 1)
                    for v in (MOE_UNITS - 2, MOE_UNITS - 1):
                        unit(i, v, 0)
                    gathered_lo(i + 1)
                    dve.wait_ge(Y_hi_done, i + 1)
                    dve.wait_ge(gslot_done, i + 2)
                    V.scalar_tensor_tensor(Y_lo[:], flat(ps[:, 2:4, :]), gslot[:, 0:1], Y_hi[:].bitcast(F32),
                                           ALU.mult, ALU.subtract).then_inc(Y_lo_done, 1)
                add_x(T)

            constants()
            mixer(0)
            if stop_at != "mixer0":
                normalise(1)
                dense()
            if LAYERS == 2:
                mixer(1)
            if stop_at is None:
                evacuated(dve, DEPTH - 1, MIX - 1)
                dve.sem_inc(m_raw_free, M_RAW)
                normalise(3)
                moe()


NAMES = ["x", "attn_norm", "ffn_norm", "w_in", "q_norm", "k_norm", "conv_w", "hgrn_lower_bounds", "hgrn_out_norm",
         "w_proj_a", "w_proj_b", "w_proj_c", "w_out", "dense_w1", "dense_w3", "dense_w2", "router_w", "moe_w1",
         "moe_w3", "moe_w2"]


def kernel(**inputs):
    import numpy as np
    import concourse.bacc as bacc
    from concourse.bass_utils import run_bass_kernel_spmd

    nc = bacc.Bacc("TRN2", target_bir_lowering=False, num_devices=1)
    arrays, args = {}, []
    for name in NAMES:
        a = np.ascontiguousarray(inputs[name])
        arrays[f"in_{name}"] = a
        args.append(nc.dram_tensor(f"in_{name}", a.shape, mybir.dt.from_np(a.dtype), kind="ExternalInput").ap())
    out = nc.dram_tensor("out_x", inputs["x"].shape, F32, kind="ExternalOutput").ap()
    decoder(nc, *args, out)
    r = run_bass_kernel_spmd(nc, [arrays], core_ids=[0])
    return r.results[0]["out_x"]
```

```python
from contextlib import ExitStack
from functools import partial

import concourse.bass as bass
from concourse import mybir

F32 = mybir.dt.float32
F32R = mybir.dt.float32r
I32 = mybir.dt.int32
ALU = mybir.AluOpType
ACT = mybir.ActivationFunctionType
AX = mybir.AxisListType.X

P = 128
KB = 1024
EPS = 1e-6
NEG_BIG = -1e30
LB_FLOOR = 1e-30
GROUPS = ((128, 1), (512, 4), (2048, 16))
SLOTS_PER_GROUP = 4
HD = 64
COLS = 256
RAW, SPLIT = 4, 3
F_SLOTS = 6
AHEAD = 3
PIECE = 2048
LN_SHIFT = 40
LN2 = 0.6931471805599453

SEGMENTS = (("q", 0, 3), ("k", 768, 3), ("v", 1536, 3), ("i", 6144, 3),
            ("f", 5376, 3), ("qc", 4608, 3), ("g", 6912, 3), ("gate_a", 7680, 4), ("proj_a", None, 4),
            ("xb", 2304, 3), ("cb", 3840, 3), ("bb", 3072, 3), ("gate_b", 8704, 4), ("gate_c", 9728, 4),
            ("proj_b", None, 4), ("proj_c", None, 4), ("w_out", None, 4))
ORDER = [(name, c, None if col is None else col + c * COLS)
         for name, col, n in SEGMENTS for c in range(n)]
FIRST = {}
for _n, (_name, _c, _col) in enumerate(ORDER):
    FIRST.setdefault(_name, _n)
MIX = len(ORDER)
LEVELS = (None, 64, 32, 16, 8, 4, 2, 1)
NLEV = len(LEVELS) - 1

ATTN_AT = {9 + 3 * j + s: (j, s) for j in range(SLOTS_PER_GROUP) for s in range(3)}
ATTN_O_AT = {12 + 3 * j: j for j in range(SLOTS_PER_GROUP)}
LEVEL_AT = {22 + 2 * n: n for n in range(NLEV + 1)}
CROSS_AT, HGRN_O_AT, HGRN_SS_AT = 38, 39, 40


def decoder(nc, x_in, attn_norm, ffn_norm, w_in, q_norm, k_norm, conv_w, hgrn_lb, hgrn_gain,
            w_proj_a, w_proj_b, w_proj_c, w_out, dense_w1, dense_w3, dense_w2, router_w,
            moe_w1, moe_w3, moe_w2, out, stop_at=None):
    DEPTH, D, _ = w_in.shape
    TOK = x_in.shape[1]
    TB = TOK // P
    DC = D // P
    FF = dense_w1.shape[2]
    NE, FFE = router_w.shape[2], moe_w1.shape[3]
    CW = conv_w.shape[2]
    CC = CW // P
    DENSE_UNITS = FF // COLS
    MOE_UNITS = FFE // COLS
    assert TB == 2 and D == 1024 and CC == 6 and DENSE_UNITS == 11 and MOE_UNITS % 2 == 0
    DENSE = 3 * DENSE_UNITS
    UNIT_PIECES = 3
    PASS_PIECES = 3 * MOE_UNITS
    OVER = 2 * TOK // (P + 1)
    PASSES = NE + OVER
    BASE = (0, MIX)

    with ExitStack() as ctx:
        def sb(name, shape, dt=F32):
            return ctx.enter_context(nc.sbuf_tensor(name, shape, dt))

        def sem(name):
            return ctx.enter_context(nc.semaphore(name))

        x = sb("x", [P, TB, D])
        ident = sb("ident", [P, P])
        ones = sb("ones", [P, P])
        mean128 = sb("mean128", [P, P])
        before = sb("before", [P, P])
        lane = sb("lane", [P, P])
        part = sb("part", [P, 1])
        lane_i = sb("lane_i", [P, P], I32)
        part_i = sb("part_i", [P, 1], I32)
        eps = sb("eps", [P, 1])
        amask = sb("amask", [P, 3 * P + 3 * TOK])
        hmask = sb("hmask", [P, len(LEVELS), P])
        rows = sb("rows", [P, P])
        cols = sb("cols", [P, P])
        hrows = sb("hrows", [4, HD])
        hcols = sb("hcols", [HD, 4])
        router = sb("router", [P, DC, NE])
        router_hi = sb("router_hi", [P, DC, NE], F32R)
        router_lo = sb("router_lo", [P, DC, NE], F32R)
        lbm = sb("lbm", [P, DEPTH, CC])
        oml = sb("oml", [P, DEPTH, CC])
        kfix = sb("kfix", [P, DEPTH, CC])
        lbt = sb("lbt", [P, 4, CC])
        scol = sb("scol", [P, 4])
        ssq = sb("ssq", [P, TB])
        rstd = sb("rstd", [P, TB])
        qkss = sb("qkss", [P, 24])
        smax = sb("smax", [P, TB])
        den = sb("den", [P, TB])
        rden = sb("rden", [P, TB])
        hT_hi = sb("hT_hi", [P, DC, TOK], F32R)
        hT_lo = sb("hT_lo", [P, DC, TOK], F32R)

        base = nc.sbuf_base
        top = [base + (-base) % 64]

        def at(name, shape, dt=F32, offset=None):
            n = 4
            for s in shape[1:]:
                n *= s
            if offset is None:
                offset = top[0]
                top[0] += -(-n // 32) * 32
            return nc.alloc_sbuf_tensor_at(name, shape, dt, offset=offset), offset

        arena = top[0]
        raw, raw_at = at("raw", [P, RAW, PIECE])
        w_lo, _ = at("w_lo", [P, RAW, PIECE], F32R, offset=raw_at)
        w_hi, _ = at("w_hi", [P, SPLIT, PIECE], F32R)
        i_tm, i_at = at("i_tm", [P, TB, CW])
        q_tm, q_at = at("q_tm", [P, TB, CW])
        k_tm, _ = at("k_tm", [P, TB, CW])
        v_tm, _ = at("v_tm", [P, TB, CW])
        sig_c, _ = at("sig_c", [P, DC, TOK], offset=q_at)
        xb, xb_at = at("xb", [P, CC, TOK])
        cb, cb_at = at("cb", [P, CC, TOK])
        bb, bb_at = at("bb", [P, CC, TOK])
        yb_hi, _ = at("yb_hi", [P, CC, TOK], F32R, offset=cb_at)
        yb_lo, _ = at("yb_lo", [P, CC, TOK], F32R, offset=bb_at)
        W3 = 3 * TOK
        qT, _ = at("qT", [HD, W3], offset=xb_at)
        kT, _ = at("kT", [HD, W3], offset=xb_at + 4 * W3)
        NS = 3 * P + W3
        prob, _ = at("prob", [P, NS], offset=xb_at + 8 * W3)
        probT, _ = at("probT", [P, NS], offset=xb_at + 8 * W3 + 4 * NS)
        h_tm, _ = at("h_tm", [P, TB, D], offset=xb_at)
        qc, qc_at = at("qc", [P, CC, TOK])
        kc, kc_at = at("kc", [P, CC, TOK])
        yc_hi, _ = at("yc_hi", [P, CC, TOK], F32R, offset=qc_at)
        yc_lo, _ = at("yc_lo", [P, CC, TOK], F32R, offset=kc_at)
        bcum, _ = at("bcum", [P, CC, TOK])
        E = [at(f"E{n}", [P, CC, TOK])[0] for n in range(2)]
        sc, _ = at("sc", [P, CC * TB, P])
        scx, _ = at("scx", [P, CC, P])
        gc, _ = at("gc", [P, CC, TOK])
        o_hi, _ = at("o_hi", [HD, SLOTS_PER_GROUP, TOK], F32R)
        o_lo, _ = at("o_lo", [HD, SLOTS_PER_GROUP, TOK], F32R)
        merged, _ = at("merged", [P, DC, TOK])
        sig_ab, _ = at("sig_ab", [P, DC, TOK])
        term, _ = at("term", [P, 2, TOK])
        assert top[0] <= nc.sbuf_usable_end, (top[0], nc.sbuf_usable_end)

        h_end = xb_at + 4 * TB * D
        assert h_end <= qc_at and i_at + 12 * PIECE <= xb_at

        def slots(name, offsets, dt=F32):
            return [at(f"{name}{s}", [P, PIECE], dt, offset=o)[0] for s, o in enumerate(offsets)]

        low = [arena + 4 * PIECE * s for s in range((i_at - arena) // (4 * PIECE))]
        early = [i_at + 4 * PIECE * s for s in range(3)]
        high = [qc_at + 4 * PIECE * s for s in range(3 * F_SLOTS - len(low) - len(early))]
        f_raw = slots("f_raw", high[:F_SLOTS])
        f_hi = slots("f_hi", [early[0], early[2]] + low[:4], F32R)
        f_lo = slots("f_lo", [early[1]] + low[4:] + high[F_SLOTS:], F32R)
        top[0] = f_top = high[-1] + 4 * PIECE
        act_tm, _ = at("act_tm", [P, TB, COLS])
        actT_hi, _ = at("actT_hi", [P, TB, 2, P], F32R)
        actT_lo, _ = at("actT_lo", [P, TB, 2, P], F32R)
        assert top[0] <= nc.sbuf_usable_end, (top[0], nc.sbuf_usable_end)

        top[0] = f_top
        XT_hi, XT_lo = hT_hi[:, :, 0:P], hT_lo[:, :, 0:P]
        sel01, _ = at("sel01", [P, TB, P])
        selT, _ = at("selT", [P, TOK], F32R)
        gslot, _ = at("gslot", [P, 1])
        m_act, _ = at("m_act", [P, COLS])
        mT_hi, _ = at("mT_hi", [P, 2, P], F32R)
        mT_lo, _ = at("mT_lo", [P, 2, P], F32R)
        assert h_end + 8 * D <= qc_at
        Y_hi, _ = at("Y_hi", [P, D], F32R, offset=h_end)
        Y_lo, _ = at("Y_lo", [P, D], F32R, offset=h_end + 4 * D)
        gain_row, _ = at("gain_row", [P, D], offset=h_end)
        logit, _ = at("logit", [P, TB, NE])
        gt, _ = at("gt", [P, TB, NE, NE])
        eq, _ = at("eq", [P, TB, NE, NE])
        tri, _ = at("tri", [P, NE, NE])
        rank, _ = at("rank", [P, TB, NE])
        chosen, _ = at("chosen", [P, TB, NE])
        lmax, _ = at("lmax", [P, TB])
        ez, _ = at("ez", [P, TB, NE])
        esum, _ = at("esum", [P, TB])
        gate, _ = at("gate", [P, TB, NE])
        place, _ = at("place", [P, TB, NE])
        over, _ = at("over", [P, NE])
        over_n, _ = at("over_n", [P, NE])
        pick, _ = at("pick", [P, OVER, NE])
        tmp8, _ = at("tmp8", [P, TB, OVER, NE])
        iota8, _ = at("iota8", [P, NE])
        POS, _ = at("POS", [P, PASSES + 1, TB])
        GATE, _ = at("GATE", [P, PASSES, TB])
        tabf, _ = at("tabf", [P, PASSES + 1])
        tab, _ = at("tab", [P, PASSES + 1], I32)
        assert top[0] <= nc.sbuf_usable_end, (top[0], nc.sbuf_usable_end)

        ps = ctx.enter_context(nc.psum_tensor("ps", [P, 8, 512], F32))
        G = [ps[:, n, :] for n in range(2)]
        SA = ps[:, 2:5, :].rearrange("p a n -> p (a n)")
        TA = ps[:, 5:8, :].rearrange("p a n -> p (a n)")

        XT_psum = ps[:, 4:6, :].rearrange("p a (c t) -> p (a c) t", t=P)

        x_in_sem, vec_in, router_in, gain_in = sem("x_loaded"), sem("vectors_loaded"), sem("router_loaded"), sem("gain_loaded")
        landed = [sem(f"raw_landed{r}") for r in range(RAW)]
        hi_done, lo_done, used = sem("hi_done"), sem("lo_done"), sem("piece_used")
        g_free = [sem(f"g_free{n}") for n in range(2)]
        masks = sem("masks_built")
        pool_step, dve_step = sem("pool_step"), sem("dve_step")
        vec_T = sem("vectors_turned")
        lb_diff, lb_exp = sem("lb_diff"), sem("lb_exp")
        squared = sem("x_squared")
        h_ready = sem("h_ready")
        hT_psum = sem("hT_in_psum")
        hT_hi_done = sem("hT_hi_done")
        hT_ready = sem("hT_ready")
        f_sig, f_arg, f_ln, cum = sem("forget_sigmoid"), sem("ln_argument"), sem("ln_done"), sem("cumsum_done")
        qk_normed = sem("qk_normed")
        conv_y, conv_hi, conv_lo = sem("conv_y"), sem("conv_hi"), sem("conv_lo")
        diff, decay, qk_level, level_mm, level_ev, level_add = (sem("level_diff"), sem("level_decay"), sem("level_qk"),
                                                                sem("level_mm"), sem("level_evacuated"), sem("level_added"))
        x_decay, x_qk, x_mm, x_ev = sem("cross_decay"), sem("cross_qk"), sem("cross_mm"), sem("cross_evacuated")
        o_mm, o_sq, o_ss, o_gated, yc_hi_done, yc_done = (sem("hgrn_o"), sem("hgrn_squared"), sem("hgrn_ss"), sem("hgrn_gated"),
                                                         sem("yc_hi_done"), sem("yc_done"))
        o_read = sem("hgrn_o_read")
        a_turn, a_qk, a_score, a_masked, a_max, a_exp, a_prob, a_pturn, a_pT, a_o, a_ohi, a_olo = (
            sem("attn_turned"), sem("attn_qkT"), sem("attn_scores"), sem("attn_masked"), sem("attn_max"), sem("attn_exp"),
            sem("attn_prob"), sem("attn_prob_turned"), sem("attn_probT"), sem("attn_o"), sem("attn_o_hi"), sem("attn_o_lo"))
        kc_done = sem("kc_done")
        x_root, qk_ss, qk_root, o_root = sem("x_root"), sem("qk_ss"), sem("qk_root"), sem("hgrn_root")
        merge = sem("merged_done")
        merged_hi, merged_lo = sem("merged_hi"), sem("merged_lo")
        silu, act_done, aT_psum, aT_hi, aT_lo = sem("dense_silu"), sem("dense_act"), sem("dense_actT_psum"), sem("dense_actT_hi"), sem("dense_actT_lo")
        x_done = sem("dense_x")
        hg = sem("h_gained")
        r_hi, r_lo, logits, z_ready, z_exp = sem("router_hi_done"), sem("router_lo_done"), sem("logits"), sem("z_ready"), sem("z_exp")
        chosen_ready, counted, table = sem("chosen_ready"), sem("tokens_counted"), sem("pass_table_ready")
        d_landed = [sem(f"dense_raw_landed{r}") for r in range(F_SLOTS)]
        m_landed = [sem(f"moe_raw_landed{r}") for r in range(F_SLOTS)]
        d_raw_free, m_raw_free = sem("dense_raw_free"), sem("moe_raw_free")
        d_hi_done, m_hi_done = sem("dense_hi_done"), sem("moe_hi_done")
        d_split_free, m_split_free = sem("dense_split_free"), sem("moe_split_free")
        sel_built, gathered, XT_hi_done, XT_lo_done = sem("sel_built"), sem("gathered"), sem("XT_hi_done"), sem("XT_lo_done")
        sel_turned, selT_done, gslot_done = sem("sel_turned"), sem("selT_done"), sem("gslot_done")
        m_silu, m_act_done, mT_psum, mT_hi_done, mT_lo_done = (sem("moe_silu"), sem("moe_act"), sem("moe_actT_psum"),
                                                               sem("moe_actT_hi"), sem("moe_actT_lo"))
        Y_hi_done, Y_lo_done, scattered = sem("Y_hi_done"), sem("Y_lo_done"), sem("scattered")
        x_added = sem("x_added")
        stored = sem("stored")

        R_AN, R_FN = 0, DEPTH * DC
        R_CV = 2 * DEPTH * DC
        R_LB = R_CV + DEPTH * 3 * CC
        R_HG = R_LB + DEPTH * CC
        NROWS = R_HG + DEPTH
        N_VEC, N_MASKS = 7, 9

        def col(r):
            return cols[:, r:r + 1]

        def conv_col(L, j, c):
            return col(R_CV + (L * 3 + j) * CC + c)

        def piece_view(t, s, parts, k):
            return t[0:parts, s, 0:k * COLS].rearrange("p (k n) -> p k n", k=k)

        SHAPE = {"proj_a": (HD, 4), "proj_b": (P, CC), "proj_c": (P, CC)}

        def source(L, m):
            name, c, c0 = ORDER[m]
            if c0 is not None:
                return w_in[L].rearrange("(k p) n -> p k n", p=P)[:, :, c0:c0 + COLS]
            w, p = {"proj_a": (w_proj_a, HD), "proj_b": (w_proj_b, P), "proj_c": (w_proj_c, P), "w_out": (w_out, P)}[name]
            return w[L].rearrange("(k p) n -> p k n", p=p)[:, :, c * COLS:(c + 1) * COLS]

        TOKEN_MAJOR = ("i", "q", "k", "v", "w_out")
        DEST = {"i": i_tm, "q": q_tm, "k": k_tm, "v": v_tm, "xb": xb, "cb": cb, "bb": bb}
        LAYERS = DEPTH if stop_at in (None, "mixer1") else 1

        FEEDS = (stop_at != "mixer0", stop_at is None)

        def evacuated(eng, L, m):
            for q in (m - 1, m):
                eng.wait_ge(g_free[q % 2], L * (MIX // 2) + q // 2 + 1)

        def halves(t, h):
            v = t[:].rearrange("p c t -> p (c t)").rearrange("p (g w) -> p g w", w=2 * h)
            return v[:, :, 0:h], v[:, :, h:2 * h]

        def flat(t):
            return t.rearrange("p a b -> p (a b)")

        def h_bank(v, b):
            return ps[:, 2 * (v % 2) + b, :]

        def n_passes(eng):
            return eng.value_load(tab[0:1, PASSES:PASSES + 1], min_val=NE, max_val=PASSES)

        def m_piece(v, c):
            return 3 * v + c

        M_UNIT_PAIRS = (MOE_UNITS - 4) // 2
        assert PASS_PIECES % F_SLOTS == 0 and F_SLOTS == 2 * 3 and AHEAD == 3

        block = ctx.enter_context(nc.Block())

        @block.sync
        def _(sp):
            sp.dma_start(x[:], x_in[0].rearrange("(b p) d -> p b d", p=P)).then_inc(x_in_sem, 16)

            def load_mixer(L):
                for m in range(MIX):
                    p = BASE[L] + m
                    parts, k = SHAPE.get(ORDER[m][0], (P, DC))
                    if p >= RAW:
                        sp.wait_ge(used, p - RAW + 1)
                    if L and m == 0:
                        sp.wait_ge(d_split_free, F_SLOTS + DENSE)
                    sp.dma_start(piece_view(raw, p % RAW, parts, k), source(L, m)).then_inc(landed[p % RAW], 16)

            w1 = dense_w1[0].rearrange("(k p) n -> p k n", p=P)
            w3 = dense_w3[0].rearrange("(k p) n -> p k n", p=P)
            w2 = dense_w2[0].rearrange("(u c p) n -> u p c n", p=P, c=2)

            def work_left(L):
                sp.wait_ge(used, BASE[L] + FIRST["w_out"])
                sp.sem_inc((d_raw_free, m_raw_free)[L], F_SLOTS)

            def load_up(q, n, half, c0):
                sp.wait_ge(d_raw_free, n * 6 + (q + 1))
                dst = f_raw[q % F_SLOTS][:].rearrange("p (k w n) -> p k w n", k=4, w=2)
                for w, src in enumerate((w1, w3)):
                    sp.dma_start(dst[:, :, w, :], src[:, 4 * half:4 * half + 4, c0]).then_inc(d_landed[q % F_SLOTS], 16)

            def load_down(q, n, src):
                sp.wait_ge(d_raw_free, n * 6 + (q + 1))
                dst = f_raw[q % F_SLOTS][:].rearrange("p (c n) -> p c n", c=2)
                for c in range(2):
                    sp.dma_start(dst[:, c, :], src[:, c, :]).then_inc(d_landed[q % F_SLOTS], 16)

            def load_dense():
                for half in range(2):
                    load_up(half, 0, half, slice(0, COLS))
                with sp.Fori(0, (DENSE_UNITS - 1) // 2) as n:
                    for v in (1, 2):
                        for half in range(2):
                            load_up(3 * v - 1 + half, n, half, bass.ds((n * 2 + v) * COLS, COLS))
                        load_down(3 * v + 1, n, w2[n * 2 + (v - 1)])
                load_down(DENSE - 1, 0, w2[DENSE_UNITS - 1])

            e1 = moe_w1[0].rearrange("e (k p) n -> e p k n", p=P)
            e3 = moe_w3[0].rearrange("e (k p) n -> e p k n", p=P)
            e2 = moe_w2[0].rearrange("e (u c p) n -> (e u) p c n", p=P, c=2)

            def moe_up(i, e, q, n, half, u):
                sp.wait_ge(m_raw_free, i * PASS_PIECES + n * 6 + (q + 1))
                dst = f_raw[q % F_SLOTS][:].rearrange("p (k w n) -> p k w n", k=4, w=2)
                for w, src in enumerate((e1, e3)):
                    sp.dma_start(dst[:, :, w, :], src[e, :, 4 * half:4 * half + 4, bass.ds(u * COLS, COLS)])\
                      .then_inc(m_landed[q % F_SLOTS], 16)

            def moe_down(i, e, q, n, u):
                sp.wait_ge(m_raw_free, i * PASS_PIECES + n * 6 + (q + 1))
                dst = f_raw[q % F_SLOTS][:].rearrange("p (c n) -> p c n", c=2)
                for c in range(2):
                    sp.dma_start(dst[:, c, :], e2[e * MOE_UNITS + u, :, c, :]).then_inc(m_landed[q % F_SLOTS], 16)

            def load_pass(i, e):
                for half in range(2):
                    moe_up(i, e, half, 0, half, 0)
                with sp.Fori(0, (MOE_UNITS - 2) // 2) as n:
                    for v in (1, 2):
                        for half in range(2):
                            moe_up(i, e, m_piece(v, half - 1), n, half, n * 2 + v)
                        moe_down(i, e, m_piece(v, 1), n, n * 2 + (v - 1))
                last = MOE_UNITS - 1
                for half in range(2):
                    moe_up(i, e, m_piece(last, half - 1), 0, half, last)
                moe_down(i, e, m_piece(last, 1), 0, last - 1)
                moe_down(i, e, m_piece(last, 2), 0, last)

            def load_moe():
                load_pass(0, 0)
                sp.wait_ge(table, 1)
                T = n_passes(sp)
                with sp.Fori(1, T) as i:
                    load_pass(i, sp.value_load(tab[0:1, bass.ds(i, 1)], min_val=0, max_val=NE - 1))
                for q in range(AHEAD):
                    sp.wait_ge(m_raw_free, T * PASS_PIECES + (q + 1))
                    for w, src in enumerate((e1, e3)):
                        sp.dma_start(f_raw[q][:, w * 16:(w + 1) * 16], src[0, :, 0, 0:16]).then_inc(m_landed[q], 16)
                sp.wait_ge(x_added, T * TB + TB)

            load_mixer(0)
            if stop_at != "mixer0":
                work_left(0)
                load_dense()
            if LAYERS == 2:
                load_mixer(1)
            if stop_at is None:
                work_left(1)
                load_moe()
            elif stop_at == "dense":
                sp.wait_ge(x_done, 2)
            else:
                evacuated(sp, LAYERS - 1, MIX - 1)
            sp.dma_start(out[0].rearrange("(b p) d -> p b d", p=P), x[:]).then_inc(stored, 16)
            sp.wait_ge(stored, 16)

        @block.gpsimd
        def _(pool):
            pool.dma_start(rows[R_AN:R_FN, :], attn_norm.rearrange("l (c p) -> (l c) p", p=P)).then_inc(vec_in, 16)
            pool.dma_start(rows[R_FN:R_CV, :], ffn_norm.rearrange("l (c p) -> (l c) p", p=P)).then_inc(vec_in, 16)
            pool.dma_start(rows[R_CV:R_LB, :], conv_w.rearrange("l j (c p) -> (l j c) p", p=P)).then_inc(vec_in, 16)
            pool.dma_start(rows[R_LB:R_HG, :], hgrn_lb.rearrange("l (c p) -> (l c) p", p=P)).then_inc(vec_in, 16)
            pool.dma_start(rows[R_HG:NROWS, :], hgrn_gain).then_inc(vec_in, 16)
            pool.dma_start(hrows[0:2, :], q_norm).then_inc(vec_in, 16)
            pool.dma_start(hrows[2:4, :], k_norm).then_inc(vec_in, 16)
            pool.dma_start(router[:], router_w[0].rearrange("(k p) e -> p k e", p=P)).then_inc(router_in, 16)
            pool.memset(ident[:], 0.0).then_inc(pool_step, 1)
            pool.memset(before[:], 1.0).then_inc(pool_step, 1)
            pool.memset(eps[:], EPS).then_inc(masks, 1)
            pool.iota(lane[:], pattern=[[1, P]], base=0, channel_multiplier=0,
                      allow_small_or_imprecise_dtypes=True).then_inc(masks, 1)
            pool.iota(part[:], pattern=[[0, 1]], base=0, channel_multiplier=1,
                      allow_small_or_imprecise_dtypes=True).then_inc(masks, 1)
            pool.iota(lane_i[:], pattern=[[1, P]], base=0, channel_multiplier=0).then_inc(masks, 1)
            pool.iota(part_i[:], pattern=[[0, 1]], base=0, channel_multiplier=1).then_inc(masks, 1)
            pool.iota(amask[:, 0:3 * P].bitcast(I32).rearrange("p (g j) -> p g j", g=3), pattern=[[0, 3], [-1, P]],
                      base=TOK, channel_multiplier=1).then_inc(masks, 1)
            pool.iota(amask[:, 3 * P:].bitcast(I32).rearrange("p (g j) -> p g j", g=3), pattern=[[0, 3], [-1, TOK]],
                      base=TOK + P, channel_multiplier=1).then_inc(masks, 1)
            pool.wait_ge(pool_step, 2)
            pool.affine_select(out=ident[:], in_=ident[:], compare_op=ALU.not_equal, fill=1.0, base=0,
                               pattern=[[-1, P]], channel_multiplier=1).then_inc(masks, 1)
            pool.affine_select(out=before[:], in_=before[:], compare_op=ALU.is_gt, fill=0.0, base=0,
                               pattern=[[1, P]], channel_multiplier=-1).then_inc(masks, 1)

            def level_diff(L, n):
                h = LEVELS[n]
                if n == 1:
                    pool.wait_ge(cum, L + 1)
                if n > 2:
                    pool.wait_ge(level_add, L * NLEV + n - 2)
                e1, e2 = halves(E[n % 2], h)
                b1, b2 = halves(bcum, h)
                mid = b1[:, :, h - 1:h].broadcast_to(b1.shape)
                pool.tensor_tensor(e1, mid, b1, ALU.subtract).then_inc(diff, 1)
                pool.tensor_tensor(e2, b2, mid, ALU.subtract).then_inc(diff, 1)

            def level_sum(L, n):
                pool.wait_ge(level_ev, L * (NLEV + 1) + n + 1)
                if n > 1:
                    pool.wait_ge(level_add, L * NLEV + n - 1)
                pool.tensor_tensor(flat(sc[:]), flat(sc[:]), flat(E[n % 2][:]), ALU.add).then_inc(level_add, 1)

            for L in range(LAYERS):
                level_diff(L, 1)
                level_diff(L, 2)
                for n in range(1, NLEV + 1):
                    level_sum(L, n)
                    if n + 2 <= NLEV:
                        level_diff(L, n + 2)
            if stop_at is None:
                evacuated(pool, DEPTH - 1, MIX - 1)
                pool.dma_start(gain_row[:], ffn_norm[DEPTH - 1:DEPTH, :].broadcast_to([P, D])).then_inc(gain_in, 16)
                pool.iota(iota8[:], pattern=[[1, NE]], base=0, channel_multiplier=0,
                          allow_small_or_imprecise_dtypes=True).then_inc(masks, 1)
                pool.memset(tri[:], 1.0).then_inc(pool_step, 1)
                pool.wait_ge(pool_step, 3)
                pool.affine_select(out=tri[:], in_=tri[:], compare_op=ALU.is_gt, fill=0.0, base=0,
                                   pattern=[[1, NE], [-1, NE]], channel_multiplier=0).then_inc(masks, 1)

        @block.scalar
        def _(act):
            A = nc.scalar.activation

            def hi(p, parts=P, n=PIECE):
                act.wait_ge(landed[p % RAW], 16 * (p // RAW + 1))
                if p >= SPLIT:
                    act.wait_ge(used, p - SPLIT + 1)
                A(w_hi[0:parts, p % SPLIT, 0:n], raw[0:parts, p % RAW, 0:n], ACT.Copy).then_inc(hi_done, 1)

            def normalise(n):
                if n == 0:
                    act.wait_ge(x_in_sem, 16)
                elif n % 2:
                    evacuated(act, n // 2, MIX - 1)
                else:
                    act.wait_ge(x_done, TB)
                for b in range(TB):
                    A(h_tm[:, b, :], x[:, b, :], ACT.Square, scale=float(D) ** -0.5,
                      accum_out=ssq[:, b:b + 1]).then_inc(squared, 1)
                act.wait_ge(squared, TB * (n + 1))
                A(rstd[:], ssq[:], ACT.Sqrt, bias=eps[:, 0:1]).then_inc(x_root, 1)
                first = R_AN if n % 2 == 0 else R_FN
                for j in range(DC // 2):
                    act.wait_ge(hT_psum, (DC // 2) * n + j + 1)
                    for c in range(2):
                        A(hT_hi[:, 2 * j + c, :], ps[:, 2 + j, c * TOK:(c + 1) * TOK], ACT.Copy,
                          scale=col(first + (n // 2) * DC + 2 * j + c)).then_inc(hT_hi_done, 1)

            def evacuate(L, m):
                name, c, _ = ORDER[m]
                if name in ("proj_a", "proj_b", "proj_c", "w_out"):
                    return
                act.wait_ge(used, BASE[L] + m + 1)
                g, free = G[m % 2], g_free[m % 2]
                if name in ("i", "q", "k", "v"):
                    A(DEST[name][:, :, c * COLS:(c + 1) * COLS], g.rearrange("p (b n) -> p b n", b=TB),
                      ACT.Copy).then_inc(free, 1)
                    return
                g = g.rearrange("p (c t) -> p c t", c=2)
                two = slice(2 * c, 2 * c + 2)
                if name in ("xb", "cb", "bb"):
                    if name == "xb" and c == 0:
                        act.wait_ge(a_o, (L + 1) * SLOTS_PER_GROUP)
                    A(DEST[name][:, two, :], g, ACT.Copy).then_inc(free, 1)
                elif name == "f":
                    A(bcum[:, two, :], g, ACT.Sigmoid).then_inc(f_sig, 1)
                    A(kc[:, two, :], g, ACT.Sigmoid, scale=-1.0).then_inc(free, 1)
                elif name in ("qc", "g"):
                    A((qc if name == "qc" else gc)[:, two, :], g, ACT.Silu).then_inc(free, 1)
                elif name == "gate_c":
                    act.wait_ge(a_turn, (L + 1) * SLOTS_PER_GROUP)
                    A(sig_c[:, two, :], g, ACT.Sigmoid).then_inc(free, 1)
                else:
                    if name == "gate_b":
                        evacuated(act, L, FIRST["proj_a"] + c)
                    A(sig_ab[:, two, :], g, ACT.Sigmoid).then_inc(free, 1)

            def cross_exp(L):
                act.wait_ge(level_add, L * NLEV + NLEV - 1)
                A(E[0][:, :, P:TOK], bcum[:, :, P:TOK], ACT.Exp).then_inc(x_decay, 1)
                for c in range(CC):
                    A(E[0][:, c, 0:P], bcum[:, c, 0:P], ACT.Exp, scale=-1.0,
                      bias=bcum[:, c, P - 1:P]).then_inc(x_decay, 1)

            def attention(L, j, stage):
                n = L * SLOTS_PER_GROUP + j
                if stage == 0:
                    act.wait_ge(a_turn, n + 1)
                    A(qT[:], TA[0:HD, 0:W3], ACT.Copy, scale=hcols[:, L:L + 1]).then_inc(a_qk, 1)
                    A(kT[:], TA[0:HD, W3:2 * W3], ACT.Copy, scale=hcols[:, 2 + L:3 + L]).then_inc(a_qk, 1)
                elif stage == 1:
                    act.wait_ge(a_max, n + 1)
                    A(prob[:, 0:3 * P], prob[:, 0:3 * P], ACT.Exp, bias=smax[:, 0:1],
                      accum_out=den[:, 0:1]).then_inc(a_exp, 1)
                    A(prob[:, 3 * P:], prob[:, 3 * P:], ACT.Exp, bias=smax[:, 1:2],
                      accum_out=den[:, 1:2]).then_inc(a_exp, 1)
                elif stage == 2:
                    act.wait_ge(a_pturn, n + 1)
                    A(probT[:], TA[:, 0:NS], ACT.Copy).then_inc(a_pT, 1)

            def mixer(L):
                normalise(2 * L)
                for m in range(MIX + 2):
                    if m < MIX:
                        parts, k = SHAPE.get(ORDER[m][0], (P, DC))
                        hi(BASE[L] + m, parts, k * COLS)
                    if m >= 2:
                        evacuate(L, m - 2)
                    if m - 2 in ATTN_O_AT:
                        j = ATTN_O_AT[m - 2]
                        act.wait_ge(a_o, L * SLOTS_PER_GROUP + j + 1)
                        A(o_hi[:, j, :], SA[0:HD, 0:TOK], ACT.Copy).then_inc(a_ohi, 1)
                    if m - 2 in ATTN_AT:
                        attention(L, *ATTN_AT[m - 2])
                    if m in (FIRST["q"] + 5, FIRST["k"] + 5):
                        n = 2 * L + (1 if m == FIRST["q"] + 5 else 2)
                        act.wait_ge(qk_ss, n)
                        A(qkss[:], qkss[:], ACT.Sqrt, scale=1.0 / HD, bias=eps[:, 0:1]).then_inc(qk_root, 1)
                    if m == 18:
                        act.wait_ge(f_arg, L + 1)
                        A(bcum[:], bcum[:], ACT.Ln).then_inc(f_ln, 1)
                    if m + 1 in LEVEL_AT and LEVEL_AT[m + 1]:
                        n = LEVEL_AT[m + 1]
                        act.wait_ge(diff, 2 * (L * NLEV + n))
                        A(E[n % 2][:], E[n % 2][:], ACT.Exp).then_inc(decay, 1)
                    if m == CROSS_AT:
                        cross_exp(L)
                    if m == CROSS_AT + 2:
                        act.wait_ge(x_mm, L + 1)
                        A(scx[:], SA[:, 0:CC * P].rearrange("p (c t) -> p c t", c=CC), ACT.Copy).then_inc(x_ev, 1)
                    if m == HGRN_O_AT + 2:
                        act.wait_ge(o_mm, L + 1)
                        A(flat(E[1][:]), TA, ACT.Square).then_inc(o_sq, 1)
                    if m == HGRN_SS_AT + 2:
                        act.wait_ge(o_ss, L + 1)
                        A(flat(E[0][:]), SA, ACT.Sqrt, bias=eps[:, 0:1]).then_inc(o_root, 1)
                        act.wait_ge(o_gated, L + 1)
                        A(yc_hi[:], E[1][:], ACT.Copy).then_inc(yc_hi_done, 1)
                    if m == FIRST["bb"] + 5:
                        act.wait_ge(conv_y, L + 1)
                        A(yb_hi[:], xb[:], ACT.Copy).then_inc(conv_hi, 1)
                    if m >= 2 and ORDER[m - 2][0] == "proj_c":
                        c = ORDER[m - 2][1]
                        act.wait_ge(merge, 4 * L + c + 1)
                        A(hT_hi[:, 2 * c:2 * c + 2, :], merged[:, 2 * c:2 * c + 2, :], ACT.Copy).then_inc(merged_hi, 1)
                    if m >= MIX and FEEDS[L]:
                        (dense_hi if L == 0 else partial(moe_hi, 0))(m - MIX, 0)

            def dense_hi(q, n):
                act.wait_ge(d_landed[q % F_SLOTS], n * 32 + 32 * (q // F_SLOTS + 1))
                act.wait_ge(d_split_free, n * 6 + (q + 1))
                A(f_hi[q % F_SLOTS][:], f_raw[q % F_SLOTS][:], ACT.Copy).then_inc(d_hi_done, 1)

            def dense():
                def silu_of(v, n):
                    act.wait_ge(d_split_free, n * 6 + (F_SLOTS + max(3 * v, 1) + 1))
                    for b in range(TB):
                        A(act_tm[:, b, :], h_bank(v, b)[:, 0:COLS], ACT.Silu).then_inc(silu, 1)

                def turned(v, n):
                    for b in range(TB):
                        act.wait_ge(aT_psum, n * 4 + (TB * v + b + 1))
                        A(flat(actT_hi[:, b]), h_bank(v, b)[:, 0:COLS], ACT.Copy).then_inc(aT_hi, 1)

                def unit(v, n, split=True):
                    if split:
                        dense_hi(3 * v + AHEAD, n)
                        dense_hi(3 * v + 1 + AHEAD, n)
                    silu_of(v, n)
                    if split:
                        dense_hi(3 * v + 2 + AHEAD, n)
                    turned(v, n)

                dense_hi(2, 0)
                unit(0, 0)
                with act.Fori(0, (DENSE_UNITS - 3) // 2) as n:
                    for v in (1, 2):
                        unit(v, n)
                unit(DENSE_UNITS - 2, 0)
                unit(DENSE_UNITS - 1, 0, split=False)

            def moe_hi(i, q, n):
                act.wait_ge(m_landed[q % F_SLOTS], i * (32 * PASS_PIECES // F_SLOTS) + n * 32 + 32 * (q // F_SLOTS + 1))
                act.wait_ge(m_split_free, i * PASS_PIECES + n * 6 + (q + 1))
                A(f_hi[q % F_SLOTS][:], f_raw[q % F_SLOTS][:], ACT.Copy).then_inc(m_hi_done, 1)

            def moe():
                def silu_of(i, v, n):
                    act.wait_ge(m_split_free, i * PASS_PIECES + n * 6 + (F_SLOTS + max(m_piece(v, 0), 1) + 1))
                    A(m_act[:], ps[:, v % 2, 0:COLS], ACT.Silu).then_inc(m_silu, 1)

                def turned(i, v, n):
                    act.wait_ge(mT_psum, i * MOE_UNITS + n * 2 + (v + 1))
                    A(flat(mT_hi[:]), ps[:, v % 2, 0:COLS], ACT.Copy).then_inc(mT_hi_done, 1)

                def unit(i, v, n):
                    moe_hi(i, m_piece(v, 0) + AHEAD, n)
                    moe_hi(i, m_piece(v, 1) + AHEAD, n)
                    silu_of(i, v, n)
                    moe_hi(i, m_piece(v, 2) + AHEAD, n)
                    turned(i, v, n)

                def gathered_hi(i):
                    act.wait_ge(gathered, i + 1)
                    A(XT_hi, XT_psum, ACT.Copy).then_inc(XT_hi_done, 1)

                act.wait_ge(router_in, 16)
                A(router_hi[:], router[:], ACT.Copy).then_inc(r_hi, 1)
                moe_hi(0, 2, 0)
                act.wait_ge(z_ready, 1)
                A(ez[:], ez[:], ACT.Exp).then_inc(z_exp, 1)
                act.wait_ge(table, 1)
                T = n_passes(act)
                gathered_hi(0)
                with act.Fori(0, T) as i:
                    unit(i, 0, 0)
                    unit(i, 1, 0)
                    act.wait_ge(sel_turned, i + 1)
                    A(selT[:], ps[:, 6, 0:TOK], ACT.Copy).then_inc(selT_done, 1)
                    with act.Fori(0, M_UNIT_PAIRS) as n:
                        for v in (2, 3):
                            unit(i, v, n)
                    for v in (MOE_UNITS - 2, MOE_UNITS - 1):
                        unit(i, v, 0)
                    gathered_hi(i + 1)
                    act.wait_ge(m_split_free, (i + 1) * PASS_PIECES + F_SLOTS)
                    act.wait_ge(gslot_done, i + 2)
                    A(Y_hi[:], flat(ps[:, 2:4, :]), ACT.Copy, scale=gslot[:, 0:1]).then_inc(Y_hi_done, 1)

            act.wait_ge(masks, N_MASKS)
            act.wait_ge(lb_diff, 1)
            A(lbt[:, 2:4, :], lbt[:, 0:2, :], ACT.Exp).then_inc(lb_exp, 1)
            mixer(0)
            if stop_at != "mixer0":
                normalise(1)
                dense()
            if LAYERS == 2:
                mixer(1)
            if stop_at is None:
                normalise(3)
                moe()

        @block.tensor
        def _(pe):
            mm = nc.tensor.matmul

            def turn(dst, src, n=P):
                return nc.tensor.transpose(dst, src, ident[0:n, 0:n])

            def split_mm(dst, a_hi, a_lo, b_hi, b_lo, first, last):
                mm(dst, a_hi, b_hi, start=first, stop=False)
                mm(dst, a_lo, b_hi, start=False, stop=False)
                return mm(dst, a_hi, b_lo, start=False, stop=last)

            def normalise(n):
                pe.wait_ge(h_ready, n + 1)
                for j in range(DC // 2):
                    for c in range(2):
                        for b in range(TB):
                            last = turn(ps[:, 2 + j, c * TOK + b * P:c * TOK + (b + 1) * P],
                                        h_tm[:, b, (2 * j + c) * P:(2 * j + c + 1) * P])
                    last.then_inc(hT_psum, 1)

            ACTS = {"proj_a": (o_hi, o_lo), "proj_b": (yb_hi, yb_lo), "proj_c": (yc_hi, yc_lo)}

            def piece(L, m):
                name, _, _ = ORDER[m]
                p = BASE[L] + m
                parts, k = SHAPE.get(name, (P, DC))
                if m == 0:
                    pe.wait_ge(hT_ready, 2 * L + 1)
                ready = {"proj_a": (a_olo, SLOTS_PER_GROUP * (L + 1)), "proj_b": (conv_lo, L + 1),
                         "proj_c": (yc_done, L + 1), "w_out": (merged_lo, 4 * (L + 1))}
                if name in ready and m == FIRST[name]:
                    pe.wait_ge(*ready[name])
                a_hi, a_lo = ACTS.get(name, (hT_hi, hT_lo))
                pe.wait_ge(lo_done, p + 1)
                pe.wait_ge(g_free[m % 2], L * (MIX // 2) + m // 2)
                wh, wl = piece_view(w_hi, p % SPLIT, parts, k), piece_view(w_lo, p % RAW, parts, k)
                g = G[m % 2]
                for half in range(2):
                    dst = g[:, half * COLS:(half + 1) * COLS]
                    for c in range(k):
                        if name in TOKEN_MAJOR:
                            tok = slice(half * P, (half + 1) * P)
                            last = split_mm(dst, a_hi[:, c, tok], a_lo[:, c, tok], wh[:, c, :], wl[:, c, :],
                                            c == 0, c == k - 1)
                        else:
                            out_c = slice(half * P, (half + 1) * P)
                            last = split_mm(dst, wh[:, c, out_c], wl[:, c, out_c], a_hi[:, c, :], a_lo[:, c, :],
                                            c == 0, c == k - 1)
                last.then_inc(used, 1)

            def attention(L, j, stage):
                n = L * SLOTS_PER_GROUP + j
                heads = [g * SLOTS_PER_GROUP + j for g in range(len(GROUPS))]
                if stage == 0:
                    if j == 0:
                        pe.wait_ge(qk_normed, 2 * (L + 1))
                    pe.wait_ge(a_pT, n)
                    if L and j == 0:
                        pe.wait_ge(o_read, L)
                    for w, t in enumerate((q_tm, k_tm)):
                        for g, hd in enumerate(heads):
                            for b in range(TB):
                                o = w * W3 + g * TOK + b * P
                                last = turn(TA[0:HD, o:o + P], t[:, b, hd * HD:(hd + 1) * HD])
                    last.then_inc(a_turn, 1)
                elif stage == 1:
                    pe.wait_ge(a_qk, 2 * (n + 1))
                    pe.wait_ge(a_olo, n)
                    for g in range(3):
                        mm(SA[:, g * P:(g + 1) * P], qT[:, g * TOK:g * TOK + P], kT[:, g * TOK:g * TOK + P],
                           start=True, stop=True)
                    for g in range(3):
                        last = mm(SA[:, 512 + g * TOK:512 + (g + 1) * TOK], qT[:, g * TOK + P:(g + 1) * TOK],
                                  kT[:, g * TOK:(g + 1) * TOK], start=True, stop=True)
                    last.then_inc(a_score, 1)
                elif stage == 2:
                    pe.wait_ge(a_prob, n + 1)
                    for q in range(NS // P):
                        last = turn(TA[:, q * P:(q + 1) * P], prob[:, q * P:(q + 1) * P])
                    last.then_inc(a_pturn, 1)
                else:
                    if j == 0:
                        evacuated(pe, L, FIRST["v"] + 2)
                    pe.wait_ge(a_pT, n + 1)
                    for g, hd in enumerate(heads):
                        mm(SA[0:HD, 0:P], v_tm[:, 0, hd * HD:(hd + 1) * HD], probT[:, g * P:(g + 1) * P],
                           start=g == 0, stop=g == 2)
                    for g, hd in enumerate(heads):
                        for b in range(TB):
                            o = 3 * P + g * TOK + b * P
                            last = mm(SA[0:HD, P:TOK], v_tm[:, b, hd * HD:(hd + 1) * HD], probT[:, o:o + P],
                                      start=g == b == 0, stop=g == 2 and b == 1)
                    last.then_inc(a_o, 1)

            def level(L, n):
                if n == 0:
                    pe.wait_ge(kc_done, L + 1)
                    evacuated(pe, L, FIRST["qc"] + 2)
                    pe.wait_ge(a_olo, SLOTS_PER_GROUP * (L + 1))
                    left, right = kc, qc
                else:
                    pe.wait_ge(qk_level, 2 * (L * NLEV + n))
                    pe.wait_ge(level_ev, L * (NLEV + 1) + n)
                    left = right = E[n % 2]
                for c in range(CC):
                    for b in range(TB):
                        o = (c * TB + b) * P
                        last = mm(SA[:, o:o + P], left[:, c, b * P:(b + 1) * P], right[:, c, b * P:(b + 1) * P],
                                  start=True, stop=True)
                last.then_inc(level_mm, 1)

            def cross(L):
                pe.wait_ge(x_qk, 2 * (L + 1))
                pe.wait_ge(level_ev, (L + 1) * (NLEV + 1))
                for c in range(CC):
                    last = mm(SA[:, c * P:(c + 1) * P], E[0][:, c, 0:P], E[0][:, c, P:TOK], start=True, stop=True)
                last.then_inc(x_mm, 1)

            def hgrn_out(L):
                evacuated(pe, L, FIRST["i"] + 2)
                pe.wait_ge(level_add, (L + 1) * NLEV)
                pe.wait_ge(x_ev, L + 1)
                for c in range(CC):
                    hd = slice(c * P, (c + 1) * P)
                    mm(TA[:, c * TOK:c * TOK + P], i_tm[:, 0, hd], sc[:, c * TB, :], start=True, stop=True)
                    mm(TA[:, c * TOK + P:(c + 1) * TOK], i_tm[:, 0, hd], scx[:, c, :], start=True, stop=False)
                    last = mm(TA[:, c * TOK + P:(c + 1) * TOK], i_tm[:, 1, hd], sc[:, c * TB + 1, :],
                              start=False, stop=True)
                last.then_inc(o_mm, 1)

            def hgrn_ss(L):
                pe.wait_ge(o_sq, L + 1)
                for q in range(3):
                    last = mm(SA[:, q * 512:(q + 1) * 512], mean128[:], flat(E[1][:])[:, q * 512:(q + 1) * 512],
                              start=True, stop=True)
                last.then_inc(o_ss, 1)

            def mixer(L):
                normalise(2 * L)
                for m in range(MIX):
                    if m == FIRST["w_out"] and FEEDS[L]:
                        pe.sem_inc((d_split_free, m_split_free)[L], F_SLOTS)
                    piece(L, m)
                    if m in ATTN_O_AT:
                        attention(L, ATTN_O_AT[m], 3)
                    if m in ATTN_AT:
                        attention(L, *ATTN_AT[m])
                    if m in LEVEL_AT:
                        level(L, LEVEL_AT[m])
                    if m == CROSS_AT:
                        cross(L)
                    if m == HGRN_O_AT:
                        hgrn_out(L)
                    if m == HGRN_SS_AT:
                        hgrn_ss(L)

            def dense():
                Y = [ps[:, 4 + b * 2 + h, :] for b in range(TB) for h in range(2)]

                def up(v, n):
                    for half in range(2):
                        q = half if v == 0 else 3 * v - 1 + half
                        pe.wait_ge(d_raw_free, n * 6 + (F_SLOTS + q + 1))
                        wh, wl = (t[q % F_SLOTS][:].rearrange("p (k n) -> p k n", k=4) for t in (f_hi, f_lo))
                        for b in range(TB):
                            if half == 0 and v > 1:
                                pe.wait_ge(aT_lo, n * 4 + (TB * (v - 2) + b + 1))
                            tok = slice(b * P, (b + 1) * P)
                            for c in range(4):
                                k = 4 * half + c
                                last = split_mm(h_bank(v, b), hT_hi[:, k, tok], hT_lo[:, k, tok], wh[:, c, :], wl[:, c, :],
                                                k == 0, k == DC - 1)
                        last.then_inc(d_split_free, 1)

                def down(v, n, first=False, final=False):
                    q = DENSE - 1 if final else 3 * (v + 1) + 1
                    pe.wait_ge(d_raw_free, n * 6 + (F_SLOTS + q + 1))
                    pe.wait_ge(aT_lo, n * 4 + TB * (v + 1))
                    wh, wl = (t[q % F_SLOTS][:].rearrange("p (c h n) -> p c h n", c=2, h=2) for t in (f_hi, f_lo))
                    for b in range(TB):
                        for c in range(2):
                            for h in range(2):
                                last = split_mm(Y[b * 2 + h], actT_hi[:, b, c, :], actT_lo[:, b, c, :], wh[:, c, h, :],
                                                wl[:, c, h, :], first and c == 0, final and c == 1)
                    last.then_inc(d_split_free, 1)

                def turn_act(v, n):
                    for b in range(TB):
                        pe.wait_ge(act_done, n * 4 + (TB * v + b + 1))
                        for c in range(2):
                            last = turn(h_bank(v, b)[:, c * P:(c + 1) * P], act_tm[:, b, c * P:(c + 1) * P])
                        last.then_inc(aT_psum, 1)

                up(0, 0)
                turn_act(0, 0)
                for v in (1, 2):
                    up(v, 0)
                    down(v - 1, 0, first=v == 1)
                    turn_act(v, 0)
                with pe.Fori(0, (DENSE_UNITS - 3) // 2) as n:
                    for v in (3, 4):
                        up(v, n)
                        down(v - 1, n)
                        turn_act(v, n)
                down(DENSE_UNITS - 1, 0, final=True)

            def moe():
                pe.wait_ge(r_lo, 1)
                for b in range(TB):
                    tok = slice(b * P, (b + 1) * P)
                    for k in range(DC):
                        last = split_mm(ps[:, 2, b * NE:(b + 1) * NE], hT_hi[:, k, tok], hT_lo[:, k, tok],
                                        router_hi[:, k, :], router_lo[:, k, :], k == 0, k == DC - 1)
                last.then_inc(logits, 1)
                pe.wait_ge(chosen_ready, 1)
                mm(ps[:, 3, 0:NE], before[:], chosen[:, 0, :], start=True, stop=True)
                mm(ps[:, 3, NE:2 * NE], before[:], chosen[:, 1, :], start=True, stop=False)
                mm(ps[:, 3, NE:2 * NE], ones[:], chosen[:, 0, :], start=False, stop=True)
                mm(ps[:, 3, 2 * NE:3 * NE], ones[:], chosen[:, 0, :], start=True, stop=False)
                mm(ps[:, 3, 2 * NE:3 * NE], ones[:], chosen[:, 1, :], start=False, stop=True).then_inc(counted, 1)
                pe.wait_ge(hg, 1)
                pe.wait_ge(table, 1)
                T = n_passes(pe)

                def gather(i):
                    pe.wait_ge(sel_built, i + 1)
                    for k in range(DC):
                        for b in range(TB):
                            last = mm(XT_psum[:, k, :], h_tm[:, b, k * P:(k + 1) * P], sel01[:, b, :],
                                      start=b == 0, stop=b == TB - 1)
                    last.then_inc(gathered, 1)

                def turn_sel(i):
                    pe.wait_ge(x_added, i * TB + TB)
                    for b in range(TB):
                        turn(ps[:, 6, b * P:(b + 1) * P], sel01[:, b, :])
                    for b in range(TB):
                        last = mm(ps[:, 7, 0:1], sel01[:, b, :], GATE[:, bass.ds(i, 1), b], start=b == 0, stop=b == TB - 1)
                    last.then_inc(sel_turned, 1)

                def scatter(i):
                    pe.wait_ge(Y_lo_done, i + 1)
                    pe.wait_ge(selT_done, i + 1)
                    pe.wait_ge(gslot_done, i + 1)
                    for b in range(TB):
                        for h in range(2):
                            half = slice(h * 512, (h + 1) * 512)
                            for y in (Y_hi, Y_lo):
                                last = mm(ps[:, 4 + 2 * b + h, :], selT[:, b * P:(b + 1) * P], y[:, half],
                                          start=y is Y_hi, stop=y is Y_lo)
                        last.then_inc(scattered, 1)

                def up(i, v, n):
                    if v > 1:
                        pe.wait_ge(mT_lo_done, i * MOE_UNITS + n * 2 + (v - 1))
                    for half in range(2):
                        q = m_piece(v, half - 1) if v else half
                        pe.wait_ge(m_raw_free, i * PASS_PIECES + n * 6 + (F_SLOTS + q + 1))
                        wh, wl = (t[q % F_SLOTS][:].rearrange("p (k n) -> p k n", k=4) for t in (f_hi, f_lo))
                        for c in range(4):
                            k = 4 * half + c
                            last = split_mm(ps[:, v % 2, :], XT_hi[:, k, :], XT_lo[:, k, :], wh[:, c, :], wl[:, c, :],
                                            k == 0, k == DC - 1)
                        last.then_inc(m_split_free, 1)

                def down(i, v, n):
                    q = m_piece(v + 1, 1) if v < MOE_UNITS - 1 else PASS_PIECES - 1
                    pe.wait_ge(m_raw_free, i * PASS_PIECES + n * 6 + (F_SLOTS + q + 1))
                    pe.wait_ge(mT_lo_done, i * MOE_UNITS + n * 2 + (v + 1))
                    wh, wl = (t[q % F_SLOTS][:].rearrange("p (c h n) -> p c h n", c=2, h=2) for t in (f_hi, f_lo))
                    for c in range(2):
                        for h in range(2):
                            last = split_mm(ps[:, 2 + h, :], mT_hi[:, c, :], mT_lo[:, c, :], wh[:, c, h, :],
                                            wl[:, c, h, :], v == 0 and c == 0, v == MOE_UNITS - 1 and c == 1)
                    last.then_inc(m_split_free, 1)

                def turn_act(i, v, n):
                    pe.wait_ge(m_act_done, i * MOE_UNITS + n * 2 + (v + 1))
                    for c in range(2):
                        last = turn(ps[:, v % 2, c * P:(c + 1) * P], m_act[:, c * P:(c + 1) * P])
                    last.then_inc(mT_psum, 1)

                def unit(i, v, n):
                    up(i, v, n)
                    down(i, v - 1, n)
                    turn_act(i, v, n)

                gather(0)
                with pe.Fori(0, T) as i:
                    pe.wait_ge(XT_lo_done, i + 1)
                    up(i, 0, 0)
                    scatter(i)
                    turn_act(i, 0, 0)
                    unit(i, 1, 0)
                    turn_sel(i)
                    unit(i, 2, 0)
                    unit(i, 3, 0)
                    with pe.Fori(0, M_UNIT_PAIRS - 1) as n:
                        for v in (4, 5):
                            unit(i, v, n)
                    for v in (MOE_UNITS - 2, MOE_UNITS - 1):
                        unit(i, v, 0)
                    gather(i + 1)
                    down(i, MOE_UNITS - 1, 0)
                pe.wait_ge(XT_lo_done, T + 1)
                scatter(T)

            pe.wait_ge(vec_in, 16 * N_VEC)
            pe.wait_ge(masks, N_MASKS)
            turn(ps[:, 7, 0:NROWS], rows[0:NROWS, :], NROWS).then_inc(vec_T, 1)
            turn(ps[0:HD, 6, 0:4], hrows[:, :], 4).then_inc(vec_T, 1)
            mixer(0)
            if stop_at != "mixer0":
                normalise(1)
                pe.wait_ge(hT_ready, 2)
                dense()
            if LAYERS == 2:
                mixer(1)
            if stop_at is None:
                normalise(3)
                pe.wait_ge(hT_ready, 2 * DEPTH)
                moe()

        @block.vector
        def _(dve):
            V = nc.vector
            steps = {"n": 0}

            def link(ins):
                steps["n"] += 1
                ins.then_inc(dve_step, 1)
                dve.wait_ge(dve_step, steps["n"])

            def lo(p, parts=P, n=PIECE):
                dve.wait_ge(hi_done, p + 1)
                V.tensor_tensor(w_lo[0:parts, p % RAW, 0:n], raw[0:parts, p % RAW, 0:n],
                                w_hi[0:parts, p % SPLIT, 0:n].bitcast(F32), ALU.subtract).then_inc(lo_done, 1)

            def constants():
                dve.wait_ge(masks, N_MASKS)
                V.memset(ones[:], 1.0)
                V.memset(mean128[:], 1.0 / P)
                V.memset(lbm[:, 0, :], LB_FLOOR)
                V.memset(oml[:, 0, :], 1.0)
                V.memset(kfix[:, 0, :], LB_FLOOR)
                dve.wait_ge(vec_T, 2)
                V.tensor_copy(cols[:, 0:NROWS], ps[:, 7, 0:NROWS])
                link(V.tensor_copy(hcols[:], ps[0:HD, 6, 0:4]))
                a0, a1 = cols[:, R_LB:R_LB + CC], cols[:, R_LB + CC:R_LB + 2 * CC]
                link(V.tensor_tensor(lbt[:, 2, :], a0, a1, ALU.max))
                V.tensor_tensor(lbt[:, 0, :], a0, lbt[:, 2, :], ALU.subtract)
                V.tensor_tensor(lbt[:, 1, :], a1, lbt[:, 2, :], ALU.subtract).then_inc(lb_diff, 1)
                dve.wait_ge(lb_exp, 1)
                link(V.tensor_tensor(lbt[:, 0, :], lbt[:, 2, :], lbt[:, 3, :], ALU.add))
                link(V.reciprocal(lbt[:, 1, :], lbt[:, 0, :]))
                V.tensor_tensor(oml[:, 1, :], lbt[:, 2, :], lbt[:, 1, :], ALU.mult)
                link(V.tensor_tensor(lbt[:, 0, :], lbt[:, 3, :], lbt[:, 1, :], ALU.mult))
                link(V.tensor_scalar(lbm[:, 1, :], lbt[:, 0, :], LB_FLOOR, None, ALU.max))
                link(V.tensor_tensor(kfix[:, 1, :], lbm[:, 1, :], lbt[:, 0, :], ALU.subtract))

            def attention_mask(at0, n, g, window, dilation):
                d = amask[:, at0 + g * n:at0 + (g + 1) * n]
                ok, dist, rem = E[0][:, 0, 0:n], E[0][:, 1, 0:n], E[1][:, 0, 0:n].bitcast(I32)
                link(V.tensor_copy(dist, d.bitcast(I32)))
                link(V.tensor_scalar(ok, dist, float(TOK), None, ALU.is_ge))
                if dilation > 1:
                    link(V.tensor_scalar(rem, d.bitcast(I32), dilation - 1, None, ALU.bitwise_and))
                    link(V.tensor_copy(dist, rem))
                    link(V.scalar_tensor_tensor(ok, dist, 0.0, ok, ALU.is_equal, ALU.mult))
                if window < TOK:
                    link(V.scalar_tensor_tensor(ok, dist, float(TOK + window), ok, ALU.is_le, ALU.mult))
                link(V.tensor_scalar(d, ok, 1.0, -NEG_BIG, ALU.subtract, ALU.mult))

            def level_mask(n):
                if n == 0:
                    V.tensor_copy(hmask[:, 0, :], ident[:])
                else:
                    h = LEVELS[n]
                    rem, start = E[0][:, 0, 0:P], E[1][:, 0, 0:P]
                    s_rem, s_start, s_first = (scol[:, q:q + 1] for q in range(3))
                    V.tensor_scalar(E[0][:, 1, 0:P].bitcast(I32), lane_i[:], 2 * h - 1, None, ALU.bitwise_and)
                    link(V.tensor_scalar(scol[:, 3:4].bitcast(I32), part_i[:], 2 * h - 1, None, ALU.bitwise_and))
                    V.tensor_copy(rem, E[0][:, 1, 0:P].bitcast(I32))
                    link(V.tensor_copy(s_rem, scol[:, 3:4].bitcast(I32)))
                    V.tensor_tensor(start, lane[:], rem, ALU.subtract)
                    V.tensor_tensor(s_start, part[:], s_rem, ALU.subtract)
                    link(V.tensor_scalar(s_first, s_rem, float(h), None, ALU.is_lt))
                    link(V.tensor_scalar(hmask[:, n, :], start, s_start, s_first, ALU.is_equal, ALU.mult))
                    link(V.scalar_tensor_tensor(hmask[:, n, :], rem, float(h), hmask[:, n, :], ALU.is_ge, ALU.mult))

            def normalise(n):
                dve.wait_ge(x_root, n + 1)
                link(V.reciprocal(rstd[:], rstd[:]))
                for b in range(TB):
                    last = V.tensor_scalar(h_tm[:, b, :], x[:, b, :], rstd[:, b:b + 1], None, ALU.mult)
                last.then_inc(h_ready, 1)
                first = (R_AN if n % 2 == 0 else R_FN) + (n // 2) * DC
                for k in range(DC):
                    dve.wait_ge(hT_hi_done, DC * n + 2 * (k // 2) + 2)
                    last = V.scalar_tensor_tensor(hT_lo[:, k, :], ps[:, 2 + k // 2, (k % 2) * TOK:(k % 2 + 1) * TOK],
                                                  col(first + k), hT_hi[:, k, :].bitcast(F32), ALU.mult, ALU.subtract)
                last.then_inc(hT_ready, 1)

            def evacuate(L, m):
                name, c, _ = ORDER[m]
                if name not in ("proj_a", "proj_b", "proj_c", "w_out"):
                    return
                dve.wait_ge(used, BASE[L] + m + 1)
                g, free = G[m % 2], g_free[m % 2]
                if name == "w_out":
                    xs = x[:, :, c * COLS:(c + 1) * COLS]
                    V.tensor_tensor(xs, g.rearrange("p (b n) -> p b n", b=TB), xs, ALU.add).then_inc(free, 1)
                    return
                g = g.rearrange("p (c t) -> p c t", c=2)
                two = slice(2 * c, 2 * c + 2)
                gate = {"proj_a": "gate_a", "proj_b": "gate_b", "proj_c": "gate_c"}[name]
                evacuated(dve, L, FIRST[gate] + c)
                if name == "proj_a":
                    V.tensor_tensor(merged[:, two, :], g, sig_ab[:, two, :], ALU.mult).then_inc(free, 1)
                    return
                V.tensor_tensor(term[:], g, (sig_ab if name == "proj_b" else sig_c)[:, two, :], ALU.mult).then_inc(free, 1)
                evacuated(dve, L, m)
                last = V.tensor_tensor(merged[:, two, :], merged[:, two, :], term[:], ALU.add)
                if name == "proj_b":
                    link(last)
                else:
                    last.then_inc(merge, 1)
                    dve.wait_ge(merged_hi, 4 * L + c + 1)
                    V.tensor_tensor(hT_lo[:, two, :], merged[:, two, :], hT_hi[:, two, :].bitcast(F32),
                                    ALU.subtract).then_inc(merged_lo, 1)

            def qk_norm(L, t, name):
                evacuated(dve, L, FIRST[name] + 2)
                v = t[:].rearrange("p b (h e) -> p (b h) e", e=HD)
                sq = flat(E[0][:]).rearrange("p (h e) -> p h e", e=HD)
                link(V.tensor_tensor(sq, v, v, ALU.mult))
                V.tensor_reduce(qkss[:], sq, AX, ALU.add).then_inc(qk_ss, 1)
                dve.wait_ge(qk_root, 2 * L + (1 if name == "q" else 2))
                link(V.reciprocal(qkss[:], qkss[:]))
                V.tensor_tensor(v, v, qkss[:].rearrange("p (h o) -> p h o", o=1).broadcast_to(v.shape),
                                ALU.mult).then_inc(qk_normed, 1)
                dve.wait_ge(qk_normed, 2 * L + (1 if name == "q" else 2))

            def forget(L):
                evacuated(dve, L, FIRST["f"] + 2)
                for c in range(CC):
                    V.tensor_scalar(kc[:, c, :], kc[:, c, :], oml[:, L, c:c + 1], kfix[:, L, c:c + 1],
                                    ALU.mult, ALU.subtract)
                    last = V.tensor_scalar(bcum[:, c, :], bcum[:, c, :], oml[:, L, c:c + 1], lbm[:, L, c:c + 1],
                                           ALU.mult, ALU.add)
                last.then_inc(kc_done, 1)
                dve.wait_ge(kc_done, L + 1)
                link(V.tensor_scalar(E[0][:], bcum[:], 2.0 ** -LN_SHIFT, None, ALU.is_lt))
                link(V.tensor_scalar(E[1][:], E[0][:], 2.0 ** LN_SHIFT, 1.0, ALU.mult, ALU.max))
                V.tensor_tensor(bcum[:], bcum[:], E[1][:], ALU.mult).then_inc(f_arg, 1)

            def cumulate(L):
                dve.wait_ge(f_ln, L + 1)
                link(V.scalar_tensor_tensor(bcum[:], E[0][:], -LN_SHIFT * LN2, bcum[:], ALU.mult, ALU.add))
                for c in range(CC):
                    for b in range(TB):
                        s = bcum[:, c, b * P:(b + 1) * P]
                        last = V.tensor_tensor_scan(s, ones[:], s, 0.0, ALU.mult, ALU.add)
                last.then_inc(cum, 1)

            def level_read(L, n):
                dve.wait_ge(level_mm, L * (NLEV + 1) + n + 1)
                dst = sc[:] if n == 0 else flat(E[n % 2][:]).rearrange("p (a t) -> p a t", t=P)
                V.tensor_tensor(dst, SA.rearrange("p (a t) -> p a t", t=P),
                                hmask[:, n:n + 1, :].broadcast_to([P, CC * TB, P]), ALU.mult).then_inc(level_ev, 1)

            def level_qk(L, n):
                h = LEVELS[n]
                dve.wait_ge(decay, L * NLEV + n)
                e1, e2 = halves(E[n % 2], h)
                V.tensor_tensor(e1, e1, halves(kc, h)[0], ALU.mult).then_inc(qk_level, 1)
                V.tensor_tensor(e2, e2, halves(qc, h)[1], ALU.mult).then_inc(qk_level, 1)

            def cross_qk(L):
                dve.wait_ge(x_decay, (L + 1) * (CC + 1))
                V.tensor_tensor(E[0][:, :, 0:P], E[0][:, :, 0:P], kc[:, :, 0:P], ALU.mult).then_inc(x_qk, 1)
                V.tensor_tensor(E[0][:, :, P:TOK], E[0][:, :, P:TOK], qc[:, :, P:TOK], ALU.mult).then_inc(x_qk, 1)

            def hgrn_gate(L):
                dve.wait_ge(o_root, L + 1)
                evacuated(dve, L, FIRST["g"] + 2)
                link(V.reciprocal(E[0][:], E[0][:]))
                V.scalar_tensor_tensor(flat(E[1][:]), TA, col(R_HG + L), flat(E[0][:]), ALU.mult,
                                       ALU.mult).then_inc(o_read, 1)
                dve.wait_ge(o_read, L + 1)
                V.tensor_tensor(E[1][:], E[1][:], gc[:], ALU.mult).then_inc(o_gated, 1)

            def attention(L, j):
                n = L * SLOTS_PER_GROUP + j
                parts = ((slice(0, 3 * P), SA[:, 0:3 * P]), (slice(3 * P, NS), SA[:, 512:512 + W3]))
                dve.wait_ge(a_score, n + 1)
                dve.wait_ge(a_pturn, n)
                for s, scores in parts:
                    last = V.scalar_tensor_tensor(prob[:, s], scores, float(HD) ** -0.5, amask[:, s], ALU.mult, ALU.add)
                link(last)
                for b, (s, _) in enumerate(parts):
                    last = V.tensor_reduce(smax[:, b:b + 1], prob[:, s], AX, ALU.max)
                link(last)
                V.tensor_scalar(smax[:], smax[:], -1.0, None, ALU.mult).then_inc(a_max, 1)
                dve.wait_ge(a_exp, 2 * (n + 1))
                link(V.reciprocal(rden[:], den[:]))
                for b, (s, _) in enumerate(parts):
                    last = V.tensor_scalar(prob[:, s], prob[:, s], rden[:, b:b + 1], None, ALU.mult)
                last.then_inc(a_prob, 1)

            def conv(L):
                evacuated(dve, L, FIRST["cb"] + 2)
                link(V.tensor_tensor(xb[:], xb[:], cb[:], ALU.mult))
                for c in range(CC):
                    last = V.tensor_scalar(cb[:, c, :], xb[:, c, :], conv_col(L, 0, c), None, ALU.mult)
                link(last)
                for j in range(1, conv_w.shape[1]):
                    for c in range(CC):
                        y = cb[:, c, j:TOK]
                        last = V.scalar_tensor_tensor(y, xb[:, c, 0:TOK - j], conv_col(L, j, c), y, ALU.mult, ALU.add)
                    link(last)

            def mixer(L):
                normalise(2 * L)
                for m in range(MIX + 2):
                    if m < MIX:
                        parts, k = SHAPE.get(ORDER[m][0], (P, DC))
                        lo(BASE[L] + m, parts, k * COLS)
                    if m >= 2:
                        evacuate(L, m - 2)
                    if L == 0 and 1 <= m <= 2 * len(GROUPS):
                        at0, n = ((0, P), (3 * P, TOK))[(m - 1) // len(GROUPS)]
                        g = (m - 1) % len(GROUPS)
                        attention_mask(at0, n, g, *GROUPS[g])
                    if L == 0 and 7 <= m <= 7 + NLEV:
                        level_mask(m - 7)
                    if m == FIRST["q"] + 5:
                        qk_norm(L, q_tm, "q")
                    if m == FIRST["k"] + 5:
                        qk_norm(L, k_tm, "k")
                    if m - 2 in ATTN_O_AT:
                        j = ATTN_O_AT[m - 2]
                        dve.wait_ge(a_ohi, L * SLOTS_PER_GROUP + j + 1)
                        V.tensor_tensor(o_lo[:, j, :], SA[0:HD, 0:TOK], o_hi[:, j, :].bitcast(F32),
                                        ALU.subtract).then_inc(a_olo, 1)
                    if m - 2 in ATTN_AT and ATTN_AT[m - 2][1] == 1:
                        attention(L, ATTN_AT[m - 2][0])
                    if m == 17:
                        forget(L)
                    if m == 19:
                        cumulate(L)
                    if m - 2 in LEVEL_AT:
                        level_read(L, LEVEL_AT[m - 2])
                    if m in LEVEL_AT and LEVEL_AT[m]:
                        level_qk(L, LEVEL_AT[m])
                    if m == CROSS_AT:
                        cross_qk(L)
                    if m == HGRN_SS_AT + 2:
                        hgrn_gate(L)
                    if m == HGRN_SS_AT + 3:
                        dve.wait_ge(yc_hi_done, L + 1)
                        V.tensor_tensor(yc_lo[:], E[1][:], yc_hi[:].bitcast(F32), ALU.subtract).then_inc(yc_done, 1)
                    if m == FIRST["cb"] + 5:
                        conv(L)
                    if m == FIRST["bb"] + 5:
                        evacuated(dve, L, FIRST["bb"] + 2)
                        V.tensor_tensor(xb[:], cb[:], bb[:], ALU.mult).then_inc(conv_y, 1)
                    if m == FIRST["bb"] + 7:
                        dve.wait_ge(conv_hi, L + 1)
                        V.tensor_tensor(yb_lo[:], xb[:], yb_hi[:].bitcast(F32), ALU.subtract).then_inc(conv_lo, 1)
                    if m == MIX and FEEDS[L]:
                        (dense_lo if L == 0 else partial(moe_lo, 0))(0, 0)

            def dense_lo(q, n):
                dve.wait_ge(d_hi_done, n * 6 + (q + 1))
                V.tensor_tensor(f_lo[q % F_SLOTS][:], f_raw[q % F_SLOTS][:], f_hi[q % F_SLOTS][:].bitcast(F32),
                                ALU.subtract).then_inc(d_raw_free, 1)

            def dense():
                def gate_up(v, n):
                    for b in range(TB):
                        dve.wait_ge(silu, n * 4 + (TB * v + b + 1))
                        V.tensor_tensor(act_tm[:, b, :], act_tm[:, b, :], h_bank(v, b)[:, COLS:2 * COLS],
                                        ALU.mult).then_inc(act_done, 1)

                def turned(v, n):
                    for b in range(TB):
                        dve.wait_ge(aT_hi, n * 4 + (TB * v + b + 1))
                        V.tensor_tensor(flat(actT_lo[:, b]), h_bank(v, b)[:, 0:COLS],
                                        flat(actT_hi[:, b]).bitcast(F32), ALU.subtract).then_inc(aT_lo, 1)

                def unit(v, n, split=True):
                    if split:
                        dense_lo(3 * v + AHEAD, n)
                        dense_lo(3 * v + 1 + AHEAD, n)
                    gate_up(v, n)
                    if split:
                        dense_lo(3 * v + 2 + AHEAD, n)
                    turned(v, n)

                for q in range(1, AHEAD):
                    dense_lo(q, 0)
                unit(0, 0)
                with dve.Fori(0, (DENSE_UNITS - 3) // 2) as n:
                    for v in (1, 2):
                        unit(v, n)
                unit(DENSE_UNITS - 2, 0)
                unit(DENSE_UNITS - 1, 0, split=False)
                dve.wait_ge(d_split_free, F_SLOTS + DENSE)
                for b in range(TB):
                    V.tensor_tensor(x[:, b, :], x[:, b, :], flat(ps[:, 4 + 2 * b:6 + 2 * b, :]), ALU.add).then_inc(x_done, 1)
                dve.wait_ge(x_done, TB)

            def moe_lo(i, q, n):
                dve.wait_ge(m_hi_done, i * PASS_PIECES + n * 6 + (q + 1))
                V.tensor_tensor(f_lo[q % F_SLOTS][:], f_raw[q % F_SLOTS][:], f_hi[q % F_SLOTS][:].bitcast(F32),
                                ALU.subtract).then_inc(m_raw_free, 1)

            def moe():
                dve.wait_ge(r_hi, 1)
                V.tensor_tensor(router_lo[:], router[:], router_hi[:].bitcast(F32), ALU.subtract).then_inc(r_lo, 1)
                dve.wait_ge(gain_in, 16)
                for b in range(TB):
                    last = V.tensor_tensor(h_tm[:, b, :], h_tm[:, b, :], gain_row[:], ALU.mult)
                last.then_inc(hg, 1)
                for q in range(1, AHEAD):
                    moe_lo(0, q, 0)
                dve.wait_ge(masks, N_MASKS + 2)
                dve.wait_ge(logits, 1)
                link(V.tensor_copy(flat(logit[:]), ps[:, 2, 0:TB * NE]))
                other = logit[:].rearrange("p b (o e) -> p b o e", o=1).broadcast_to([P, TB, NE, NE])
                own = logit[:].rearrange("p b (e o) -> p b e o", o=1).broadcast_to([P, TB, NE, NE])
                V.tensor_tensor(gt[:], other, own, ALU.is_gt)
                link(V.tensor_tensor(eq[:], other, own, ALU.is_equal))
                link(V.tensor_tensor(eq[:], eq[:], tri[:].rearrange("p (o e) f -> p o e f", o=1)
                                     .broadcast_to([P, TB, NE, NE]), ALU.mult))
                link(V.tensor_tensor(gt[:], gt[:], eq[:], ALU.add))
                link(V.tensor_reduce(rank[:], gt[:], AX, ALU.add))
                V.tensor_scalar(chosen[:], rank[:], 1.5, None, ALU.is_lt).then_inc(chosen_ready, 1)
                link(V.tensor_reduce(lmax[:], logit[:], AX, ALU.max))
                V.tensor_tensor(ez[:], logit[:], lmax[:].rearrange("p (b o) -> p b o", o=1).broadcast_to([P, TB, NE]),
                                ALU.subtract).then_inc(z_ready, 1)
                dve.wait_ge(z_exp, 1)
                link(V.tensor_tensor(ez[:], ez[:], chosen[:], ALU.mult))
                link(V.tensor_reduce(esum[:], ez[:], AX, ALU.add))
                link(V.reciprocal(esum[:], esum[:]))
                link(V.tensor_tensor(gate[:], ez[:], esum[:].rearrange("p (b o) -> p b o", o=1)
                                     .broadcast_to([P, TB, NE]), ALU.mult))
                dve.wait_ge(counted, 1)
                link(V.scalar_tensor_tensor(flat(place[:]), ps[:, 3, 0:TB * NE], 1000.0, flat(chosen[:]), ALU.add, ALU.mult))
                link(V.tensor_scalar(place[:], place[:], 1000.0, None, ALU.subtract))
                link(V.tensor_scalar(over[:], ps[:, 3, TB * NE:(TB + 1) * NE], P + 0.5, None, ALU.is_gt))
                link(V.tensor_tensor_scan(over_n[:], ones[:, 0:NE], over[:], 0.0, ALU.mult, ALU.add))
                link(V.tensor_scalar(tabf[:, PASSES:PASSES + 1], over_n[:, NE - 1:NE], float(NE), None, ALU.add))
                link(V.tensor_tensor(over_n[:], over_n[:], over[:], ALU.subtract))
                for j in range(OVER):
                    last = V.scalar_tensor_tensor(pick[:, j, :], over_n[:], float(j), over[:], ALU.is_equal, ALU.mult)
                link(last)
                for t, tb, shift in ((POS, place, float(P)), (GATE, gate, 0.0)):
                    V.tensor_copy(t[:, 0:NE, :].rearrange("p e b -> p b e"), tb[:])
                    for b in range(TB):
                        last = V.tensor_tensor(tmp8[:, b], pick[:], tb[:, b:b + 1, :].broadcast_to([P, OVER, NE]), ALU.mult)
                    link(last)
                    o = t[:, NE:PASSES, :].rearrange("p j b -> p b j")
                    link(V.tensor_reduce(o, tmp8[:], AX, ALU.add))
                    link(V.tensor_scalar(o, o, shift, None, ALU.subtract))
                V.tensor_copy(tabf[:, 0:NE], iota8[:])
                link(V.tensor_tensor(tmp8[:, 0], pick[:], iota8[:].rearrange("p (o e) -> p o e", o=1)
                                     .broadcast_to([P, OVER, NE]), ALU.mult))
                link(V.tensor_reduce(tabf[:, NE:PASSES], tmp8[:, 0], AX, ALU.add))
                V.memset(POS[:, PASSES, :], -1.0)
                V.tensor_copy(tab[:], tabf[:]).then_inc(table, 1)
                dve.wait_ge(table, 1)
                T = n_passes(dve)

                def gate_up(i, v, n):
                    dve.wait_ge(m_silu, i * MOE_UNITS + n * 2 + (v + 1))
                    V.tensor_tensor(m_act[:], m_act[:], ps[:, v % 2, COLS:2 * COLS], ALU.mult).then_inc(m_act_done, 1)

                def turned(i, v, n):
                    dve.wait_ge(mT_hi_done, i * MOE_UNITS + n * 2 + (v + 1))
                    V.tensor_tensor(flat(mT_lo[:]), ps[:, v % 2, 0:COLS], flat(mT_hi[:]).bitcast(F32),
                                    ALU.subtract).then_inc(mT_lo_done, 1)

                def unit(i, v, n, between=None):
                    moe_lo(i, m_piece(v, 0) + AHEAD, n)
                    moe_lo(i, m_piece(v, 1) + AHEAD, n)
                    gate_up(i, v, n)
                    moe_lo(i, m_piece(v, 2) + AHEAD, n)
                    if between is not None:
                        between(i)
                    turned(i, v, n)

                def select(i):
                    for b in range(TB):
                        last = V.tensor_scalar(sel01[:, b, :], lane[:], POS[:, bass.ds(i, 1), b], None, ALU.is_equal)
                    last.then_inc(sel_built, 1)

                def gathered_lo(i):
                    dve.wait_ge(XT_hi_done, i + 1)
                    V.tensor_tensor(XT_lo, XT_psum, XT_hi.bitcast(F32), ALU.subtract).then_inc(XT_lo_done, 1)

                def add_x(i):
                    for b in range(TB):
                        dve.wait_ge(scattered, i * TB + (b + 1))
                        V.tensor_tensor(x[:, b, :], x[:, b, :], flat(ps[:, 4 + 2 * b:6 + 2 * b, :]),
                                        ALU.add).then_inc(x_added, 1)

                V.memset(Y_hi[:].bitcast(F32), 0.0)
                V.memset(selT[:].bitcast(F32), 0.0).then_inc(selT_done, 1)
                V.memset(gslot[:], 0.0).then_inc(gslot_done, 1)
                V.memset(Y_lo[:].bitcast(F32), 0.0).then_inc(Y_lo_done, 1)
                select(0)
                gathered_lo(0)
                with dve.Fori(0, T) as i:
                    dve.wait_ge(Y_lo_done, i + 1)
                    unit(i, 0, 0, add_x)
                    unit(i, 1, 0)
                    dve.wait_ge(sel_turned, i + 1)
                    V.tensor_copy(gslot[:], ps[:, 7, 0:1]).then_inc(gslot_done, 1)
                    with dve.Fori(0, M_UNIT_PAIRS) as n:
                        for v in (2, 3):
                            unit(i, v, n)
                    select(i + 1)
                    for v in (MOE_UNITS - 2, MOE_UNITS - 1):
                        unit(i, v, 0)
                    gathered_lo(i + 1)
                    dve.wait_ge(Y_hi_done, i + 1)
                    dve.wait_ge(gslot_done, i + 2)
                    V.scalar_tensor_tensor(Y_lo[:], flat(ps[:, 2:4, :]), gslot[:, 0:1], Y_hi[:].bitcast(F32),
                                           ALU.mult, ALU.subtract).then_inc(Y_lo_done, 1)
                add_x(T)

            constants()
            mixer(0)
            if stop_at != "mixer0":
                normalise(1)
                dense()
            if LAYERS == 2:
                mixer(1)
            if stop_at is None:
                evacuated(dve, DEPTH - 1, MIX - 1)
                normalise(3)
                moe()


NAMES = ["x", "attn_norm", "ffn_norm", "w_in", "q_norm", "k_norm", "conv_w", "hgrn_lower_bounds", "hgrn_out_norm",
         "w_proj_a", "w_proj_b", "w_proj_c", "w_out", "dense_w1", "dense_w3", "dense_w2", "router_w", "moe_w1",
         "moe_w3", "moe_w2"]


def kernel(**inputs):
    import numpy as np
    import concourse.bacc as bacc
    from concourse.bass_utils import run_bass_kernel_spmd

    nc = bacc.Bacc("TRN2", target_bir_lowering=False, num_devices=1)
    arrays, args = {}, []
    for name in NAMES:
        a = np.ascontiguousarray(inputs[name])
        arrays[f"in_{name}"] = a
        args.append(nc.dram_tensor(f"in_{name}", a.shape, mybir.dt.from_np(a.dtype), kind="ExternalInput").ap())
    out = nc.dram_tensor("out_x", inputs["x"].shape, F32, kind="ExternalOutput").ap()
    decoder(nc, *args, out)
    r = run_bass_kernel_spmd(nc, [arrays], core_ids=[0])
    return r.results[0]["out_x"]
```

```python
from contextlib import ExitStack
from functools import partial

import concourse.bass as bass
from concourse import mybir

F32 = mybir.dt.float32
F32R = mybir.dt.float32r
I32 = mybir.dt.int32
ALU = mybir.AluOpType
ACT = mybir.ActivationFunctionType
AX = mybir.AxisListType.X

P = 128
EPS = 1e-6
NEG_BIG = -1e30
LB_FLOOR = 1e-30
GROUPS = ((128, 1), (512, 4), (2048, 16))
SLOTS_PER_GROUP = 4
HD = 64
COLS = 256
RAW, SPLIT = 4, 3
F_SLOTS = 6
AHEAD, M_AHEAD = 3, 6
PIECE = 2048
LN_SHIFT = 40
LN2 = 0.6931471805599453

SEGMENTS = (("q", 0, 3), ("k", 768, 3), ("v", 1536, 3), ("i", 6144, 3),
            ("f", 5376, 3), ("qc", 4608, 3), ("g", 6912, 3), ("gate_a", 7680, 4), ("proj_a", None, 4),
            ("xb", 2304, 3), ("cb", 3840, 3), ("bb", 3072, 3), ("gate_b", 8704, 4), ("gate_c", 9728, 4),
            ("proj_b", None, 4), ("proj_c", None, 4), ("w_out", None, 4))
ORDER = [(name, c, None if col is None else col + c * COLS)
         for name, col, n in SEGMENTS for c in range(n)]
FIRST = {}
for _n, (_name, _c, _col) in enumerate(ORDER):
    FIRST.setdefault(_name, _n)
MIX = len(ORDER)
LEVELS = (None, 64, 32, 16, 8, 4, 2, 1)
NLEV = len(LEVELS) - 1

ATTN_AT = {9 + 3 * j + s: (j, s) for j in range(SLOTS_PER_GROUP) for s in range(3)
           if s or j % 2 == 0}
ATTN_O_AT = {12 + 3 * j: j for j in range(SLOTS_PER_GROUP)}
LEVEL_AT = {22 + 2 * n: n for n in range(NLEV + 1)}
CROSS_AT, HGRN_O_AT, HGRN_SS_AT = 38, 39, 40
FORGET_AT = 17


def decoder(nc, x_in, attn_norm, ffn_norm, w_in, q_norm, k_norm, conv_w, hgrn_lb, hgrn_gain,
            w_proj_a, w_proj_b, w_proj_c, w_out, dense_w1, dense_w3, dense_w2, router_w,
            moe_w1, moe_w3, moe_w2, out, stop_at=None):
    DEPTH, D, _ = w_in.shape
    TOK = x_in.shape[1]
    TB = TOK // P
    DC = D // P
    FF = dense_w1.shape[2]
    NE, FFE = router_w.shape[2], moe_w1.shape[3]
    CW = conv_w.shape[2]
    CC = CW // P
    DENSE_UNITS = FF // COLS
    MOE_UNITS = FFE // COLS
    assert TB == 2 and D == 1024 and CC == 6 and DENSE_UNITS == 11 and MOE_UNITS % 2 == 0
    DENSE = 3 * DENSE_UNITS
    UNIT_PIECES = 3
    PASS_PIECES = 3 * MOE_UNITS
    OVER = 2 * TOK // (P + 1)
    PASSES = NE + OVER
    BASE = (0, MIX)

    with ExitStack() as ctx:
        def sb(name, shape, dt=F32):
            return ctx.enter_context(nc.sbuf_tensor(name, shape, dt))

        def sem(name):
            return ctx.enter_context(nc.semaphore(name))

        x = sb("x", [P, TB, D])
        ident = sb("ident", [P, P])
        ones = sb("ones", [P, P])
        mean128 = sb("mean128", [P, P])
        before = sb("before", [P, P])
        lane = sb("lane", [P, P])
        part = sb("part", [P, 1])
        lane_i = sb("lane_i", [P, P], I32)
        part_i = sb("part_i", [P, 1], I32)
        eps = sb("eps", [P, 1])
        amask = sb("amask", [P, 3 * P + 3 * TOK])
        hmask = sb("hmask", [P, len(LEVELS), P])
        rows = sb("rows", [P, P])
        cols = sb("cols", [P, P])
        hrows = sb("hrows", [4, 2 * HD])
        hcols = sb("hcols", [2 * HD, 4])
        router = sb("router", [P, DC, NE])
        router_hi = sb("router_hi", [P, DC, NE], F32R)
        router_lo = sb("router_lo", [P, DC, NE], F32R)
        lbm = sb("lbm", [P, DEPTH, CC])
        oml = sb("oml", [P, DEPTH, CC])
        kfix = sb("kfix", [P, DEPTH, CC])
        lbt = sb("lbt", [P, 4, CC])
        scol = sb("scol", [P, 4])
        ssq = sb("ssq", [P, TB])
        rstd = sb("rstd", [P, TB])
        root_warm = sb("root_warm", [P, 1])
        qkss = sb("qkss", [P, 24])
        smax = sb("smax", [P, TB])
        den = sb("den", [P, TB])
        rden = sb("rden", [P, TB])
        hT_hi = sb("hT_hi", [P, DC, TOK], F32R)
        hT_lo = sb("hT_lo", [P, DC, TOK], F32R)

        base = nc.sbuf_base
        top = [base + (-base) % 64]

        def at(name, shape, dt=F32, offset=None):
            n = 4
            for s in shape[1:]:
                n *= s
            if offset is None:
                offset = top[0]
                top[0] += -(-n // 32) * 32
            return nc.alloc_sbuf_tensor_at(name, shape, dt, offset=offset), offset

        arena = top[0]
        raw, raw_at = at("raw", [P, RAW, PIECE])
        w_lo, _ = at("w_lo", [P, RAW, PIECE], F32R, offset=raw_at)
        w_hi, _ = at("w_hi", [P, SPLIT, PIECE], F32R)
        i_tm, i_at = at("i_tm", [P, TB, CW])
        q_tm, q_at = at("q_tm", [P, TB, CW])
        k_tm, _ = at("k_tm", [P, TB, CW])
        v_tm, _ = at("v_tm", [P, TB, CW])
        sig_c, _ = at("sig_c", [P, DC, TOK], offset=q_at)
        xb, xb_at = at("xb", [P, CC, TOK])
        cb, cb_at = at("cb", [P, CC, TOK])
        bb, bb_at = at("bb", [P, CC, TOK])
        yb_hi, _ = at("yb_hi", [P, CC, TOK], F32R, offset=cb_at)
        yb_lo, _ = at("yb_lo", [P, CC, TOK], F32R, offset=bb_at)
        W3 = 3 * TOK
        qT, _ = at("qT", [2 * HD, W3], offset=xb_at)
        kT, _ = at("kT", [2 * HD, W3], offset=xb_at + 4 * W3)
        NS = 3 * P + W3
        prob, _ = at("prob", [P, NS], offset=xb_at + 8 * W3)
        probT, _ = at("probT", [P, NS], offset=xb_at + 8 * W3 + 4 * NS)
        h_tm, _ = at("h_tm", [P, TB, D], offset=xb_at)
        qc, qc_at = at("qc", [P, CC, TOK])
        kc, kc_at = at("kc", [P, CC, TOK])
        yc_hi, _ = at("yc_hi", [P, CC, TOK], F32R, offset=qc_at)
        yc_lo, _ = at("yc_lo", [P, CC, TOK], F32R, offset=kc_at)
        bcum, _ = at("bcum", [P, CC, TOK])
        E = [at(f"E{n}", [P, CC, TOK])[0] for n in range(2)]
        sc, _ = at("sc", [P, CC * TB, P])
        scx, _ = at("scx", [P, CC, P])
        gc, _ = at("gc", [P, CC, TOK])
        o_hi, _ = at("o_hi", [HD, SLOTS_PER_GROUP, TOK], F32R)
        o_lo, _ = at("o_lo", [HD, SLOTS_PER_GROUP, TOK], F32R)
        merged, _ = at("merged", [P, DC, TOK])
        sig_ab, _ = at("sig_ab", [P, DC, TOK])
        term, _ = at("term", [P, 2, TOK])
        assert top[0] <= nc.sbuf_usable_end, (top[0], nc.sbuf_usable_end)

        h_end = xb_at + 4 * TB * D
        assert h_end <= qc_at and i_at + 12 * PIECE <= xb_at

        def slots(name, offsets, dt=F32):
            return [at(f"{name}{s}", [P, PIECE], dt, offset=o)[0] for s, o in enumerate(offsets)]

        low = [arena + 4 * PIECE * s for s in range((i_at - arena) // (4 * PIECE))]
        early = [i_at + 4 * PIECE * s for s in range(3)]
        high = [qc_at + 4 * PIECE * s for s in range(3 * F_SLOTS - len(low) - len(early))]
        assert len(low) == RAW + SPLIT and len(high) == F_SLOTS + 2
        f_raw = slots("f_raw", high[:F_SLOTS])
        hi_at = [low[RAW + (BASE[1] + m) % SPLIT] for m in range(SPLIT)]
        f_hi = slots("f_hi", [early[0], early[2], hi_at[2], low[0], low[1], hi_at[0]], F32R)
        f_lo = slots("f_lo", [early[1], high[6], high[7], low[2], low[3], hi_at[1]], F32R)
        top[0] = f_top = high[-1] + 4 * PIECE
        act_tm, _ = at("act_tm", [P, TB, COLS])
        actT_hi, _ = at("actT_hi", [P, TB, 2, P], F32R)
        actT_lo, _ = at("actT_lo", [P, TB, 2, P], F32R)
        assert top[0] <= nc.sbuf_usable_end, (top[0], nc.sbuf_usable_end)

        top[0] = f_top
        XT_hi, XT_lo = hT_hi[:, :, 0:P], hT_lo[:, :, 0:P]
        sel01, _ = at("sel01", [P, TB, P])
        selT, _ = at("selT", [P, TOK], F32R)
        gslot, _ = at("gslot", [P, 1])
        m_act, m_act_at = at("m_act", [P, COLS], offset=h_end + 8 * D)
        mT_hi, _ = at("mT_hi", [P, 2, P], F32R)
        mT_lo, _ = at("mT_lo", [P, 2, P], F32R)
        assert h_end + 8 * D + 4 * COLS <= qc_at
        Y_hi, _ = at("Y_hi", [P, D], F32R, offset=h_end)
        Y_lo, _ = at("Y_lo", [P, D], F32R, offset=h_end + 4 * D)
        gain_row, _ = at("gain_row", [P, D], offset=h_end)
        logitsT, _ = at("logitsT", [NE, TOK], offset=m_act_at)
        logit, _ = at("logit", [P, TB, NE])
        gt, _ = at("gt", [P, TB, NE, NE])
        eq, _ = at("eq", [P, TB, NE, NE])
        tri, _ = at("tri", [P, NE, NE])
        rank, _ = at("rank", [P, TB, NE])
        chosen, _ = at("chosen", [P, TB, NE])
        lmax, _ = at("lmax", [P, TB])
        ez, _ = at("ez", [P, TB, NE])
        esum, _ = at("esum", [P, TB])
        gate, _ = at("gate", [P, TB, NE])
        place, _ = at("place", [P, TB, NE])
        over, _ = at("over", [P, NE])
        over_n, _ = at("over_n", [P, NE])
        pick, _ = at("pick", [P, OVER, NE])
        tmp8, _ = at("tmp8", [P, TB, OVER, NE])
        iota8, _ = at("iota8", [P, NE])
        POS, _ = at("POS", [P, PASSES, TB])
        GATE, _ = at("GATE", [P, PASSES, TB])
        tabf, _ = at("tabf", [P, PASSES + 1])
        tab, _ = at("tab", [P, PASSES + 1], I32)
        assert top[0] <= nc.sbuf_usable_end, (top[0], nc.sbuf_usable_end)

        ps = ctx.enter_context(nc.psum_tensor("ps", [P, 8, 512], F32))
        G = [ps[:, n, :] for n in range(2)]
        SA = ps[:, 2:5, :].rearrange("p a n -> p (a n)")
        TA = ps[:, 5:8, :].rearrange("p a n -> p (a n)")

        XT_psum = ps[:, 4:6, :].rearrange("p a (c t) -> p (a c) t", t=P)

        x_in_sem = [sem(f"x_loaded{b}") for b in range(TB)]
        vec_in, router_in, gain_in = sem("vectors_loaded"), sem("router_loaded"), sem("gain_loaded")
        landed = [sem(f"raw_landed{r}") for r in range(RAW)]
        hi_done, lo_done, used = sem("hi_done"), sem("lo_done"), sem("piece_used")
        g_free = [sem(f"g_free{n}") for n in range(2)]
        eps_ready, ident_ready = sem("eps_ready"), sem("ident_ready")
        masks = sem("masks_built")
        pool_step, dve_step = sem("pool_step"), sem("dve_step")
        vec_T, cols_ready = sem("vectors_turned"), sem("cols_ready")
        lb_diff, lb_exp = sem("lb_diff"), sem("lb_exp")
        squared = sem("x_squared")
        h_ready = sem("h_ready")
        hT_psum = sem("hT_in_psum")
        hT_hi_done = sem("hT_hi_done")
        hT_ready = sem("hT_ready")
        f_sig, f_arg, f_ln, cum = sem("forget_sigmoid"), sem("ln_argument"), sem("ln_done"), sem("cumsum_done")
        qk_normed = sem("qk_normed")
        conv_y, conv_hi, conv_lo = sem("conv_y"), sem("conv_hi"), sem("conv_lo")
        diff, decay, qk_level, level_mm, level_ev, level_add = (sem("level_diff"), sem("level_decay"), sem("level_qk"),
                                                                sem("level_mm"), sem("level_evacuated"), sem("level_added"))
        x_decay, x_qk, x_mm, x_ev = sem("cross_decay"), sem("cross_qk"), sem("cross_mm"), sem("cross_evacuated")
        o_mm, o_sq, o_ss, o_gated, yc_hi_done, yc_done = (sem("hgrn_o"), sem("hgrn_squared"), sem("hgrn_ss"), sem("hgrn_gated"),
                                                         sem("yc_hi_done"), sem("yc_done"))
        o_read = sem("hgrn_o_read")
        a_turn, a_qk, a_score, a_masked, a_max, a_exp, a_prob, a_pturn, a_pT, a_o, a_ohi, a_olo = (
            sem("attn_turned"), sem("attn_qkT"), sem("attn_scores"), sem("attn_masked"), sem("attn_max"), sem("attn_exp"),
            sem("attn_prob"), sem("attn_prob_turned"), sem("attn_probT"), sem("attn_o"), sem("attn_o_hi"), sem("attn_o_lo"))
        kc_done = sem("kc_done")
        x_root, qk_ss, qk_root, o_root = sem("x_root"), sem("qk_ss"), sem("qk_root"), sem("hgrn_root")
        merge = sem("merged_done")
        merged_hi, merged_lo = sem("merged_hi"), sem("merged_lo")
        silu, act_done, aT_psum, aT_hi, aT_lo = sem("dense_silu"), sem("dense_act"), sem("dense_actT_psum"), sem("dense_actT_hi"), sem("dense_actT_lo")
        y_first, x_done = sem("dense_y_first"), sem("dense_x")
        hg = sem("h_gained")
        r_hi, r_lo, logits, z_ready, z_exp = sem("router_hi_done"), sem("router_lo_done"), sem("logits"), sem("z_ready"), sem("z_exp")
        logitsT_done = sem("logitsT_done")
        chosen_ready, counted, table = sem("chosen_ready"), sem("tokens_counted"), sem("pass_table_ready")
        d_landed = [sem(f"dense_raw_landed{r}") for r in range(F_SLOTS)]
        m_landed = [sem(f"moe_raw_landed{r}") for r in range(F_SLOTS)]
        d_raw_free, m_raw_free = sem("dense_raw_free"), sem("moe_raw_free")
        d_hi_done, m_hi_done = sem("dense_hi_done"), sem("moe_hi_done")
        d_split_free, m_split_free = sem("dense_split_free"), sem("moe_split_free")
        sel_built, gathered, XT_hi_done, XT_lo_done = sem("sel_built"), sem("gathered"), sem("XT_hi_done"), sem("XT_lo_done")
        sel_turned, selT_done, gslot_done = sem("sel_turned"), sem("selT_done"), sem("gslot_done")
        m_silu, m_act_done, mT_psum, mT_hi_done, mT_lo_done = (sem("moe_silu"), sem("moe_act"), sem("moe_actT_psum"),
                                                               sem("moe_actT_hi"), sem("moe_actT_lo"))
        Y_hi_done, Y_lo_done, scattered = sem("Y_hi_done"), sem("Y_lo_done"), sem("scattered")
        x_added = sem("x_added")
        stored = sem("stored")

        R_AN, R_FN = 0, DEPTH * DC
        R_CV = 2 * DEPTH * DC
        R_LB = R_CV + DEPTH * 3 * CC
        R_HG = R_LB + DEPTH * CC
        NROWS = R_HG + DEPTH
        N_VEC, N_MASKS = 9, 7

        def col(r):
            return cols[:, r:r + 1]

        def conv_col(L, j, c):
            return col(R_CV + (L * 3 + j) * CC + c)

        def piece_view(t, s, parts, k):
            return t[0:parts, s, 0:k * COLS].rearrange("p (k n) -> p k n", k=k)

        SHAPE = {"proj_a": (HD, 4), "proj_b": (P, CC), "proj_c": (P, CC)}

        def source(L, m):
            name, c, c0 = ORDER[m]
            if c0 is not None:
                return w_in[L].rearrange("(k p) n -> p k n", p=P)[:, :, c0:c0 + COLS]
            w, p = {"proj_a": (w_proj_a, HD), "proj_b": (w_proj_b, P), "proj_c": (w_proj_c, P), "w_out": (w_out, P)}[name]
            return w[L].rearrange("(k p) n -> p k n", p=p)[:, :, c * COLS:(c + 1) * COLS]

        TOKEN_MAJOR = ("i", "q", "k", "v", "w_out")
        DEST = {"i": i_tm, "q": q_tm, "k": k_tm, "v": v_tm, "xb": xb, "cb": cb, "bb": bb}
        LAYERS = DEPTH if stop_at in (None, "mixer1") else 1

        FEEDS = (stop_at != "mixer0", stop_at is None)

        def evacuated(eng, L, m):
            for q in (m - 1, m):
                eng.wait_ge(g_free[q % 2], L * (MIX // 2) + q // 2 + 1)

        def halves(t, h):
            v = t[:].rearrange("p c t -> p (c t)").rearrange("p (g w) -> p g w", w=2 * h)
            return v[:, :, 0:h], v[:, :, h:2 * h]

        def flat(t):
            return t.rearrange("p a b -> p (a b)")

        def h_bank(v, b):
            return ps[:, 2 * (v % 2) + b, :]

        def last_pass_of(eng):
            return eng.value_load(tab[0:1, PASSES:PASSES + 1], min_val=NE - 1, max_val=PASSES - 1)

        def split_ahead(split, i, q, n, final):
            if not (final and q >= PASS_PIECES):
                split(i, q, n)

        def m_piece(v, c):
            return 3 * v + c

        M_UNIT_PAIRS = (MOE_UNITS - 4) // 2
        assert PASS_PIECES % F_SLOTS == 0 and F_SLOTS == 2 * 3 and AHEAD == 3 and M_AHEAD == F_SLOTS

        HI_HEAD, LO_HEAD = (1, 2), (1, 2)

        block = ctx.enter_context(nc.Block())

        @block.sync
        def _(sp):
            for b in range(TB):
                sp.dma_start(x[:, b, :], x_in[0, b * P:(b + 1) * P, :]).then_inc(x_in_sem[b], 16)
            sp.dma_start(rows[R_AN:R_FN, :], attn_norm.rearrange("l (c p) -> (l c) p", p=P)).then_inc(vec_in, 16)
            sp.dma_start(rows[R_FN:R_CV, :], ffn_norm.rearrange("l (c p) -> (l c) p", p=P)).then_inc(vec_in, 16)
            sp.dma_start(rows[R_CV:R_LB, :], conv_w.rearrange("l j (c p) -> (l j c) p", p=P)).then_inc(vec_in, 16)
            sp.dma_start(rows[R_LB:R_HG, :], hgrn_lb.rearrange("l (c p) -> (l c) p", p=P)).then_inc(vec_in, 16)
            sp.dma_start(rows[R_HG:NROWS, :], hgrn_gain).then_inc(vec_in, 16)
            for h in range(2):
                sp.dma_start(hrows[0:2, h * HD:(h + 1) * HD], q_norm).then_inc(vec_in, 16)
                sp.dma_start(hrows[2:4, h * HD:(h + 1) * HD], k_norm).then_inc(vec_in, 16)

            def load_mixer(L):
                for m in range(MIX):
                    p = BASE[L] + m
                    parts, k = SHAPE.get(ORDER[m][0], (P, DC))
                    if p >= RAW:
                        sp.wait_ge(used, p - RAW + 1)
                    if L and m == 0:
                        sp.wait_ge(d_split_free, F_SLOTS + DENSE - 3)
                    sp.dma_start(piece_view(raw, p % RAW, parts, k), source(L, m)).then_inc(landed[p % RAW], 16)

            w1 = dense_w1[0].rearrange("(k p) n -> p k n", p=P)
            w3 = dense_w3[0].rearrange("(k p) n -> p k n", p=P)
            w2 = dense_w2[0].rearrange("(u c p) n -> u p c n", p=P, c=2)

            def work_left(L):
                sp.wait_ge(used, BASE[L] + FIRST["w_out"])
                sp.sem_inc((d_raw_free, m_raw_free)[L], F_SLOTS)

            def load_up(q, n, half, c0):
                sp.wait_ge(d_raw_free, n * 6 + (q + 1))
                dst = f_raw[q % F_SLOTS][:].rearrange("p (k w n) -> p k w n", k=4, w=2)
                for w, src in enumerate((w1, w3)):
                    sp.dma_start(dst[:, :, w, :], src[:, 4 * half:4 * half + 4, c0]).then_inc(d_landed[q % F_SLOTS], 16)

            def load_down(q, n, src):
                sp.wait_ge(d_raw_free, n * 6 + (q + 1))
                dst = f_raw[q % F_SLOTS][:].rearrange("p (c n) -> p c n", c=2)
                for c in range(2):
                    sp.dma_start(dst[:, c, :], src[:, c, :]).then_inc(d_landed[q % F_SLOTS], 16)

            def load_dense():
                for half in range(2):
                    load_up(half, 0, half, slice(0, COLS))
                with sp.Fori(0, (DENSE_UNITS - 1) // 2) as n:
                    for v in (1, 2):
                        for half in range(2):
                            load_up(3 * v - 1 + half, n, half, bass.ds((n * 2 + v) * COLS, COLS))
                        load_down(3 * v + 1, n, w2[n * 2 + (v - 1)])
                load_down(DENSE - 1, 0, w2[DENSE_UNITS - 1])

            e1 = moe_w1[0].rearrange("e (k p) n -> e p k n", p=P)
            e3 = moe_w3[0].rearrange("e (k p) n -> e p k n", p=P)
            e2 = moe_w2[0].rearrange("e (u c p) n -> (e u) p c n", p=P, c=2)

            def moe_up(i, e, q, n, half, u):
                sp.wait_ge(m_raw_free, i * PASS_PIECES + n * 6 + (q + 1))
                dst = f_raw[q % F_SLOTS][:].rearrange("p (k w n) -> p k w n", k=4, w=2)
                for w, src in enumerate((e1, e3)):
                    sp.dma_start(dst[:, :, w, :], src[e, :, 4 * half:4 * half + 4, bass.ds(u * COLS, COLS)])\
                      .then_inc(m_landed[q % F_SLOTS], 16)

            def moe_down(i, e, q, n, u):
                sp.wait_ge(m_raw_free, i * PASS_PIECES + n * 6 + (q + 1))
                dst = f_raw[q % F_SLOTS][:].rearrange("p (c n) -> p c n", c=2)
                for c in range(2):
                    sp.dma_start(dst[:, c, :], e2[e * MOE_UNITS + u, :, c, :]).then_inc(m_landed[q % F_SLOTS], 16)

            def load_pass(i, e):
                for half in range(2):
                    moe_up(i, e, half, 0, half, 0)
                with sp.Fori(0, (MOE_UNITS - 2) // 2) as n:
                    for v in (1, 2):
                        for half in range(2):
                            moe_up(i, e, m_piece(v, half - 1), n, half, n * 2 + v)
                        moe_down(i, e, m_piece(v, 1), n, n * 2 + (v - 1))
                last = MOE_UNITS - 1
                for half in range(2):
                    moe_up(i, e, m_piece(last, half - 1), 0, half, last)
                moe_down(i, e, m_piece(last, 1), 0, last - 1)
                moe_down(i, e, m_piece(last, 2), 0, last)

            def load_moe():
                load_pass(0, 0)
                sp.wait_ge(table, 1)
                last_pass = last_pass_of(sp)
                with sp.Fori(1, last_pass + 1) as i:
                    load_pass(i, sp.value_load(tab[0:1, bass.ds(i, 1)], min_val=0, max_val=NE - 1))
                return last_pass

            load_mixer(0)
            if stop_at != "mixer0":
                work_left(0)
                load_dense()
            if LAYERS == 2:
                load_mixer(1)
            if stop_at is None:
                work_left(1)
                last_pass = load_moe()
            for b in range(TB):
                if stop_at is None:
                    sp.wait_ge(x_added, last_pass * TB + (TB + b + 1))
                elif stop_at == "dense":
                    sp.wait_ge(x_done, 2)
                else:
                    evacuated(sp, LAYERS - 1, MIX - 1)
                sp.dma_start(out[0, b * P:(b + 1) * P, :], x[:, b, :]).then_inc(stored, 16)
            sp.wait_ge(stored, 16 * TB)

        @block.gpsimd
        def _(pool):
            pool.memset(eps[:], EPS).then_inc(eps_ready, 1)
            pool.memset(ident[:], 0.0).then_inc(pool_step, 1)
            pool.wait_ge(pool_step, 1)
            pool.affine_select(out=ident[:], in_=ident[:], compare_op=ALU.not_equal, fill=1.0, base=0,
                               pattern=[[-1, P]], channel_multiplier=1).then_inc(ident_ready, 1)
            pool.memset(before[:], 1.0).then_inc(pool_step, 1)
            pool.iota(lane[:], pattern=[[1, P]], base=0, channel_multiplier=0,
                      allow_small_or_imprecise_dtypes=True).then_inc(masks, 1)
            pool.iota(part[:], pattern=[[0, 1]], base=0, channel_multiplier=1,
                      allow_small_or_imprecise_dtypes=True).then_inc(masks, 1)
            pool.iota(lane_i[:], pattern=[[1, P]], base=0, channel_multiplier=0).then_inc(masks, 1)
            pool.iota(part_i[:], pattern=[[0, 1]], base=0, channel_multiplier=1).then_inc(masks, 1)
            pool.iota(amask[:, 0:3 * P].bitcast(I32).rearrange("p (g j) -> p g j", g=3), pattern=[[0, 3], [-1, P]],
                      base=TOK, channel_multiplier=1).then_inc(masks, 1)
            pool.iota(amask[:, 3 * P:].bitcast(I32).rearrange("p (g j) -> p g j", g=3), pattern=[[0, 3], [-1, TOK]],
                      base=TOK + P, channel_multiplier=1).then_inc(masks, 1)
            pool.wait_ge(pool_step, 2)
            pool.affine_select(out=before[:], in_=before[:], compare_op=ALU.is_gt, fill=0.0, base=0,
                               pattern=[[1, P]], channel_multiplier=-1).then_inc(masks, 1)
            pool.dma_start(router[:], router_w[0].rearrange("(k p) e -> p k e", p=P)).then_inc(router_in, 16)

            def level_diff(L, n):
                h = LEVELS[n]
                if n == 1:
                    pool.wait_ge(cum, L + 1)
                if n > 2:
                    pool.wait_ge(level_add, L * NLEV + n - 2)
                e1, e2 = halves(E[n % 2], h)
                b1, b2 = halves(bcum, h)
                mid = b1[:, :, h - 1:h].broadcast_to(b1.shape)
                pool.tensor_tensor(e1, mid, b1, ALU.subtract).then_inc(diff, 1)
                pool.tensor_tensor(e2, b2, mid, ALU.subtract).then_inc(diff, 1)

            def level_sum(L, n):
                pool.wait_ge(level_ev, L * (NLEV + 1) + n + 1)
                if n > 1:
                    pool.wait_ge(level_add, L * NLEV + n - 1)
                h = LEVELS[n]
                late = flat(sc[:]).rearrange("p (q w) -> p q w", w=2 * h)[:, :, h:2 * h]
                level = flat(E[n % 2][:])[:, 0:CC * TB * P // 2].rearrange("p (q h) -> p q h", h=h)
                pool.tensor_tensor(late, late, level, ALU.add).then_inc(level_add, 1)

            for L in range(LAYERS):
                level_diff(L, 1)
                level_diff(L, 2)
                for n in range(1, NLEV + 1):
                    level_sum(L, n)
                    if n + 2 <= NLEV:
                        level_diff(L, n + 2)
            if stop_at is None:
                evacuated(pool, DEPTH - 1, MIX - 1)
                pool.dma_start(gain_row[:], ffn_norm[DEPTH - 1:DEPTH, :].broadcast_to([P, D])).then_inc(gain_in, 16)
                pool.iota(iota8[:], pattern=[[1, NE]], base=0, channel_multiplier=0,
                          allow_small_or_imprecise_dtypes=True).then_inc(masks, 1)
                pool.memset(tri[:], 1.0).then_inc(pool_step, 1)
                pool.wait_ge(pool_step, 3)
                pool.affine_select(out=tri[:], in_=tri[:], compare_op=ALU.is_gt, fill=0.0, base=0,
                                   pattern=[[1, NE], [-1, NE]], channel_multiplier=0).then_inc(masks, 1)
                pool.wait_ge(gain_in, 16)
                pool.wait_ge(hT_psum, DC // 2 * 2 * DEPTH)
                for b in range(TB):
                    pool.tensor_tensor(h_tm[:, b, :], h_tm[:, b, :], gain_row[:], ALU.mult).then_inc(hg, 1)
                pool.wait_ge(hg, TB)
                pool.memset(Y_hi[:].bitcast(F32), 0.0)
                pool.memset(selT[:].bitcast(F32), 0.0).then_inc(selT_done, 1)
                pool.memset(gslot[:], 0.0).then_inc(gslot_done, 1)
                pool.memset(Y_lo[:].bitcast(F32), 0.0).then_inc(Y_lo_done, 1)

        @block.scalar
        def _(act):
            A = nc.scalar.activation

            def hi(p, parts=P, n=PIECE):
                act.wait_ge(landed[p % RAW], 16 * (p // RAW + 1))
                if p >= SPLIT:
                    act.wait_ge(used, p - SPLIT + 1)
                A(w_hi[0:parts, p % SPLIT, 0:n], raw[0:parts, p % RAW, 0:n], ACT.Copy).then_inc(hi_done, 1)

            def normalise(n):
                if n % 2:
                    evacuated(act, n // 2, MIX - 1)
                for b in range(TB):
                    if n == 0:
                        act.wait_ge(x_in_sem[b], 16)
                    elif n == 2:
                        act.wait_ge(x_done, b + 1)
                    A(h_tm[:, b, :], x[:, b, :], ACT.Square, scale=float(D) ** -0.5,
                      accum_out=ssq[:, b:b + 1]).then_inc(squared, 1)
                act.wait_ge(squared, TB * (n + 1))
                A(rstd[:], ssq[:], ACT.Sqrt, bias=eps[:, 0:1]).then_inc(x_root, 1)
                if n == 0:
                    hi(0)
                elif n == 1:
                    dense_hi(2, 0)
                elif n == 3:
                    moe_hi(0, 2, 0)
                first = R_AN if n % 2 == 0 else R_FN
                if n == 0:
                    act.wait_ge(cols_ready, 1)
                for j in range(DC // 2):
                    act.wait_ge(hT_psum, (DC // 2) * n + j + 1)
                    for c in range(2):
                        A(hT_hi[:, 2 * j + c, :], ps[:, 2 + j, c * TOK:(c + 1) * TOK], ACT.Copy,
                          scale=col(first + (n // 2) * DC + 2 * j + c)).then_inc(hT_hi_done, 1)

            def evacuate(L, m):
                name, c, _ = ORDER[m]
                if name in ("proj_a", "proj_b", "proj_c", "w_out"):
                    return
                act.wait_ge(used, BASE[L] + m + 1)
                g, free = G[m % 2], g_free[m % 2]
                if name in ("i", "q", "k", "v"):
                    A(DEST[name][:, :, c * COLS:(c + 1) * COLS], g.rearrange("p (b n) -> p b n", b=TB),
                      ACT.Copy).then_inc(free, 1)
                    return
                g = g.rearrange("p (c t) -> p c t", c=2)
                two = slice(2 * c, 2 * c + 2)
                if name in ("xb", "cb", "bb"):
                    if name == "xb" and c == 0:
                        act.wait_ge(a_o, (L + 1) * SLOTS_PER_GROUP)
                    A(DEST[name][:, two, :], g, ACT.Copy).then_inc(free, 1)
                elif name == "f":
                    A(bcum[:, two, :], g, ACT.Sigmoid).then_inc(f_sig, 1)
                    A(kc[:, two, :], g, ACT.Sigmoid, scale=-1.0).then_inc(free, 1)
                elif name in ("qc", "g"):
                    A((qc if name == "qc" else gc)[:, two, :], g, ACT.Silu).then_inc(free, 1)
                elif name == "gate_c":
                    act.wait_ge(a_turn, (L + 1) * SLOTS_PER_GROUP // 2)
                    A(sig_c[:, two, :], g, ACT.Sigmoid).then_inc(free, 1)
                else:
                    if name == "gate_b":
                        evacuated(act, L, FIRST["proj_a"] + c)
                    A(sig_ab[:, two, :], g, ACT.Sigmoid).then_inc(free, 1)

            def cross_exp(L):
                act.wait_ge(level_add, L * NLEV + NLEV - 1)
                A(E[0][:, :, P:TOK], bcum[:, :, P:TOK], ACT.Exp).then_inc(x_decay, 1)
                for c in range(CC):
                    A(E[0][:, c, 0:P], bcum[:, c, 0:P], ACT.Exp, scale=-1.0,
                      bias=bcum[:, c, P - 1:P]).then_inc(x_decay, 1)

            def attention(L, j, stage):
                n = L * SLOTS_PER_GROUP + j
                if stage == 0:
                    act.wait_ge(a_turn, n // 2 + 1)
                    A(qT[:], TA[:, 0:W3], ACT.Copy, scale=hcols[:, L:L + 1]).then_inc(a_qk, 1)
                    A(kT[:], TA[:, W3:2 * W3], ACT.Copy, scale=hcols[:, 2 + L:3 + L]).then_inc(a_qk, 1)
                elif stage == 1:
                    act.wait_ge(a_max, n + 1)
                    A(prob[:, 0:3 * P], prob[:, 0:3 * P], ACT.Exp, bias=smax[:, 0:1],
                      accum_out=den[:, 0:1]).then_inc(a_exp, 1)
                    A(prob[:, 3 * P:], prob[:, 3 * P:], ACT.Exp, bias=smax[:, 1:2],
                      accum_out=den[:, 1:2]).then_inc(a_exp, 1)
                elif stage == 2:
                    act.wait_ge(a_pturn, n + 1)
                    A(probT[:], TA[:, 0:NS], ACT.Copy).then_inc(a_pT, 1)

            def merged_round(L, m):
                c = ORDER[m][1]
                act.wait_ge(merge, 4 * L + c + 1)
                A(hT_hi[:, 2 * c:2 * c + 2, :], merged[:, 2 * c:2 * c + 2, :], ACT.Copy).then_inc(merged_hi, 1)

            def mixer(L):
                normalise(2 * L)
                for m in range(MIX + 2):
                    if m == FIRST["w_out"] + 1:
                        merged_round(L, m - 2)
                    if HI_HEAD[L] <= m < MIX:
                        parts, k = SHAPE.get(ORDER[m][0], (P, DC))
                        hi(BASE[L] + m, parts, k * COLS)
                    if m >= 2 and ORDER[m - 2][0] == "proj_c" and m != FIRST["w_out"] + 1:
                        merged_round(L, m - 2)
                    if L == 0 and m == 2:
                        act.wait_ge(lb_diff, 1)
                        A(lbt[:, 2:4, :], lbt[:, 0:2, :], ACT.Exp).then_inc(lb_exp, 1)
                    if m >= 2:
                        evacuate(L, m - 2)
                    if m - 2 in ATTN_O_AT:
                        j = ATTN_O_AT[m - 2]
                        act.wait_ge(a_o, L * SLOTS_PER_GROUP + j + 1)
                        A(o_hi[:, j, :], SA[0:HD, 0:TOK], ACT.Copy).then_inc(a_ohi, 1)
                    if m - 2 in ATTN_AT:
                        attention(L, *ATTN_AT[m - 2])
                    if m in (FIRST["q"] + 5, FIRST["k"] + 5):
                        n = 2 * L + (1 if m == FIRST["q"] + 5 else 2)
                        act.wait_ge(qk_ss, n)
                        A(qkss[:], qkss[:], ACT.Sqrt, scale=1.0 / HD, bias=eps[:, 0:1]).then_inc(qk_root, 1)
                    if m == FORGET_AT + 3:
                        act.wait_ge(f_arg, L + 1)
                        A(bcum[:], bcum[:], ACT.Ln).then_inc(f_ln, 1)
                    if m + 1 in LEVEL_AT and LEVEL_AT[m + 1]:
                        n = LEVEL_AT[m + 1]
                        act.wait_ge(diff, 2 * (L * NLEV + n))
                        A(E[n % 2][:], E[n % 2][:], ACT.Exp).then_inc(decay, 1)
                    if m == CROSS_AT:
                        cross_exp(L)
                    if m == CROSS_AT + 2:
                        act.wait_ge(x_mm, L + 1)
                        A(scx[:], SA[:, 0:CC * P].rearrange("p (c t) -> p c t", c=CC), ACT.Copy).then_inc(x_ev, 1)
                    if m == HGRN_O_AT + 2:
                        act.wait_ge(o_mm, L + 1)
                        A(flat(E[1][:]), TA, ACT.Square).then_inc(o_sq, 1)
                    if m == HGRN_SS_AT + 2:
                        act.wait_ge(o_ss, L + 1)
                        A(flat(E[0][:]), SA, ACT.Sqrt, bias=eps[:, 0:1]).then_inc(o_root, 1)
                    if m == HGRN_SS_AT + 6:
                        act.wait_ge(o_gated, L + 1)
                        A(yc_hi[:], E[1][:], ACT.Copy).then_inc(yc_hi_done, 1)
                    if m == FIRST["bb"] + 5:
                        act.wait_ge(conv_y, L + 1)
                        A(yb_hi[:], xb[:], ACT.Copy).then_inc(conv_hi, 1)
                    if m == MIX:
                        A(root_warm[:], eps[:], ACT.Sqrt)
                    if m >= MIX and FEEDS[L]:
                        (dense_hi if L == 0 else partial(moe_hi, 0))(m - MIX, 0)

            def dense_hi(q, n):
                act.wait_ge(d_landed[q % F_SLOTS], n * 32 + 32 * (q // F_SLOTS + 1))
                act.wait_ge(d_split_free, n * 6 + (q + 1))
                A(f_hi[q % F_SLOTS][:], f_raw[q % F_SLOTS][:], ACT.Copy).then_inc(d_hi_done, 1)

            def dense():
                def silu_of(v, n):
                    act.wait_ge(d_split_free, n * 6 + (F_SLOTS + max(3 * v, 1) + 1))
                    for b in range(TB):
                        A(act_tm[:, b, :], h_bank(v, b)[:, 0:COLS], ACT.Silu).then_inc(silu, 1)

                def turned(v, n):
                    for b in range(TB):
                        act.wait_ge(aT_psum, n * 4 + (TB * v + b + 1))
                        A(flat(actT_hi[:, b]), h_bank(v, b)[:, 0:COLS], ACT.Copy).then_inc(aT_hi, 1)

                def unit(v, n, split=True):
                    if split:
                        dense_hi(3 * v + AHEAD, n)
                        dense_hi(3 * v + 1 + AHEAD, n)
                    silu_of(v, n)
                    if split:
                        dense_hi(3 * v + 2 + AHEAD, n)
                    turned(v, n)

                unit(0, 0)
                with act.Fori(0, (DENSE_UNITS - 3) // 2) as n:
                    for v in (1, 2):
                        unit(v, n)
                unit(DENSE_UNITS - 2, 0)
                unit(DENSE_UNITS - 1, 0, split=False)
                A(root_warm[:], eps[:], ACT.Sqrt)
                if LAYERS == 2:
                    hi(BASE[1])
                    hi(BASE[1] + 1)

            def moe_hi(i, q, n):
                act.wait_ge(m_landed[q % F_SLOTS], i * (32 * PASS_PIECES // F_SLOTS) + n * 32 + 32 * (q // F_SLOTS + 1))
                act.wait_ge(m_split_free, i * PASS_PIECES + n * 6 + (q + 1))
                A(f_hi[q % F_SLOTS][:], f_raw[q % F_SLOTS][:], ACT.Copy).then_inc(m_hi_done, 1)

            def moe():
                def silu_of(i, v, n):
                    act.wait_ge(m_split_free, i * PASS_PIECES + n * 6 + (F_SLOTS + max(m_piece(v, 0), 1) + 1))
                    A(m_act[:], ps[:, v % 2, 0:COLS], ACT.Silu).then_inc(m_silu, 1)

                def turned(i, v, n):
                    act.wait_ge(mT_psum, i * MOE_UNITS + n * 2 + (v + 1))
                    A(flat(mT_hi[:]), ps[:, v % 2, 0:COLS], ACT.Copy).then_inc(mT_hi_done, 1)

                def unit(i, v, n, final, next_tokens=None):
                    silu_of(i, v, n)
                    split_ahead(moe_hi, i, m_piece(v, 0) + M_AHEAD, n, final)
                    turned(i, v, n)
                    if next_tokens is not None:
                        next_tokens(i + 1)
                    split_ahead(moe_hi, i, m_piece(v, 1) + M_AHEAD, n, final)
                    split_ahead(moe_hi, i, m_piece(v, 2) + M_AHEAD, n, final)

                def gathered_hi(i):
                    for h in range(2):
                        chunks = slice(h * DC // 2, (h + 1) * DC // 2)
                        act.wait_ge(gathered, 2 * i + (h + 1))
                        A(XT_hi[:, chunks, :], XT_psum[:, chunks, :], ACT.Copy).then_inc(XT_hi_done, 1)

                def one_pass(i, final):
                    unit(i, 0, 0, False)
                    unit(i, 1, 0, False)
                    with act.Fori(0, M_UNIT_PAIRS) as n:
                        for v in (2, 3):
                            unit(i, v, n, False)
                    act.wait_ge(sel_turned, i + 1)
                    A(selT[:], ps[:, 6, 0:TOK], ACT.Copy).then_inc(selT_done, 1)
                    unit(i, MOE_UNITS - 2, 0, final)
                    unit(i, MOE_UNITS - 1, 0, final, None if final else gathered_hi)
                    act.wait_ge(m_split_free, i * PASS_PIECES + (PASS_PIECES + F_SLOTS))
                    act.wait_ge(gslot_done, i + 2)
                    A(Y_hi[:], flat(ps[:, 2:4, :]), ACT.Copy, scale=gslot[:, 0:1]).then_inc(Y_hi_done, 1)

                act.wait_ge(router_in, 16)
                A(router_hi[:], router[:], ACT.Copy).then_inc(r_hi, 1)
                for q in range(3, M_AHEAD):
                    moe_hi(0, q, 0)
                act.wait_ge(z_ready, 1)
                A(ez[:], ez[:], ACT.Exp).then_inc(z_exp, 1)
                gathered_hi(0)
                act.wait_ge(table, 1)
                last_pass = last_pass_of(act)
                with act.Fori(0, last_pass) as i:
                    one_pass(i, False)
                one_pass(last_pass, True)

            act.wait_ge(eps_ready, 1)
            A(root_warm[:], eps[:], ACT.Sqrt)
            mixer(0)
            if stop_at != "mixer0":
                normalise(1)
                dense()
            if LAYERS == 2:
                mixer(1)
            if stop_at is None:
                normalise(3)
                moe()

        @block.tensor
        def _(pe):
            mm = nc.tensor.matmul

            def turn(dst, src, n=P):
                return nc.tensor.transpose(dst, src, ident[0:n, 0:n])

            def split_mm(dst, a_hi, a_lo, b_hi, b_lo, first, last):
                mm(dst, a_hi, b_hi, start=first, stop=False)
                mm(dst, a_lo, b_hi, start=False, stop=False)
                return mm(dst, a_hi, b_lo, start=False, stop=last)

            def normalise(n):
                for b in range(TB):
                    pe.wait_ge(h_ready, TB * n + b + 1)
                    for j in range(DC // 2):
                        for c in range(2):
                            last = turn(ps[:, 2 + j, c * TOK + b * P:c * TOK + (b + 1) * P],
                                        h_tm[:, b, (2 * j + c) * P:(2 * j + c + 1) * P])
                        if b == TB - 1:
                            last.then_inc(hT_psum, 1)

            ACTS = {"proj_a": (o_hi, o_lo), "proj_b": (yb_hi, yb_lo), "proj_c": (yc_hi, yc_lo)}

            def piece(L, m):
                name, _, _ = ORDER[m]
                p = BASE[L] + m
                parts, k = SHAPE.get(name, (P, DC))
                ready = {"proj_a": (a_olo, SLOTS_PER_GROUP * (L + 1)), "proj_b": (conv_lo, L + 1),
                         "proj_c": (yc_done, L + 1)}
                if name in ready and m == FIRST[name]:
                    pe.wait_ge(*ready[name])
                a_hi, a_lo = ACTS.get(name, (hT_hi, hT_lo))
                pe.wait_ge(lo_done, p + 1)
                pe.wait_ge(g_free[m % 2], L * (MIX // 2) + m // 2)
                wh, wl = piece_view(w_hi, p % SPLIT, parts, k), piece_view(w_lo, p % RAW, parts, k)
                g = G[m % 2]
                for half in range(2):
                    dst = g[:, half * COLS:(half + 1) * COLS]
                    for c in range(k):
                        if m == 0 and half == 0:
                            pe.wait_ge(hT_ready, DC * 2 * L + c + 1)
                        if m == FIRST["w_out"] and half == 0 and c % 2 == 0:
                            pe.wait_ge(merged_lo, 4 * L + c // 2 + 1)
                        if name in TOKEN_MAJOR:
                            tok = slice(half * P, (half + 1) * P)
                            last = split_mm(dst, a_hi[:, c, tok], a_lo[:, c, tok], wh[:, c, :], wl[:, c, :],
                                            c == 0, c == k - 1)
                        else:
                            out_c = slice(half * P, (half + 1) * P)
                            last = split_mm(dst, wh[:, c, out_c], wl[:, c, out_c], a_hi[:, c, :], a_lo[:, c, :],
                                            c == 0, c == k - 1)
                last.then_inc(used, 1)

            def attention(L, j, stage):
                n = L * SLOTS_PER_GROUP + j
                heads = [g * SLOTS_PER_GROUP + j for g in range(len(GROUPS))]
                if stage == 0:
                    if j == 0:
                        pe.wait_ge(qk_normed, 2 * (L + 1))
                    pe.wait_ge(a_pT, n)
                    if L and j == 0:
                        pe.wait_ge(o_read, L)
                    for w, t in enumerate((q_tm, k_tm)):
                        for g, hd in enumerate(heads):
                            for b in range(TB):
                                o = w * W3 + g * TOK + b * P
                                last = turn(TA[:, o:o + P], t[:, b, hd * HD:(hd + 2) * HD])
                    last.then_inc(a_turn, 1)
                elif stage == 1:
                    pe.wait_ge(a_qk, 2 * (n // 2 + 1))
                    own = slice(j % 2 * HD, (j % 2 + 1) * HD)
                    pe.wait_ge(a_olo, n)
                    for g in range(3):
                        mm(SA[:, g * P:(g + 1) * P], qT[own, g * TOK:g * TOK + P], kT[own, g * TOK:g * TOK + P],
                           start=True, stop=True)
                    for g in range(3):
                        last = mm(SA[:, 512 + g * TOK:512 + (g + 1) * TOK], qT[own, g * TOK + P:(g + 1) * TOK],
                                  kT[own, g * TOK:(g + 1) * TOK], start=True, stop=True)
                    last.then_inc(a_score, 1)
                elif stage == 2:
                    pe.wait_ge(a_prob, n + 1)
                    for q in range(NS // P):
                        last = turn(TA[:, q * P:(q + 1) * P], prob[:, q * P:(q + 1) * P])
                    last.then_inc(a_pturn, 1)
                else:
                    if j == 0:
                        evacuated(pe, L, FIRST["v"] + 2)
                    pe.wait_ge(a_pT, n + 1)
                    for g, hd in enumerate(heads):
                        mm(SA[0:HD, 0:P], v_tm[:, 0, hd * HD:(hd + 1) * HD], probT[:, g * P:(g + 1) * P],
                           start=g == 0, stop=g == 2)
                    for g, hd in enumerate(heads):
                        for b in range(TB):
                            o = 3 * P + g * TOK + b * P
                            last = mm(SA[0:HD, P:TOK], v_tm[:, b, hd * HD:(hd + 1) * HD], probT[:, o:o + P],
                                      start=g == b == 0, stop=g == 2 and b == 1)
                    last.then_inc(a_o, 1)

            def level(L, n):
                if n == 0:
                    pe.wait_ge(kc_done, L + 1)
                    evacuated(pe, L, FIRST["qc"] + 2)
                    pe.wait_ge(a_olo, SLOTS_PER_GROUP * (L + 1))
                    left, right = kc, qc
                else:
                    pe.wait_ge(qk_level, 2 * (L * NLEV + n))
                    pe.wait_ge(level_ev, L * (NLEV + 1) + n)
                    left = right = E[n % 2]
                for c in range(CC):
                    for b in range(TB):
                        block = slice(b * P, (b + 1) * P)
                        if n == 0:
                            o = (c * TB + b) * P
                            dst, rhs = SA[:, o:o + P], right[:, c, block]
                        else:
                            o, h = (c * TB + b) * (P // 2), LEVELS[n]
                            dst = SA[:, o:o + P // 2].rearrange("p (g h) -> p g h", h=h)
                            rhs = right[:, c, block].rearrange("p (g w) -> p g w", w=2 * h)[:, :, h:2 * h]
                        last = mm(dst, left[:, c, block], rhs, start=True, stop=True)
                last.then_inc(level_mm, 1)

            def cross(L):
                pe.wait_ge(x_qk, 2 * (L + 1))
                pe.wait_ge(level_ev, (L + 1) * (NLEV + 1))
                for c in range(CC):
                    last = mm(SA[:, c * P:(c + 1) * P], E[0][:, c, 0:P], E[0][:, c, P:TOK], start=True, stop=True)
                last.then_inc(x_mm, 1)

            def hgrn_out(L):
                evacuated(pe, L, FIRST["i"] + 2)
                pe.wait_ge(level_add, (L + 1) * NLEV)
                pe.wait_ge(x_ev, L + 1)
                for c in range(CC):
                    hd = slice(c * P, (c + 1) * P)
                    mm(TA[:, c * TOK:c * TOK + P], i_tm[:, 0, hd], sc[:, c * TB, :], start=True, stop=True)
                    mm(TA[:, c * TOK + P:(c + 1) * TOK], i_tm[:, 0, hd], scx[:, c, :], start=True, stop=False)
                    last = mm(TA[:, c * TOK + P:(c + 1) * TOK], i_tm[:, 1, hd], sc[:, c * TB + 1, :],
                              start=False, stop=True)
                last.then_inc(o_mm, 1)

            def hgrn_ss(L):
                pe.wait_ge(o_sq, L + 1)
                for q in range(3):
                    last = mm(SA[:, q * 512:(q + 1) * 512], mean128[:], flat(E[1][:])[:, q * 512:(q + 1) * 512],
                              start=True, stop=True)
                last.then_inc(o_ss, 1)

            def mixer(L):
                normalise(2 * L)
                for m in range(MIX):
                    if m == FIRST["w_out"] and FEEDS[L]:
                        pe.sem_inc((d_split_free, m_split_free)[L], F_SLOTS)
                    piece(L, m)
                    if m in ATTN_O_AT:
                        attention(L, ATTN_O_AT[m], 3)
                    if m in ATTN_AT:
                        attention(L, *ATTN_AT[m])
                    if m in LEVEL_AT:
                        level(L, LEVEL_AT[m])
                    if m == CROSS_AT:
                        cross(L)
                    if m == HGRN_O_AT:
                        hgrn_out(L)
                    if m == HGRN_SS_AT:
                        hgrn_ss(L)

            def dense():
                Y = [ps[:, 4 + b * 2 + h, :] for b in range(TB) for h in range(2)]

                def up(v, n):
                    for half in range(2):
                        q = half if v == 0 else 3 * v - 1 + half
                        pe.wait_ge(d_raw_free, n * 6 + (F_SLOTS + q + 1))
                        wh, wl = (t[q % F_SLOTS][:].rearrange("p (k n) -> p k n", k=4) for t in (f_hi, f_lo))
                        for b in range(TB):
                            if half == 0 and v > 1:
                                pe.wait_ge(aT_lo, n * 4 + (TB * (v - 2) + b + 1))
                            tok = slice(b * P, (b + 1) * P)
                            for c in range(4):
                                k = 4 * half + c
                                if v == 0 and b == 0:
                                    pe.wait_ge(hT_ready, DC + k + 1)
                                last = split_mm(h_bank(v, b), hT_hi[:, k, tok], hT_lo[:, k, tok], wh[:, c, :], wl[:, c, :],
                                                k == 0, k == DC - 1)
                        last.then_inc(d_split_free, 1)

                def down(v, n, first=False, final=False):
                    q = DENSE - 1 if final else 3 * (v + 1) + 1
                    pe.wait_ge(d_raw_free, n * 6 + (F_SLOTS + q + 1))
                    pe.wait_ge(aT_lo, n * 4 + TB * (v + 1))
                    wh, wl = (t[q % F_SLOTS][:].rearrange("p (c h n) -> p c h n", c=2, h=2) for t in (f_hi, f_lo))
                    for b in range(TB):
                        for c in range(2):
                            for h in range(2):
                                last = split_mm(Y[b * 2 + h], actT_hi[:, b, c, :], actT_lo[:, b, c, :], wh[:, c, h, :],
                                                wl[:, c, h, :], first and c == 0, final and c == 1)
                        if final and b == 0:
                            last.then_inc(y_first, 1)
                    last.then_inc(d_split_free, 1)

                def turn_act(v, n):
                    for b in range(TB):
                        pe.wait_ge(act_done, n * 4 + (TB * v + b + 1))
                        for c in range(2):
                            last = turn(h_bank(v, b)[:, c * P:(c + 1) * P], act_tm[:, b, c * P:(c + 1) * P])
                        last.then_inc(aT_psum, 1)

                up(0, 0)
                turn_act(0, 0)
                for v in (1, 2):
                    up(v, 0)
                    down(v - 1, 0, first=v == 1)
                    turn_act(v, 0)
                with pe.Fori(0, (DENSE_UNITS - 3) // 2) as n:
                    for v in (3, 4):
                        up(v, n)
                        down(v - 1, n)
                        turn_act(v, n)
                down(DENSE_UNITS - 1, 0, final=True)

            def moe():
                pe.wait_ge(r_lo, 1)
                pe.wait_ge(hT_ready, 2 * DEPTH * DC)
                for k in range(DC):
                    last = split_mm(ps[0:NE, 2, 0:TOK], router_hi[:, k, :], router_lo[:, k, :],
                                    hT_hi[:, k, :], hT_lo[:, k, :], k == 0, k == DC - 1)
                last.then_inc(logits, 1)
                pe.wait_ge(logitsT_done, 1)
                for b in range(TB):
                    last = turn(ps[:, 3, b * NE:(b + 1) * NE], logitsT[:, b * P:(b + 1) * P], NE)
                last.then_inc(logits, 1)
                pe.wait_ge(chosen_ready, 1)
                mm(ps[:, 3, 0:NE], before[:], chosen[:, 0, :], start=True, stop=True)
                mm(ps[:, 3, NE:2 * NE], before[:], chosen[:, 1, :], start=True, stop=False)
                mm(ps[:, 3, NE:2 * NE], ones[:], chosen[:, 0, :], start=False, stop=True)
                mm(ps[:, 3, 2 * NE:3 * NE], ones[:], chosen[:, 0, :], start=True, stop=False)
                mm(ps[:, 3, 2 * NE:3 * NE], ones[:], chosen[:, 1, :], start=False, stop=True).then_inc(counted, 1)
                def gather(i):
                    pe.wait_ge(sel_built, i + 1)
                    for k in range(DC):
                        for b in range(TB):
                            last = mm(XT_psum[:, k, :], h_tm[:, b, k * P:(k + 1) * P], sel01[:, b, :],
                                      start=b == 0, stop=b == TB - 1)
                        if k % (DC // 2) == DC // 2 - 1:
                            last.then_inc(gathered, 1)

                def turn_sel(i):
                    pe.wait_ge(x_added, i * TB + TB)
                    for b in range(TB):
                        turn(ps[:, 6, b * P:(b + 1) * P], sel01[:, b, :])
                    for b in range(TB):
                        last = mm(ps[:, 7, 0:1], sel01[:, b, :], GATE[:, bass.ds(i, 1), b], start=b == 0, stop=b == TB - 1)
                    last.then_inc(sel_turned, 1)

                def scatter(i):
                    pe.wait_ge(Y_lo_done, i + 1)
                    pe.wait_ge(selT_done, i + 1)
                    pe.wait_ge(gslot_done, i + 1)
                    for b in range(TB):
                        for h in range(2):
                            half = slice(h * 512, (h + 1) * 512)
                            for y in (Y_hi, Y_lo):
                                last = mm(ps[:, 4 + 2 * b + h, :], selT[:, b * P:(b + 1) * P], y[:, half],
                                          start=y is Y_hi, stop=y is Y_lo)
                        last.then_inc(scattered, 1)

                def up(i, v, n):
                    if v > 1:
                        pe.wait_ge(mT_lo_done, i * MOE_UNITS + n * 2 + (v - 1))
                    for half in range(2):
                        q = m_piece(v, half - 1) if v else half
                        pe.wait_ge(m_raw_free, i * PASS_PIECES + n * 6 + (F_SLOTS + q + 1))
                        if v == 0:
                            pe.wait_ge(XT_lo_done, 2 * i + (half + 1))
                        wh, wl = (t[q % F_SLOTS][:].rearrange("p (k n) -> p k n", k=4) for t in (f_hi, f_lo))
                        for c in range(4):
                            k = 4 * half + c
                            last = split_mm(ps[:, v % 2, :], XT_hi[:, k, :], XT_lo[:, k, :], wh[:, c, :], wl[:, c, :],
                                            k == 0, k == DC - 1)
                        last.then_inc(m_split_free, 1)

                def down(i, v, n):
                    q = m_piece(v + 1, 1) if v < MOE_UNITS - 1 else PASS_PIECES - 1
                    pe.wait_ge(m_raw_free, i * PASS_PIECES + n * 6 + (F_SLOTS + q + 1))
                    pe.wait_ge(mT_lo_done, i * MOE_UNITS + n * 2 + (v + 1))
                    wh, wl = (t[q % F_SLOTS][:].rearrange("p (c h n) -> p c h n", c=2, h=2) for t in (f_hi, f_lo))
                    for c in range(2):
                        for h in range(2):
                            last = split_mm(ps[:, 2 + h, :], mT_hi[:, c, :], mT_lo[:, c, :], wh[:, c, h, :],
                                            wl[:, c, h, :], v == 0 and c == 0, v == MOE_UNITS - 1 and c == 1)
                    last.then_inc(m_split_free, 1)

                def turn_act(i, v, n):
                    pe.wait_ge(m_act_done, i * MOE_UNITS + n * 2 + (v + 1))
                    for c in range(2):
                        last = turn(ps[:, v % 2, c * P:(c + 1) * P], m_act[:, c * P:(c + 1) * P])
                    last.then_inc(mT_psum, 1)

                def unit(i, v, n):
                    up(i, v, n)
                    down(i, v - 1, n)
                    turn_act(i, v, n)

                def one_pass(i, final):
                    up(i, 0, 0)
                    scatter(i)
                    turn_act(i, 0, 0)
                    unit(i, 1, 0)
                    unit(i, 2, 0)
                    unit(i, 3, 0)
                    turn_sel(i)
                    with pe.Fori(0, M_UNIT_PAIRS - 1) as n:
                        for v in (4, 5):
                            unit(i, v, n)
                    for v in (MOE_UNITS - 2, MOE_UNITS - 1):
                        unit(i, v, 0)
                    if not final:
                        gather(i + 1)
                    down(i, MOE_UNITS - 1, 0)

                pe.wait_ge(hg, TB)
                gather(0)
                pe.wait_ge(table, 1)
                last_pass = last_pass_of(pe)
                with pe.Fori(0, last_pass) as i:
                    one_pass(i, False)
                one_pass(last_pass, True)
                scatter(last_pass + 1)

            pe.wait_ge(vec_in, 16 * N_VEC)
            pe.wait_ge(ident_ready, 1)
            turn(ps[:, 7, 0:NROWS], rows[0:NROWS, :], NROWS).then_inc(vec_T, 1)
            turn(ps[:, 6, 0:4], hrows[:, :], 4).then_inc(vec_T, 1)
            mixer(0)
            if stop_at != "mixer0":
                normalise(1)
                dense()
            if LAYERS == 2:
                mixer(1)
            if stop_at is None:
                normalise(3)
                moe()

        @block.vector
        def _(dve):
            V = nc.vector
            steps = {"n": 0}

            def link(ins):
                steps["n"] += 1
                ins.then_inc(dve_step, 1)
                dve.wait_ge(dve_step, steps["n"])

            def lo(p, parts=P, n=PIECE):
                dve.wait_ge(hi_done, p + 1)
                V.tensor_tensor(w_lo[0:parts, p % RAW, 0:n], raw[0:parts, p % RAW, 0:n],
                                w_hi[0:parts, p % SPLIT, 0:n].bitcast(F32), ALU.subtract).then_inc(lo_done, 1)

            def constants():
                V.memset(ones[:], 1.0)
                V.memset(mean128[:], 1.0 / P)
                V.memset(lbm[:, 0, :], LB_FLOOR)
                V.memset(oml[:, 0, :], 1.0)
                V.memset(kfix[:, 0, :], LB_FLOOR)
                dve.wait_ge(vec_T, 2)
                V.tensor_copy(hcols[:], ps[:, 6, 0:4])
                V.tensor_copy(cols[:, 0:NROWS], ps[:, 7, 0:NROWS]).then_inc(cols_ready, 1)
                dve.wait_ge(cols_ready, 1)

            def lower_bounds():
                a0, a1 = cols[:, R_LB:R_LB + CC], cols[:, R_LB + CC:R_LB + 2 * CC]
                link(V.tensor_tensor(lbt[:, 2, :], a0, a1, ALU.max))
                V.tensor_tensor(lbt[:, 0, :], a0, lbt[:, 2, :], ALU.subtract)
                V.tensor_tensor(lbt[:, 1, :], a1, lbt[:, 2, :], ALU.subtract).then_inc(lb_diff, 1)

            def lower_bounds_shared():
                dve.wait_ge(lb_exp, 1)
                link(V.tensor_tensor(lbt[:, 0, :], lbt[:, 2, :], lbt[:, 3, :], ALU.add))
                link(V.reciprocal(lbt[:, 1, :], lbt[:, 0, :]))
                V.tensor_tensor(oml[:, 1, :], lbt[:, 2, :], lbt[:, 1, :], ALU.mult)
                link(V.tensor_tensor(lbt[:, 0, :], lbt[:, 3, :], lbt[:, 1, :], ALU.mult))
                link(V.tensor_scalar(lbm[:, 1, :], lbt[:, 0, :], LB_FLOOR, None, ALU.max))
                link(V.tensor_tensor(kfix[:, 1, :], lbm[:, 1, :], lbt[:, 0, :], ALU.subtract))

            def attention_mask(at0, n, g, window, dilation):
                d = amask[:, at0 + g * n:at0 + (g + 1) * n]
                ok, dist, rem = E[0][:, 0, 0:n], E[0][:, 1, 0:n], E[1][:, 0, 0:n].bitcast(I32)
                link(V.tensor_copy(dist, d.bitcast(I32)))
                link(V.tensor_scalar(ok, dist, float(TOK), None, ALU.is_ge))
                if dilation > 1:
                    link(V.tensor_scalar(rem, d.bitcast(I32), dilation - 1, None, ALU.bitwise_and))
                    link(V.tensor_copy(dist, rem))
                    link(V.scalar_tensor_tensor(ok, dist, 0.0, ok, ALU.is_equal, ALU.mult))
                if window < TOK:
                    link(V.scalar_tensor_tensor(ok, dist, float(TOK + window), ok, ALU.is_le, ALU.mult))
                link(V.tensor_scalar(d, ok, 1.0, -NEG_BIG, ALU.subtract, ALU.mult))

            def level_mask(n):
                if n == 0:
                    V.tensor_copy(hmask[:, 0, :], ident[:])
                else:
                    h = LEVELS[n]
                    rem, start = E[0][:, 0, 0:P], E[1][:, 0, 0:P]
                    s_rem, s_start, s_first = (scol[:, q:q + 1] for q in range(3))
                    V.tensor_scalar(E[0][:, 1, 0:P].bitcast(I32), lane_i[:], 2 * h - 1, None, ALU.bitwise_and)
                    link(V.tensor_scalar(scol[:, 3:4].bitcast(I32), part_i[:], 2 * h - 1, None, ALU.bitwise_and))
                    V.tensor_copy(rem, E[0][:, 1, 0:P].bitcast(I32))
                    link(V.tensor_copy(s_rem, scol[:, 3:4].bitcast(I32)))
                    V.tensor_tensor(start, lane[:], rem, ALU.subtract)
                    V.tensor_tensor(s_start, part[:], s_rem, ALU.subtract)
                    link(V.tensor_scalar(s_first, s_rem, float(h), None, ALU.is_lt))
                    link(V.tensor_scalar(hmask[:, n, :], start, s_start, s_first, ALU.is_equal, ALU.mult))
                    link(V.scalar_tensor_tensor(hmask[:, n, :], rem, float(h), hmask[:, n, :], ALU.is_ge, ALU.mult))

            def normalise(n):
                if n == 1:
                    dense_lo(1, 0)
                elif n == 3:
                    moe_lo(0, 1, 0)
                dve.wait_ge(x_root, n + 1)
                link(V.reciprocal(rstd[:], rstd[:]))
                for b in range(TB):
                    V.tensor_scalar(h_tm[:, b, :], x[:, b, :], rstd[:, b:b + 1], None, ALU.mult).then_inc(h_ready, 1)
                if n == 0:
                    constants()
                    lo(0)
                elif n == 1:
                    dense_lo(2, 0)
                elif n == 2:
                    lo(BASE[1] + 1)
                elif n == 3:
                    moe_lo(0, 2, 0)
                first = (R_AN if n % 2 == 0 else R_FN) + (n // 2) * DC
                for k in range(DC):
                    dve.wait_ge(hT_hi_done, DC * n + 2 * (k // 2) + 2)
                    V.scalar_tensor_tensor(hT_lo[:, k, :], ps[:, 2 + k // 2, (k % 2) * TOK:(k % 2 + 1) * TOK],
                                           col(first + k), hT_hi[:, k, :].bitcast(F32), ALU.mult,
                                           ALU.subtract).then_inc(hT_ready, 1)

            def evacuate(L, m):
                name, c, _ = ORDER[m]
                if name not in ("proj_a", "proj_b", "proj_c", "w_out"):
                    return
                dve.wait_ge(used, BASE[L] + m + 1)
                g, free = G[m % 2], g_free[m % 2]
                if name == "w_out":
                    xs = x[:, :, c * COLS:(c + 1) * COLS]
                    V.tensor_tensor(xs, g.rearrange("p (b n) -> p b n", b=TB), xs, ALU.add).then_inc(free, 1)
                    return
                g = g.rearrange("p (c t) -> p c t", c=2)
                two = slice(2 * c, 2 * c + 2)
                gate = {"proj_a": "gate_a", "proj_b": "gate_b", "proj_c": "gate_c"}[name]
                evacuated(dve, L, FIRST[gate] + c)
                if name == "proj_a":
                    V.tensor_tensor(merged[:, two, :], g, sig_ab[:, two, :], ALU.mult).then_inc(free, 1)
                    return
                V.tensor_tensor(term[:], g, (sig_ab if name == "proj_b" else sig_c)[:, two, :], ALU.mult).then_inc(free, 1)
                evacuated(dve, L, m)
                last = V.tensor_tensor(merged[:, two, :], merged[:, two, :], term[:], ALU.add)
                if name == "proj_b":
                    link(last)
                else:
                    last.then_inc(merge, 1)
                    dve.wait_ge(merged_hi, 4 * L + c + 1)
                    V.tensor_tensor(hT_lo[:, two, :], merged[:, two, :], hT_hi[:, two, :].bitcast(F32),
                                    ALU.subtract).then_inc(merged_lo, 1)

            def qk_norm(L, t, name):
                evacuated(dve, L, FIRST[name] + 2)
                v = t[:].rearrange("p b (h e) -> p (b h) e", e=HD)
                sq = flat(E[0][:]).rearrange("p (h e) -> p h e", e=HD)
                link(V.tensor_tensor(sq, v, v, ALU.mult))
                V.tensor_reduce(qkss[:], sq, AX, ALU.add).then_inc(qk_ss, 1)
                dve.wait_ge(qk_root, 2 * L + (1 if name == "q" else 2))
                link(V.reciprocal(qkss[:], qkss[:]))
                V.tensor_tensor(v, v, qkss[:].rearrange("p (h o) -> p h o", o=1).broadcast_to(v.shape),
                                ALU.mult).then_inc(qk_normed, 1)
                dve.wait_ge(qk_normed, 2 * L + (1 if name == "q" else 2))

            def forget(L):
                evacuated(dve, L, FIRST["f"] + 2)
                for c in range(CC):
                    V.tensor_scalar(kc[:, c, :], kc[:, c, :], oml[:, L, c:c + 1], kfix[:, L, c:c + 1],
                                    ALU.mult, ALU.subtract)
                    last = V.tensor_scalar(bcum[:, c, :], bcum[:, c, :], oml[:, L, c:c + 1], lbm[:, L, c:c + 1],
                                           ALU.mult, ALU.add)
                last.then_inc(kc_done, 1)

            def ln_argument(L):
                dve.wait_ge(kc_done, L + 1)
                link(V.tensor_scalar(E[0][:], bcum[:], 2.0 ** -LN_SHIFT, None, ALU.is_lt))
                link(V.tensor_scalar(E[1][:], E[0][:], 2.0 ** LN_SHIFT, 1.0, ALU.mult, ALU.max))
                V.tensor_tensor(bcum[:], bcum[:], E[1][:], ALU.mult).then_inc(f_arg, 1)

            def cumulate(L):
                dve.wait_ge(f_ln, L + 1)
                link(V.scalar_tensor_tensor(bcum[:], E[0][:], -LN_SHIFT * LN2, bcum[:], ALU.mult, ALU.add))
                for c in range(CC):
                    for b in range(TB):
                        s = bcum[:, c, b * P:(b + 1) * P]
                        last = V.tensor_tensor_scan(s, ones[:], s, 0.0, ALU.mult, ALU.add)
                last.then_inc(cum, 1)

            def level_read(L, n):
                dve.wait_ge(level_mm, L * (NLEV + 1) + n + 1)
                if n == 0:
                    V.tensor_tensor(sc[:], SA.rearrange("p (a t) -> p a t", t=P),
                                    hmask[:, 0:1, :].broadcast_to([P, CC * TB, P]), ALU.mult).then_inc(level_ev, 1)
                    return
                h = LEVELS[n]
                shape = [P, CC * TB, P // (2 * h), h]
                keep = hmask[:, n:n + 1, :].rearrange("p o (g w) -> p o g w", w=2 * h)[:, :, :, h:2 * h]
                dst, scores = (t[:, 0:CC * TB * P // 2].rearrange("p (a g h) -> p a g h", a=CC * TB, h=h)
                               for t in (flat(E[n % 2][:]), SA))
                V.tensor_tensor(dst, scores, keep.broadcast_to(shape), ALU.mult).then_inc(level_ev, 1)

            def level_qk(L, n):
                h = LEVELS[n]
                dve.wait_ge(decay, L * NLEV + n)
                e1, e2 = halves(E[n % 2], h)
                V.tensor_tensor(e1, e1, halves(kc, h)[0], ALU.mult).then_inc(qk_level, 1)
                V.tensor_tensor(e2, e2, halves(qc, h)[1], ALU.mult).then_inc(qk_level, 1)

            def cross_qk(L):
                dve.wait_ge(x_decay, (L + 1) * (CC + 1))
                V.tensor_tensor(E[0][:, :, 0:P], E[0][:, :, 0:P], kc[:, :, 0:P], ALU.mult).then_inc(x_qk, 1)
                V.tensor_tensor(E[0][:, :, P:TOK], E[0][:, :, P:TOK], qc[:, :, P:TOK], ALU.mult).then_inc(x_qk, 1)

            def hgrn_gate(L, step):
                dve.wait_ge(o_root, L + 1)
                if step < 3:
                    part_of = slice(step * CC // 3, (step + 1) * CC // 3)
                    link(V.reciprocal(E[0][:, part_of, :], E[0][:, part_of, :]))
                    return
                evacuated(dve, L, FIRST["g"] + 2)
                V.scalar_tensor_tensor(flat(E[1][:]), TA, col(R_HG + L), flat(E[0][:]), ALU.mult,
                                       ALU.mult).then_inc(o_read, 1)
                dve.wait_ge(o_read, L + 1)
                V.tensor_tensor(E[1][:], E[1][:], gc[:], ALU.mult).then_inc(o_gated, 1)

            def attention(L, j):
                n = L * SLOTS_PER_GROUP + j
                parts = ((slice(0, 3 * P), SA[:, 0:3 * P]), (slice(3 * P, NS), SA[:, 512:512 + W3]))
                dve.wait_ge(a_score, n + 1)
                dve.wait_ge(a_pturn, n)
                for s, scores in parts:
                    last = V.scalar_tensor_tensor(prob[:, s], scores, float(HD) ** -0.5, amask[:, s], ALU.mult, ALU.add)
                link(last)
                for b, (s, _) in enumerate(parts):
                    last = V.tensor_reduce(smax[:, b:b + 1], prob[:, s], AX, ALU.max)
                link(last)
                V.tensor_scalar(smax[:], smax[:], -1.0, None, ALU.mult).then_inc(a_max, 1)
                dve.wait_ge(a_exp, 2 * (n + 1))
                link(V.reciprocal(rden[:], den[:]))
                for b, (s, _) in enumerate(parts):
                    last = V.tensor_scalar(prob[:, s], prob[:, s], rden[:, b:b + 1], None, ALU.mult)
                last.then_inc(a_prob, 1)

            def conv(L):
                evacuated(dve, L, FIRST["cb"] + 2)
                link(V.tensor_tensor(xb[:], xb[:], cb[:], ALU.mult))
                for c in range(CC):
                    last = V.tensor_scalar(cb[:, c, :], xb[:, c, :], conv_col(L, 0, c), None, ALU.mult)
                link(last)
                for j in range(1, conv_w.shape[1]):
                    for c in range(CC):
                        y = cb[:, c, j:TOK]
                        last = V.scalar_tensor_tensor(y, xb[:, c, 0:TOK - j], conv_col(L, j, c), y, ALU.mult, ALU.add)
                    link(last)

            def mixer(L):
                normalise(2 * L)
                for m in range(MIX + 2):
                    if m == FIRST["w_out"] + 1:
                        evacuate(L, m - 2)
                    if LO_HEAD[L] <= m < MIX:
                        parts, k = SHAPE.get(ORDER[m][0], (P, DC))
                        lo(BASE[L] + m, parts, k * COLS)
                    if m >= 2 and m != FIRST["w_out"] + 1:
                        evacuate(L, m - 2)
                    if L == 0 and m == 1:
                        dve.wait_ge(masks, N_MASKS)
                        lower_bounds()
                    if L == 0 and m == 3:
                        lower_bounds_shared()
                    if L == 0 and 1 <= m <= 2 * len(GROUPS):
                        at0, n = ((0, P), (3 * P, TOK))[(m - 1) // len(GROUPS)]
                        g = (m - 1) % len(GROUPS)
                        attention_mask(at0, n, g, *GROUPS[g])
                    if L == 0 and 7 <= m <= 7 + NLEV:
                        level_mask(m - 7)
                    if m == FIRST["q"] + 5:
                        qk_norm(L, q_tm, "q")
                    if m == FIRST["k"] + 5:
                        qk_norm(L, k_tm, "k")
                    if m - 2 in ATTN_O_AT:
                        j = ATTN_O_AT[m - 2]
                        dve.wait_ge(a_ohi, L * SLOTS_PER_GROUP + j + 1)
                        V.tensor_tensor(o_lo[:, j, :], SA[0:HD, 0:TOK], o_hi[:, j, :].bitcast(F32),
                                        ALU.subtract).then_inc(a_olo, 1)
                    if m - 2 in ATTN_AT and ATTN_AT[m - 2][1] == 1:
                        attention(L, ATTN_AT[m - 2][0])
                    if m == FORGET_AT:
                        forget(L)
                    if m == FORGET_AT + 2:
                        ln_argument(L)
                    if m == FORGET_AT + 4:
                        cumulate(L)
                    if m - 2 in LEVEL_AT:
                        level_read(L, LEVEL_AT[m - 2])
                    if m in LEVEL_AT and LEVEL_AT[m]:
                        level_qk(L, LEVEL_AT[m])
                    if m == CROSS_AT:
                        cross_qk(L)
                    if HGRN_SS_AT + 2 <= m < HGRN_SS_AT + 6:
                        hgrn_gate(L, m - HGRN_SS_AT - 2)
                    if m == HGRN_SS_AT + 7:
                        dve.wait_ge(yc_hi_done, L + 1)
                        V.tensor_tensor(yc_lo[:], E[1][:], yc_hi[:].bitcast(F32), ALU.subtract).then_inc(yc_done, 1)
                    if m == FIRST["cb"] + 5:
                        conv(L)
                    if m == FIRST["bb"] + 5:
                        evacuated(dve, L, FIRST["bb"] + 2)
                        V.tensor_tensor(xb[:], cb[:], bb[:], ALU.mult).then_inc(conv_y, 1)
                    if m == FIRST["bb"] + 7:
                        dve.wait_ge(conv_hi, L + 1)
                        V.tensor_tensor(yb_lo[:], xb[:], yb_hi[:].bitcast(F32), ALU.subtract).then_inc(conv_lo, 1)
                    if m == MIX and FEEDS[L]:
                        (dense_lo if L == 0 else partial(moe_lo, 0))(0, 0)

            def dense_lo(q, n):
                dve.wait_ge(d_hi_done, n * 6 + (q + 1))
                V.tensor_tensor(f_lo[q % F_SLOTS][:], f_raw[q % F_SLOTS][:], f_hi[q % F_SLOTS][:].bitcast(F32),
                                ALU.subtract).then_inc(d_raw_free, 1)

            def dense():
                def gate_up(v, n):
                    for b in range(TB):
                        dve.wait_ge(silu, n * 4 + (TB * v + b + 1))
                        V.tensor_tensor(act_tm[:, b, :], act_tm[:, b, :], h_bank(v, b)[:, COLS:2 * COLS],
                                        ALU.mult).then_inc(act_done, 1)

                def turned(v, n):
                    for b in range(TB):
                        dve.wait_ge(aT_hi, n * 4 + (TB * v + b + 1))
                        V.tensor_tensor(flat(actT_lo[:, b]), h_bank(v, b)[:, 0:COLS],
                                        flat(actT_hi[:, b]).bitcast(F32), ALU.subtract).then_inc(aT_lo, 1)

                def unit(v, n, split=True):
                    if split:
                        dense_lo(3 * v + AHEAD, n)
                        dense_lo(3 * v + 1 + AHEAD, n)
                    gate_up(v, n)
                    if split:
                        dense_lo(3 * v + 2 + AHEAD, n)
                    turned(v, n)

                unit(0, 0)
                with dve.Fori(0, (DENSE_UNITS - 3) // 2) as n:
                    for v in (1, 2):
                        unit(v, n)
                unit(DENSE_UNITS - 2, 0)
                unit(DENSE_UNITS - 1, 0, split=False)
                if LAYERS == 2:
                    lo(BASE[1])
                for b in range(TB):
                    if b == 0:
                        dve.wait_ge(y_first, 1)
                    else:
                        dve.wait_ge(d_split_free, F_SLOTS + DENSE)
                    V.tensor_tensor(x[:, b, :], x[:, b, :], flat(ps[:, 4 + 2 * b:6 + 2 * b, :]), ALU.add).then_inc(x_done, 1)
                dve.wait_ge(x_done, TB)

            def moe_lo(i, q, n):
                dve.wait_ge(m_hi_done, i * PASS_PIECES + n * 6 + (q + 1))
                V.tensor_tensor(f_lo[q % F_SLOTS][:], f_raw[q % F_SLOTS][:], f_hi[q % F_SLOTS][:].bitcast(F32),
                                ALU.subtract).then_inc(m_raw_free, 1)

            def moe():
                dve.wait_ge(r_hi, 1)
                V.tensor_tensor(router_lo[:], router[:], router_hi[:].bitcast(F32), ALU.subtract).then_inc(r_lo, 1)
                def select(slot_of):
                    for b in range(TB):
                        last = V.tensor_scalar(sel01[:, b, :], lane[:], slot_of[:, b:b + 1], None, ALU.is_equal)
                    last.then_inc(sel_built, 1)

                for q in range(3, M_AHEAD - 1):
                    moe_lo(0, q, 0)
                dve.wait_ge(masks, N_MASKS + 2)
                dve.wait_ge(logits, 1)
                V.tensor_copy(logitsT[:], ps[0:NE, 2, 0:TOK]).then_inc(logitsT_done, 1)
                dve.wait_ge(logits, 2)
                link(V.tensor_copy(flat(logit[:]), ps[:, 3, 0:TB * NE]))
                other = logit[:].rearrange("p b (o e) -> p b o e", o=1).broadcast_to([P, TB, NE, NE])
                own = logit[:].rearrange("p b (e o) -> p b e o", o=1).broadcast_to([P, TB, NE, NE])
                V.tensor_tensor(gt[:], other, own, ALU.is_gt)
                link(V.tensor_tensor(eq[:], other, own, ALU.is_equal))
                link(V.tensor_tensor(eq[:], eq[:], tri[:].rearrange("p (o e) f -> p o e f", o=1)
                                     .broadcast_to([P, TB, NE, NE]), ALU.mult))
                link(V.tensor_tensor(gt[:], gt[:], eq[:], ALU.add))
                link(V.tensor_reduce(rank[:], gt[:], AX, ALU.add))
                V.tensor_scalar(chosen[:], rank[:], 1.5, None, ALU.is_lt).then_inc(chosen_ready, 1)
                link(V.tensor_reduce(lmax[:], logit[:], AX, ALU.max))
                V.tensor_tensor(ez[:], logit[:], lmax[:].rearrange("p (b o) -> p b o", o=1).broadcast_to([P, TB, NE]),
                                ALU.subtract).then_inc(z_ready, 1)
                dve.wait_ge(z_exp, 1)
                link(V.tensor_tensor(ez[:], ez[:], chosen[:], ALU.mult))
                link(V.tensor_reduce(esum[:], ez[:], AX, ALU.add))
                link(V.reciprocal(esum[:], esum[:]))
                link(V.tensor_tensor(gate[:], ez[:], esum[:].rearrange("p (b o) -> p b o", o=1)
                                     .broadcast_to([P, TB, NE]), ALU.mult))
                dve.wait_ge(counted, 1)
                link(V.scalar_tensor_tensor(flat(place[:]), ps[:, 3, 0:TB * NE], 1000.0, flat(chosen[:]), ALU.add, ALU.mult))
                link(V.tensor_scalar(place[:], place[:], 1000.0, None, ALU.subtract))
                select(place[:, :, 0])
                link(V.tensor_scalar(over[:], ps[:, 3, TB * NE:(TB + 1) * NE], P + 0.5, None, ALU.is_gt))
                link(V.tensor_tensor_scan(over_n[:], ones[:, 0:NE], over[:], 0.0, ALU.mult, ALU.add))
                link(V.tensor_scalar(tabf[:, PASSES:PASSES + 1], over_n[:, NE - 1:NE], float(NE - 1), None, ALU.add))
                link(V.tensor_tensor(over_n[:], over_n[:], over[:], ALU.subtract))
                for j in range(OVER):
                    last = V.scalar_tensor_tensor(pick[:, j, :], over_n[:], float(j), over[:], ALU.is_equal, ALU.mult)
                link(last)
                for t, tb, shift in ((POS, place, float(P)), (GATE, gate, 0.0)):
                    V.tensor_copy(t[:, 0:NE, :].rearrange("p e b -> p b e"), tb[:])
                    for b in range(TB):
                        last = V.tensor_tensor(tmp8[:, b], pick[:], tb[:, b:b + 1, :].broadcast_to([P, OVER, NE]), ALU.mult)
                    link(last)
                    o = t[:, NE:PASSES, :].rearrange("p j b -> p b j")
                    link(V.tensor_reduce(o, tmp8[:], AX, ALU.add))
                    link(V.tensor_scalar(o, o, shift, None, ALU.subtract))
                V.tensor_copy(tabf[:, 0:NE], iota8[:])
                link(V.tensor_tensor(tmp8[:, 0], pick[:], iota8[:].rearrange("p (o e) -> p o e", o=1)
                                     .broadcast_to([P, OVER, NE]), ALU.mult))
                link(V.tensor_reduce(tabf[:, NE:PASSES], tmp8[:, 0], AX, ALU.add))
                V.tensor_copy(tab[:], tabf[:]).then_inc(table, 1)
                def gate_up(i, v, n):
                    dve.wait_ge(m_silu, i * MOE_UNITS + n * 2 + (v + 1))
                    V.tensor_tensor(m_act[:], m_act[:], ps[:, v % 2, COLS:2 * COLS], ALU.mult).then_inc(m_act_done, 1)

                def turned(i, v, n):
                    dve.wait_ge(mT_hi_done, i * MOE_UNITS + n * 2 + (v + 1))
                    V.tensor_tensor(flat(mT_lo[:]), ps[:, v % 2, 0:COLS], flat(mT_hi[:]).bitcast(F32),
                                    ALU.subtract).then_inc(mT_lo_done, 1)

                def unit(i, v, n, final, next_tokens=None):
                    gate_up(i, v, n)
                    split_ahead(moe_lo, i, m_piece(v, 0) + M_AHEAD, n, final)
                    turned(i, v, n)
                    if next_tokens is not None:
                        next_tokens(i + 1)
                    split_ahead(moe_lo, i, m_piece(v, 1) + M_AHEAD, n, final)
                    split_ahead(moe_lo, i, m_piece(v, 2) + M_AHEAD, n, final)

                def gathered_lo(i):
                    for h in range(2):
                        chunks = slice(h * DC // 2, (h + 1) * DC // 2)
                        dve.wait_ge(XT_hi_done, 2 * i + (h + 1))
                        V.tensor_tensor(XT_lo[:, chunks, :], XT_psum[:, chunks, :], XT_hi[:, chunks, :].bitcast(F32),
                                        ALU.subtract).then_inc(XT_lo_done, 1)

                def add_x(i, b):
                    dve.wait_ge(scattered, i * TB + (b + 1))
                    V.tensor_tensor(x[:, b, :], x[:, b, :], flat(ps[:, 4 + 2 * b:6 + 2 * b, :]),
                                    ALU.add).then_inc(x_added, 1)

                def one_pass(i, final):
                    dve.wait_ge(Y_lo_done, i + 1)
                    gate_up(i, 0, 0)
                    moe_lo(i, m_piece(0, 0) + M_AHEAD, 0)
                    add_x(i, 0)
                    turned(i, 0, 0)
                    moe_lo(i, m_piece(0, 1) + M_AHEAD, 0)
                    gate_up(i, 1, 0)
                    moe_lo(i, m_piece(0, 2) + M_AHEAD, 0)
                    turned(i, 1, 0)
                    add_x(i, 1)
                    for c in range(3):
                        moe_lo(i, m_piece(1, c) + M_AHEAD, 0)
                    with dve.Fori(0, M_UNIT_PAIRS) as n:
                        for v in (2, 3):
                            unit(i, v, n, False)
                    dve.wait_ge(sel_turned, i + 1)
                    V.tensor_copy(gslot[:], ps[:, 7, 0:1]).then_inc(gslot_done, 1)
                    if not final:
                        select(POS[:, bass.ds(i + 1, 1), :].rearrange("p o b -> p (o b)"))
                    unit(i, MOE_UNITS - 2, 0, final)
                    unit(i, MOE_UNITS - 1, 0, final, None if final else gathered_lo)
                    dve.wait_ge(Y_hi_done, i + 1)
                    dve.wait_ge(gslot_done, i + 2)
                    V.scalar_tensor_tensor(Y_lo[:], flat(ps[:, 2:4, :]), gslot[:, 0:1], Y_hi[:].bitcast(F32),
                                           ALU.mult, ALU.subtract).then_inc(Y_lo_done, 1)

                gathered_lo(0)
                moe_lo(0, M_AHEAD - 1, 0)
                dve.wait_ge(table, 1)
                last_pass = last_pass_of(dve)
                with dve.Fori(0, last_pass) as i:
                    one_pass(i, False)
                one_pass(last_pass, True)
                for b in range(TB):
                    add_x(last_pass + 1, b)

            mixer(0)
            if stop_at != "mixer0":
                normalise(1)
                dense()
            if LAYERS == 2:
                mixer(1)
            if stop_at is None:
                evacuated(dve, DEPTH - 1, MIX - 1)
                normalise(3)
                moe()


NAMES = ["x", "attn_norm", "ffn_norm", "w_in", "q_norm", "k_norm", "conv_w", "hgrn_lower_bounds", "hgrn_out_norm",
         "w_proj_a", "w_proj_b", "w_proj_c", "w_out", "dense_w1", "dense_w3", "dense_w2", "router_w", "moe_w1",
         "moe_w3", "moe_w2"]


def kernel(**inputs):
    import numpy as np
    import concourse.bacc as bacc
    from concourse.bass_utils import run_bass_kernel_spmd

    nc = bacc.Bacc("TRN2", target_bir_lowering=False, num_devices=1)
    arrays, args = {}, []
    for name in NAMES:
        a = np.ascontiguousarray(inputs[name])
        arrays[f"in_{name}"] = a
        args.append(nc.dram_tensor(f"in_{name}", a.shape, mybir.dt.from_np(a.dtype), kind="ExternalInput").ap())
    out = nc.dram_tensor("out_x", inputs["x"].shape, F32, kind="ExternalOutput").ap()
    decoder(nc, *args, out)
    r = run_bass_kernel_spmd(nc, [arrays], core_ids=[0])
    return r.results[0]["out_x"]
```
